# Optimizing a Trainium2 kernel written in Bass

```python
import math
import jax
import jax.numpy as jnp
from jax import lax
import numpy as np

D_MODEL = 1024
BATCH = 1
SEQ = 512
DEPTH = 2
DEC_BATCH = 8
DEC_SEQ = 4
PAST_LEN = 2048
PAGE_SIZE = 128

SSM_GROUP = 16
N_GROUPS = D_MODEL // SSM_GROUP
SSM_STATE = 64
HEAD_DIM = 64
N_HEADS = D_MODEL // HEAD_DIM
N_KV_HEADS = 4
Q_PER_KV = N_HEADS // N_KV_HEADS
WINDOW = 128
NUM_BUCKETS = 32
MAX_DISTANCE = 128
D_FF = ((8 * D_MODEL // 3 + 127) // 128) * 128
CONV_WIDTH = 3
PLE_DIM = 256
N_A_LAYERS = DEPTH // 2
N_B_LAYERS = DEPTH - N_A_LAYERS
EPS = 1e-6

kernel_name = 'yoco_s5_swa_sink_convffn_step'

def _rmsnorm(x, g):
    xf = x.astype(jnp.float32)
    y = xf * lax.rsqrt(jnp.mean(xf * xf, axis=-1, keepdims=True) + EPS)
    return (y * g.astype(jnp.float32)).astype(x.dtype)

def _complex_affine_combine(e1, e2):
    a1r, a1i, b1r, b1i = e1
    a2r, a2i, b2r, b2i = e2
    return (a1r * a2r - a1i * a2i,
            a1r * a2i + a1i * a2r,
            a2r * b1r - a2i * b1i + b2r,
            a2r * b1i + a2i * b1r + b2i)

def _s5_ssm(u, h0_re, h0_im, lam_re, lam_im, log_dt, b_re, b_im, c_re, c_im, d_skip):
    f32 = jnp.float32
    n, l, _ = u.shape
    uf = u.astype(f32)
    ug = uf.reshape(n, l, N_GROUPS, SSM_GROUP)
    lr = lam_re.astype(f32)
    li = lam_im.astype(f32)
    dt = jnp.exp(log_dt.astype(f32))[:, None]
    mag = jnp.exp(lr * dt)
    ang = li * dt
    ab_re = mag * jnp.cos(ang)
    ab_im = mag * jnp.sin(ang)
    den = lr * lr + li * li
    nr = ab_re - 1.0
    f_re = (nr * lr + ab_im * li) / den
    f_im = (ab_im * lr - nr * li) / den
    br = b_re.astype(f32)
    bi = b_im.astype(f32)
    bb_re = f_re[..., None] * br - f_im[..., None] * bi
    bb_im = f_re[..., None] * bi + f_im[..., None] * br
    bu_re = jnp.einsum('nlgc,gpc->nlgp', ug, bb_re)
    bu_im = jnp.einsum('nlgc,gpc->nlgp', ug, bb_im)
    h0r = h0_re.astype(f32)
    h0i = h0_im.astype(f32)
    bu_re = bu_re.at[:, 0].add(ab_re * h0r - ab_im * h0i)
    bu_im = bu_im.at[:, 0].add(ab_re * h0i + ab_im * h0r)
    a_re = jnp.broadcast_to(ab_re, (1, l) + ab_re.shape)
    a_im = jnp.broadcast_to(ab_im, (1, l) + ab_im.shape)
    _, _, h_re, h_im = lax.associative_scan(_complex_affine_combine, (a_re, a_im, bu_re, bu_im), axis=1)
    y = (jnp.einsum('nlgp,gcp->nlgc', h_re, c_re.astype(f32))
         - jnp.einsum('nlgp,gcp->nlgc', h_im, c_im.astype(f32)))
    y = y.reshape(n, l, D_MODEL) + d_skip.astype(f32) * uf
    return y, h_re[:, -1], h_im[:, -1]

def _conv_ffn(xn, buf, w_up, conv_w, conv_b, w_down):
    up = xn @ w_up
    l = up.shape[1]
    ext = jnp.concatenate([buf.astype(up.dtype), up], axis=1)
    c = conv_b + ext[:, 0:l] * conv_w[0]
    for k in range(1, CONV_WIDTH):
        c = c + ext[:, k:k + l] * conv_w[k]
    gate, val = jnp.split(c, 2, axis=-1)
    return (jax.nn.silu(gate) * val) @ w_down, ext[:, l:]

def _t5_bucket(d):
    max_exact = NUM_BUCKETS // 2
    df = jnp.maximum(d, 1).astype(jnp.float32)
    large = max_exact + (jnp.log(df / max_exact) / math.log(MAX_DISTANCE / max_exact)
                         * (NUM_BUCKETS - max_exact)).astype(jnp.int32)
    return jnp.where(d < max_exact, d, jnp.minimum(large, NUM_BUCKETS - 1))

def _shared_kv(h, kbuf, vbuf, buf_valid, g_kv, w_k, w_v, k_norm, rel_bias):
    n, l, _ = h.shape
    s = _rmsnorm(h, g_kv)
    k = _rmsnorm((s @ w_k).reshape(n, l, N_KV_HEADS, HEAD_DIM), k_norm)
    v = (s @ w_v).reshape(n, l, N_KV_HEADS, HEAD_DIM)
    k_full = jnp.concatenate([kbuf.astype(k.dtype), k], axis=1)
    v_full = jnp.concatenate([vbuf.astype(v.dtype), v], axis=1)
    lb = kbuf.shape[1]
    qb = WINDOW if l > WINDOW else l
    nb = l // qb
    lk = lb + qb
    idx = (jnp.arange(nb) * qb)[:, None] + jnp.arange(lk)[None, :]
    d = lb + jnp.arange(qb)[:, None] - jnp.arange(lk)[None, :]
    bias = jnp.transpose(rel_bias[_t5_bucket(jnp.maximum(d, 0))], (2, 0, 1))
    key_ok = jnp.logical_or(idx >= lb, buf_valid)
    mask = ((d >= 0) & (d <= WINDOW))[None] & key_ok[:, None, :]
    return (k_full[:, idx], v_full[:, idx], bias, mask, k_full[:, -lb:], v_full[:, -lb:])

def _window_attention(xn, k_blk, v_blk, bias, mask, w_q, q_norm, sinks, w_o):
    f32 = jnp.float32
    n, l, _ = xn.shape
    nb, lk = k_blk.shape[1], k_blk.shape[2]
    qb = l // nb
    q = _rmsnorm((xn @ w_q).reshape(n, nb, qb, N_KV_HEADS, Q_PER_KV, HEAD_DIM), q_norm)
    s = jnp.einsum('nbtkrd,nbskd->nbkrts', q.astype(f32), k_blk.astype(f32)) * (HEAD_DIM ** -0.5)
    s = s + bias.reshape(N_KV_HEADS, Q_PER_KV, qb, lk).astype(f32)
    s = jnp.where(mask[None, :, None, None], s, -jnp.inf)
    sink = sinks.astype(f32).reshape(N_KV_HEADS, Q_PER_KV, 1, 1)
    m = jnp.maximum(jnp.max(s, axis=-1, keepdims=True), sink)
    pr = jnp.exp(s - m)
    w = pr / (jnp.sum(pr, axis=-1, keepdims=True) + jnp.exp(sink - m))
    o = jnp.einsum('nbkrts,nbskd->nbtkrd', w, v_blk.astype(f32))
    o = o.reshape(n, l, N_HEADS * HEAD_DIM).astype(xn.dtype)
    return o @ w_o

def _trunk(x, p, ssm_re0, ssm_im0, conv0, kbuf, vbuf, buf_valid, prm):
    h = x
    ssm_re, ssm_im, conv = [], [], []
    kv = None
    for i in range(DEPTH):
        xn = _rmsnorm(h, prm['g_mix'][i])
        if i < N_A_LAYERS:
            y, hr, hi = _s5_ssm(xn, ssm_re0[i], ssm_im0[i], prm['ssm_lam_re'][i], prm['ssm_lam_im'][i],
                                prm['ssm_log_dt'][i], prm['ssm_b_re'][i], prm['ssm_b_im'][i],
                                prm['ssm_c_re'][i], prm['ssm_c_im'][i], prm['ssm_d'][i])
            ssm_re.append(hr)
            ssm_im.append(hi)
            z = jax.nn.gelu(y)
            gl = z @ prm['w_glu'][i] + prm['b_glu'][i]
            h = h + (gl[..., :D_MODEL] * jax.nn.sigmoid(gl[..., D_MODEL:])).astype(h.dtype)
        else:
            j = i - N_A_LAYERS
            if kv is None:
                kv = _shared_kv(h, kbuf, vbuf, buf_valid, prm['g_kv'], prm['w_k'], prm['w_v'],
                                prm['k_norm'], prm['rel_bias'])
            h = h + _window_attention(xn, kv[0], kv[1], kv[2], kv[3], prm['w_q'][j], prm['q_norm'][j],
                                      prm['sinks'][j], prm['w_o'][j])
        f, cb = _conv_ffn(_rmsnorm(h, prm['g_ffn'][i]), conv0[i], prm['w_up'][i], prm['conv_w'][i],
                          prm['conv_b'][i], prm['w_down'][i])
        conv.append(cb)
        h = h + f
        gate = jax.nn.sigmoid(_rmsnorm(h, prm['g_ple'][i]) @ prm['w_ple_gate'][i])
        h = h + (p[i] @ prm['w_ple_in'][i]) * gate
    return h, jnp.stack(ssm_re), jnp.stack(ssm_im), jnp.stack(conv), kv[4], kv[5]

def setup_inputs(seed: int = 0) -> dict:
    key = jax.random.key(seed)
    ks = iter(jax.random.split(key, 48))
    f32 = jnp.float32

    def nrm(shape, scale):
        return scale * jax.random.normal(next(ks), shape, f32)

    win_buf = min(WINDOW, PAST_LEN)
    hk = N_KV_HEADS * HEAD_DIM
    hq = N_HEADS * HEAD_DIM
    return {
        'x_prompt': nrm((BATCH, SEQ, D_MODEL), 1.0),
        'x_sample': nrm((DEC_BATCH, DEC_SEQ, D_MODEL), 1.0),
        'state_ssm_re': nrm((N_A_LAYERS, DEC_BATCH, N_GROUPS, SSM_STATE), 0.5),
        'state_ssm_im': nrm((N_A_LAYERS, DEC_BATCH, N_GROUPS, SSM_STATE), 0.5),
        'state_ffn_conv': nrm((DEPTH, DEC_BATCH, CONV_WIDTH - 1, 2 * D_FF), 1.0),
        'cache_k_win': nrm((DEC_BATCH, win_buf, N_KV_HEADS, HEAD_DIM), 1.0),
        'cache_v_win': nrm((DEC_BATCH, win_buf, N_KV_HEADS, HEAD_DIM), 1.0),
        'p_prompt': nrm((DEPTH, BATCH, SEQ, PLE_DIM), 1.0),
        'p_sample': nrm((DEPTH, DEC_BATCH, DEC_SEQ, PLE_DIM), 1.0),
        'g_mix': 1.0 + nrm((DEPTH, D_MODEL), 0.05),
        'g_ffn': 1.0 + nrm((DEPTH, D_MODEL), 0.05),
        'g_ple': 1.0 + nrm((DEPTH, D_MODEL), 0.05),
        'ssm_lam_re': -0.5 + nrm((N_A_LAYERS, N_GROUPS, SSM_STATE), 0.01),
        'ssm_lam_im': math.pi * jnp.arange(SSM_STATE, dtype=f32) + nrm((N_A_LAYERS, N_GROUPS, SSM_STATE), 0.01),
        'ssm_log_dt': jax.random.uniform(next(ks), (N_A_LAYERS, N_GROUPS), f32, math.log(1e-3), math.log(1e-1)),
        'ssm_b_re': nrm((N_A_LAYERS, N_GROUPS, SSM_STATE, SSM_GROUP), (2 * SSM_GROUP) ** -0.5),
        'ssm_b_im': nrm((N_A_LAYERS, N_GROUPS, SSM_STATE, SSM_GROUP), (2 * SSM_GROUP) ** -0.5),
        'ssm_c_re': nrm((N_A_LAYERS, N_GROUPS, SSM_GROUP, SSM_STATE), SSM_STATE ** -0.5),
        'ssm_c_im': nrm((N_A_LAYERS, N_GROUPS, SSM_GROUP, SSM_STATE), SSM_STATE ** -0.5),
        'ssm_d': nrm((N_A_LAYERS, D_MODEL), 1.0),
        'w_glu': nrm((N_A_LAYERS, D_MODEL, 2 * D_MODEL), D_MODEL ** -0.5),
        'b_glu': nrm((N_A_LAYERS, 2 * D_MODEL), 0.01),
        'g_kv': 1.0 + nrm((D_MODEL,), 0.05),
        'w_k': nrm((D_MODEL, hk), D_MODEL ** -0.5),
        'w_v': nrm((D_MODEL, hk), D_MODEL ** -0.5),
        'k_norm': 1.0 + nrm((HEAD_DIM,), 0.05),
        'w_q': nrm((N_B_LAYERS, D_MODEL, hq), D_MODEL ** -0.5),
        'q_norm': 1.0 + nrm((N_B_LAYERS, HEAD_DIM), 0.05),
        'sinks': nrm((N_B_LAYERS, N_HEADS), 0.5),
        'w_o': nrm((N_B_LAYERS, hq, D_MODEL), hq ** -0.5),
        'rel_bias': nrm((NUM_BUCKETS, N_HEADS), 0.1),
        'w_up': nrm((DEPTH, D_MODEL, 2 * D_FF), D_MODEL ** -0.5),
        'conv_w': nrm((DEPTH, CONV_WIDTH, 2 * D_FF), CONV_WIDTH ** -0.5),
        'conv_b': nrm((DEPTH, 2 * D_FF), 0.01),
        'w_down': nrm((DEPTH, D_FF, D_MODEL), D_FF ** -0.5),
        'w_ple_in': nrm((DEPTH, PLE_DIM, D_MODEL), PLE_DIM ** -0.5),
        'w_ple_gate': nrm((DEPTH, D_MODEL, D_MODEL), D_MODEL ** -0.5),
    }

def reference(x_prompt, x_sample, state_ssm_re, state_ssm_im, state_ffn_conv, cache_k_win, cache_v_win,
              p_prompt, p_sample, g_mix, g_ffn, g_ple, ssm_lam_re, ssm_lam_im, ssm_log_dt, ssm_b_re,
              ssm_b_im, ssm_c_re, ssm_c_im, ssm_d, w_glu, b_glu, g_kv, w_k, w_v, k_norm, w_q, q_norm,
              sinks, w_o, rel_bias, w_up, conv_w, conv_b, w_down, w_ple_in, w_ple_gate):
    prm = dict(g_mix=g_mix, g_ffn=g_ffn, g_ple=g_ple, ssm_lam_re=ssm_lam_re, ssm_lam_im=ssm_lam_im,
               ssm_log_dt=ssm_log_dt, ssm_b_re=ssm_b_re, ssm_b_im=ssm_b_im, ssm_c_re=ssm_c_re,
               ssm_c_im=ssm_c_im, ssm_d=ssm_d, w_glu=w_glu, b_glu=b_glu, g_kv=g_kv, w_k=w_k, w_v=w_v,
               k_norm=k_norm, w_q=w_q, q_norm=q_norm, sinks=sinks, w_o=w_o, rel_bias=rel_bias,
               w_up=w_up, conv_w=conv_w, conv_b=conv_b, w_down=w_down, w_ple_in=w_ple_in,
               w_ple_gate=w_ple_gate)
    bp = x_prompt.shape[0]
    zero_ssm = jnp.zeros((N_A_LAYERS, bp, N_GROUPS, SSM_STATE), jnp.float32)
    zero_conv = jnp.zeros((DEPTH, bp, CONV_WIDTH - 1, 2 * D_FF), x_prompt.dtype)
    zero_win = jnp.zeros((bp, WINDOW, N_KV_HEADS, HEAD_DIM), x_prompt.dtype)
    y_prompt, ssm_re_p, ssm_im_p, conv_p, k_win_p, v_win_p = _trunk(
        x_prompt, p_prompt, zero_ssm, zero_ssm, zero_conv, zero_win, zero_win, False, prm)
    y_sample, ssm_re_s, ssm_im_s, conv_s, k_win_s, v_win_s = _trunk(
        x_sample, p_sample, state_ssm_re, state_ssm_im, state_ffn_conv, cache_k_win, cache_v_win, True, prm)
    return (y_prompt, y_sample, ssm_re_p, ssm_im_p, ssm_re_s, ssm_im_s, conv_p, conv_s,
            k_win_p, v_win_p, k_win_s, v_win_s)


_drawn_inputs = setup_inputs


def setup_inputs(seed=0):
    import zlib

    import numpy as np

    out = dict(_drawn_inputs(seed))
    spreads = {}
    factors = {'g_ple': 5.487,
     'ssm_lam_re': 17.308,
     'b_glu': 8.0,
     'q_norm': 8.0,
     'sinks': 50.336,
     'rel_bias': 4.837,
     'conv_b': 6.333}
    for name, (base, spread) in spreads.items():
        noise = np.random.default_rng([zlib.crc32(name.encode()), seed]).standard_normal(out[name].shape)
        drawn = base * np.exp(spread * noise) if base else spread * noise
        out[name] = jnp.asarray(drawn.astype(out[name].dtype))
    for name, factor in factors.items():
        out[name] = (out[name] * factor).astype(out[name].dtype)
    return out
```

```python
import math
from contextlib import ExitStack

import numpy as np
import concourse.bass as bass
from concourse import mybir

F32 = mybir.dt.float32
F32R = mybir.dt.float32r
I32 = mybir.dt.int32
ALU = mybir.AluOpType
ACT = mybir.ActivationFunctionType
AX_X = mybir.AxisListType.X

P = 128
D = 1024
KC = D // P
SEQ = 512
NSEQ = 8
STEPS = 4
NTOK = SEQ + NSEQ * STEPS
HT = NTOK // 2
HP = SEQ // 2
HS_ = HT - HP
NBLK = SEQ // STEPS
HB = HT // STEPS
HPB = HP // STEPS
NCOL = NTOK // STEPS
PAIRS = 32
FQ = 4
CG = 16
FF = 2816
FC = FF // P
EXT = 2 + SEQ + NSEQ * (2 + STEPS)
CONV = EXT - 2
WKW = EXT + 4
TAIL0 = SEQ
KVH = 4
RQ = 4
HD = 64
WIN = 128
NBUCK = 32
MAXD = 128
PLE = 256
SLOT = 11
EPS = 1e-6
NEG = -1.0e30
BW = 384

C_ID, C_OH, C_BM, C_SEL, C_W = 0, 128, 128 + BW, 164 + BW, 292 + BW

(LR, LI, DT, A_RE, A_IM, C1, S1, R4, E_RE, E_IM, MAG, X0, X1, X2, X3, X4, X5, X6, X7, X8, F_RE, F_IM,
 A2_RE, A2_IM, A4_RE, A4_IM, KI) = range(27)
PRN_ = 27

V_GMIX, V_GFFN, V_GPLE, V_GKV, V_D, V_BGLU, V_KN, V_QN, V_N = 0, 16, 32, 48, 56, 64, 80, 81, 82


def constants():
    c = np.zeros((P, C_W), np.float32)
    c[:, C_ID:C_ID + P] = np.eye(P, dtype=np.float32)
    for x in range(BW):
        d = BW - P - 1 - x
        if 0 <= d <= WIN:
            half = NBUCK // 2
            if d < half:
                b = d
            else:
                f = np.log(np.float32(d) / np.float32(half)) / np.float32(math.log(MAXD / half))
                b = min(half + int(np.float32(f) * np.float32(NBUCK - half)), NBUCK - 1)
            c[b, C_OH + x] = 1.0
        else:
            c[NBUCK, C_OH + x] = 1.0
    for b in range(NSEQ):
        for b2 in range(NSEQ):
            if b != b2:
                c[16 * b:16 * b + 16, C_BM + 4 * b2:C_BM + 4 * b2 + 4] = NEG
    for row in range(P):
        c[row, C_BM + 32 + row // STEPS % RQ] = 1.0
    c[0, C_SEL:C_SEL + 64] = 1.0
    c[1, C_SEL + 64:C_SEL + 128] = 1.0
    return c


class Chain:

    def __init__(self, eng, sem):
        self.eng, self.sem, self.base, self.k, self.i, self.per = eng, sem, 0, 0, None, 0

    def link(self, ins):
        self.k += 1
        ins.then_inc(self.sem, 1)
        at = self.base + self.k
        self.eng.wait_ge(self.sem, at if self.i is None else self.i * self.per + at)

    def enter(self, i, per):
        self.base += self.k
        self.k, self.i, self.per = 0, i, per

    def leave(self, turns):
        assert self.k == self.per, (self.k, self.per)
        self.base += turns * self.per
        self.k, self.i = 0, None


def build(nc, x_prompt, x_sample, state_ssm_re, state_ssm_im, state_ffn_conv, cache_k_win, cache_v_win,
          p_prompt, p_sample, g_mix, g_ffn, g_ple, ssm_lam_re, ssm_lam_im, ssm_log_dt, ssm_b_re,
          ssm_b_im, ssm_c_re, ssm_c_im, ssm_d, w_glu, b_glu, g_kv, w_k, w_v, k_norm, w_q, q_norm,
          sinks, w_o, rel_bias, w_up, conv_w, conv_b, w_down, w_ple_in, w_ple_gate, consts, bias_rows,
          y_prompt, y_sample, ssm_re_p, ssm_im_p, ssm_re_s, ssm_im_s, conv_p, conv_s,
          k_win_p, v_win_p, k_win_s, v_win_s):
    with ExitStack() as ctx:
        sems = {}

        def shared(name):
            stage, _, what = name.partition("_")
            if stage in ("n0", "n1", "n2", "n3", "n4", "n5", "n6", "xq") and what:
                if what in ("sq", "summed"):
                    return "norm_" + what, KC * int(stage[1])
                if what == "root":
                    return "norm_root", int(stage[1])
                if what == "h":
                    return "residual_added", KC * (int(stage[1]) - 1)
                return "norm_" + what, KC * ("n1", "n2", "n3", "xq", "n4", "n5").index(stage)
            if stage in ("up0", "up1"):
                return "up_" + what, FC * int(stage[2])
            if stage in ("ple0", "ple1"):
                return "ple_" + what, KC * int(stage[3])
            if name[:-1] in ("cst_in", "ct_done", "ct_made", "cs_turned", "cs_done", "p_made", "p_high", "p_done"):
                return name[:-1], {"cst_in": 48, "ct_done": FC // 2, "ct_made": FC // 2}.get(name[:-1], 1) * int(name[-1])
            return name, 0

        def sem(name):
            name, _ = shared(name)
            if name not in sems:
                sems[name] = ctx.enter_context(nc.semaphore(name))
            return sems[name]

        def before(name):
            return shared(name)[1]

        base = (nc.sbuf_base + 31) // 32 * 32
        room = (nc.sbuf_usable_end - base) // 32 * 32
        ctx.enter_context(nc.sbuf_tensor("arena", [P, room // 4 - 8], F32))

        class Region:
            def __init__(self, at):
                self.at = at

            def __call__(self, name, shape, dt=F32):
                t = nc.alloc_sbuf_tensor_at(name, shape, dt, offset=self.at)
                self.at += (int(np.prod(shape[1:])) * 4 + 31) // 32 * 32
                assert self.at <= base + room - 32, (name, self.at - base - room)
                return t

        perm = Region(base)
        H = perm("H", [P, KC, NTOK])
        n_at = perm.at
        NH = perm("NH", [P, KC, NTOK], F32R)
        nl_at = perm.at
        NL = perm("NL", [P, KC, NTOK], F32R)
        RAW = perm("RAW", [P, 2, SLOT, P])
        SPL = perm("SPL", [P, 2, 2, SLOT, P], F32R)
        WK = perm("WK", [P, 4, WKW])
        RSTD = perm("RSTD", [P, NTOK])
        ONES = perm("ONES", [P, P])
        BONES = perm("BONES", [P, P])
        IDN = perm("IDN", [P, P])
        VEC = perm("VEC", [P, V_N])
        CP = perm("CP", [P, 2, 4, FC * 2])
        EPSB = perm("EPSB", [P, 1])
        TIC2 = perm("TIC2", [P, 1])
        TIC = perm("TIC", [P, 1])
        TT = RSTD
        SQ = WK[:, 0, 0:NTOK]
        NT = [WK[:, 1, 0:NTOK], WK[:, 2, 0:NTOK]]
        SG = WK[:, 3, 0:NTOK]

        U = nc.alloc_sbuf_tensor_at("U", [P, KC, NTOK], F32, offset=n_at)
        PC = nc.alloc_sbuf_tensor_at("PC", [P, KC, NTOK], F32, offset=nl_at)
        ph1 = Region(perm.at)
        EROT = ph1("EROT", [P, 2, PAIRS, NBLK])
        CAC = ph1("CAC", [P, 5, 2, PAIRS, CG])
        H0 = ph1("H0", [P, 2, NSEQ, PAIRS])
        VSM = ph1("VSM", [P, 2, NSEQ, PAIRS])
        FS = ph1("FS", [P, 2, PAIRS])
        PRN = PRN_
        PR = ph1("PR", [P, PRN, PAIRS])
        xs_at = ph1.at
        BT = ph1("BT", [P, 8, 2, P])
        PBD = ph1("PBD", [P, 8, P])
        CBD = ph1("CBD", [P, 4, 2, P])
        C0BD = ph1("C0BD", [P, 2, P])
        KM = ph1("KM", [P, 2, 4, P])
        xs_room = ph1.at
        UF = ph1("UF", [P, 2, NTOK])
        V = ph1("V", [P, 2, FQ, NBLK])
        T2 = ph1("T2", [P, 2, FQ, NBLK])
        HSV = ph1("HSV", [P, 2, 2, FQ, NCOL])
        T1 = WK[:, 2:4, :].rearrange("p a b -> p (a b)")[:, 0:2 * FQ * NBLK]
        YT, ZT = WK[:, 0, 0:NTOK], WK[:, 1, 0:NTOK]
        XS = nc.alloc_sbuf_tensor_at("XS", [P, 5, D], F32, offset=xs_at)
        stg = Region(max(xs_room, xs_at + 5 * D * 4))
        LAMS = stg("LAMS", [64, P])
        VECS = stg("VECS", [V_N, P])
        CPS = stg("CPS", [88, 4, P])
        CS_ = stg("CSTG", [P, 2, 4, P])
        STS = stg("STS", [P, 2, 2, P])
        BC = stg("BC", [P, 2, PAIRS, CG])
        TAB = stg("TAB", [P, 2, 512])
        TE = stg("TE", [P, 2, 1024])
        LD2 = stg("LD2", [2, PAIRS])
        SEL = stg("SEL", [2, P])


        ff = Region(perm.at)
        AH = ff("AH", [P, FC, NTOK], F32R)
        AL = ff("AL", [P, FC, NTOK], F32R)
        PTH = ff("PTH", [P, 2, NTOK], F32R)
        PTL = ff("PTL", [P, 2, NTOK], F32R)
        CSP = ff("CSP", [P, 2 * FC, 2 * NSEQ])
        CT = ff("CT", [P, 2 * FC, 18])

        fst = Region(perm.at)
        CST = fst("CST", [16, 2 * FF])
        CTO = nc.alloc_sbuf_tensor_at("CTO", [18, 2 * FF], F32, offset=perm.at)
        yst = Region(perm.at)
        YS = yst("YS", [P, 2, D])
        HSMP = yst("HSMP", [P, KC, 32])
        FSO = nc.alloc_sbuf_tensor_at("FSO", [PAIRS, 2, P], F32, offset=xs_at)
        VSO = nc.alloc_sbuf_tensor_at("VSO", [P, 2, 2, P], F32, offset=xs_at + 1024)
        PST = nc.alloc_sbuf_tensor_at("PST", [P, 5, PLE], F32, offset=fst.at + 32)

        at = Region(perm.at)
        QN = at("QN", [P, KC, NTOK])
        KN = at("KN", [P, 2, NTOK])
        VT = at("VT", [P, 2, NTOK])
        VTOK = at("VTOK", [P, 4, KVH * HD])
        KVS = at("KVS", [2 * NSEQ * 2, 2, KVH * HD])
        KTP = at("KTP", [P, KVH * HD])
        KCT = at("KCT", [P, 2, NSEQ, WIN])
        VCS = at("VCS", [P, NSEQ, KVH * HD])
        RBR = at("RBR", [16, BW])
        RB = at("RB", [NBUCK + 1, 16])
        OHB = at("OHB", [NBUCK + 1, BW])
        BM = at("BM", [P, 32 + RQ])
        SNK = at("SNK", [P, 16])
        SNKS = at("SNKS", [P, KVH])
        SBT = at("SBT", [P, KVH, WIN + STEPS])
        SBI = at("SBI", [P, KVH, 160])
        BIAS = at("BIAS", [P, 16, 256])
        VTS = at("VTS", [P, 2, 32])
        SM = at("SM", [P, 2, 6, 4])
        ux = Region(at.at)
        XQH = ux("XQH", [P, KC, NTOK], F32R)
        XQL = ux("XQL", [P, KC, NTOK], F32R)
        ug = Region(at.at)
        PB = ug("PB", [P, 2, 4, 256])
        KCS = ug("KCS", [P, NSEQ, KVH * HD])
        PTR = ug("PTR", [P, 2, 2, 512])


        ACC = ctx.enter_context(nc.psum_tensor("ACC", [P, 4, 512], F32))
        SS = ctx.enter_context(nc.psum_tensor("SS", [P, 2, 512], F32))
        MI = ctx.enter_context(nc.psum_tensor("MI", [P, 2, 512], F32))

        def acc(u):
            return ACC[:, 2 * u:2 * u + 2, 0:HT]

        def halves(row):
            return row.rearrange("p (h t) -> p h t", h=2)

        order = [("glu", 16), ("up0", 44), ("down0", 16), ("ple0", 8), ("kv", 4), ("q", 8), ("wo", 8),
                 ("up1", 44), ("down1", 16), ("ple1", 8)]
        first, at_ = {}, 0
        for name, n in order:
            first[name] = at_
            at_ += n

        def strip_of(name, n):
            return n + first[name]

        block = ctx.enter_context(nc.Block())
        outs = [0]

        @block.sync
        def _(sp):
            LOAD = [sem("load0"), sem("load1")]

            with nc.allow_non_contiguous_dma(reason="64 small elements"):
                sp.dma_start(IDN[:], consts[:, C_ID:C_ID + P]).then_inc(sem("const_in"), 16)
                sp.dma_start(SEL[:], consts[0:2, C_SEL:C_SEL + P]).then_inc(sem("const_in"), 16)
                sp.dma_start(LAMS[0:32, :], ssm_lam_re[0].rearrange("(q a) s -> q (a s)", a=2)).then_inc(sem("lam_in"), 16)
                sp.dma_start(LAMS[32:64, :], ssm_lam_im[0].rearrange("(q a) s -> q (a s)", a=2)).then_inc(sem("lam_in"), 16)
                sp.dma_start(LD2[:], ssm_log_dt[0].rearrange("(q a) -> a q", a=2)).then_inc(sem("lam_in"), 16)
            for r, src in enumerate((ssm_b_re, ssm_b_im)):
                sp.dma_start(BC[:, r], src[0].rearrange("(q a) s c -> (a s) q c", a=2)).then_inc(sem("b_in"), 16)
            for r, src in enumerate((ssm_c_re, ssm_c_im)):
                for t in range(4):
                    for a in range(2):
                        sp.dma_start(CS_[:, r, t, 64 * a:64 * a + 64],
                                     src[0].rearrange("(t q a) c s -> t a q c s", t=4, a=2)[t, a]).then_inc(sem("c_in"), 16)
            for b in range(4):
                sp.dma_start(XS[:, b, :], x_prompt[0, P * b:P * b + P, :]).then_inc(sem("x_in"), 16)
            sp.dma_start(XS[0:32, 4, :], x_sample.rearrange("b t d -> (b t) d")).then_inc(sem("x_in"), 16)
            for at0, src in ((V_GMIX, g_mix), (V_GFFN, g_ffn), (V_GPLE, g_ple)):
                sp.dma_start(VECS[at0:at0 + 16, :], src.rearrange("l (c p) -> (l c) p", p=P)).then_inc(sem("vec_in"), 16)
            sp.dma_start(VECS[V_GKV:V_GKV + 8, :], g_kv.rearrange("(c p) -> c p", p=P)).then_inc(sem("vec_in"), 16)
            sp.dma_start(VECS[V_D:V_D + 8, :], ssm_d.rearrange("l (c p) -> (l c) p", p=P)).then_inc(sem("vec_in"), 16)
            sp.dma_start(VECS[V_BGLU:V_BGLU + 16, :], b_glu.rearrange("l (c p) -> (l c) p", p=P)).then_inc(sem("vec_in"), 16)
            for row, src in ((V_KN, k_norm.rearrange("(a d) -> a d", a=1)), (V_QN, q_norm)):
                for a in range(2):
                    sp.dma_start(VECS[row:row + 1, 64 * a:64 * a + 64], src).then_inc(sem("vec_in"), 16)
            for r, src in enumerate((state_ssm_re, state_ssm_im)):
                for hf in range(2):
                    sp.dma_start(STS[:, r, hf, :],
                                 src[0].rearrange("b (h q a) s -> h b q (a s)", h=2, a=2)[hf]).then_inc(sem("st_in"), 16)
            for l in range(2):
                sp.dma_start(CPS[0:44, 2 * l, :], conv_b[l].rearrange("(c p) -> c p", p=P)).then_inc(sem("cp_in"), 16)
                sp.dma_start(CPS[44:88, 2 * l, :], conv_w[l, 0].rearrange("(c p) -> c p", p=P)).then_inc(sem("cp_in"), 16)
                sp.dma_start(CPS[0:44, 2 * l + 1, :], conv_w[l, 1].rearrange("(c p) -> c p", p=P)).then_inc(sem("cp_in"), 16)
                sp.dma_start(CPS[44:88, 2 * l + 1, :], conv_w[l, 2].rearrange("(c p) -> c p", p=P)).then_inc(sem("cp_in"), 16)

            def columns(w, c0, n=P):
                return w.rearrange("(k p) n -> p k n", p=P)[:, :, bass.ds(c0, n)]

            def stream(name, parts):
                def turn(i, free):
                    for u in range(2):
                        if free:
                            sp.wait_ge(sem("split_done"), i * 2 + (strip_of(name, u) - 1))
                        todo = parts(i, u)
                        for dst, src in todo:
                            sp.dma_start(dst, src).then_inc(LOAD[u], 64 // len(todo))

                n = dict(order)[name] // 2
                if name == "glu":
                    turn(0, False)
                    with sp.Fori(1, n) as i:
                        turn(i, True)
                else:
                    with sp.Fori(0, n) as i:
                        turn(i, True)

            def up_parts(l):
                return lambda i, u: [(RAW[:, u, 0:KC, :], columns(w_up[l], i * P + FF * u))]

            def down_parts(l):
                return lambda i, u: [(RAW[:, u, 0:SLOT, :],
                                      w_down[l, SLOT * P * u:SLOT * P * (u + 1), :].rearrange("(k p) n -> p k n", p=P)[:, :, bass.ds(i * P, P)])]

            def ple_parts(l):
                return lambda i, u: [(RAW[:, u, 0:KC, :], columns(w_ple_gate[l], i * 2 * P + P * u)),
                                     (RAW[:, u, KC:KC + 2, :], columns(w_ple_in[l], i * 2 * P + P * u))]

            stream("glu", lambda i, u: [(RAW[:, u, 0:KC, :], columns(w_glu[0], i * P + D * u))])
            stream("up0", up_parts(0))
            stream("down0", down_parts(0))
            stream("ple0", ple_parts(0))
            for s in range(4):
                sp.wait_ge(sem("split_done"), strip_of("kv", s) - 1)
                sp.dma_start(RAW[:, s % 2, 0:KC, :], columns((w_k, w_v)[s // 2], (s % 2) * P)).then_inc(LOAD[s % 2], 64)
            for s in range(8):
                p2, r = s // 4, s % 4
                sp.wait_ge(sem("split_done"), strip_of("q", s) - 1)
                for a in range(2):
                    sp.dma_start(RAW[:, s % 2, 0:KC, HD * a:HD * a + HD],
                                 columns(w_q[0], (8 * p2 + 4 * a + r) * HD, HD)).then_inc(LOAD[s % 2], 32)
            wo_v = w_o[0].rearrange("(p a r d) n -> p a d r n", p=2, a=2, r=4)
            stream("wo", lambda i, u: [(RAW[HD * a:HD * a + HD, u, 4 * p2:4 * p2 + 4, :],
                                        wo_v[p2, a, :, :, bass.ds(i * 2 * P + P * u, P)])
                                       for p2 in range(2) for a in range(2)])
            stream("up1", up_parts(1))
            stream("down1", down_parts(1))
            stream("ple1", ple_parts(1))

        @block.gpsimd
        def _(pool):
            chain = Chain(pool, sem("pool_chain"))
            LOAD = [sem("load0"), sem("load1")]
            PIN = nc.gpsimd
            chain.link(PIN.memset(ONES[:], 1.0))
            chain.link(PIN.memset(EPSB[:], EPS))
            chain.link(PIN.memset(BONES[0:64, 64:128], 0.0))
            chain.link(PIN.memset(BONES[64:128, 0:64], 0.0))
            chain.link(PIN.memset(BONES[0:64, 0:64], 1.0))
            chain.link(PIN.memset(BONES[64:128, 64:128], 1.0))
            PIN.memset(TIC[:], 0.0).then_inc(sem("ones_set"), 1)
            pool.wait_ge(sem("a_ready"), 1)
            pool.wait_ge(sem("c_turned"), 2)

            def wide(j):
                return PR[:, j, :].unsqueeze(2).to_broadcast([P, PAIRS, CG])

            tab = [TAB[:, j, :].rearrange("p (q c) -> p q c", c=CG) for j in range(2)]
            for i in range(4):
                for o in range(2):
                    chain.link(PIN.tensor_tensor(tab[0], CAC[:, i, 0], wide(A_RE + o), ALU.mult))
                    chain.link(PIN.tensor_tensor(tab[1], CAC[:, i, 1], wide(A_IM - o), ALU.mult))
                    chain.link(PIN.tensor_tensor(CAC[:, i + 1, o], tab[0], tab[1], (ALU.subtract, ALU.add)[o]))
            PIN.memset(TAB[:, 0, 0:1], 0.0).then_inc(sem("ca_ready"), 1)
            pool.wait_ge(sem("x_turned"), KC + 1)
            for t in (BT, PBD, CBD, C0BD):
                chain.link(PIN.memset(t[:], 0.0))
            PIN.memset(KM[:], 0.0).then_inc(sem("zeros_set"), 1)

            def split(name, i, u, kt, count):
                n = i * 2 + strip_of(name, u)
                hi, lo = SPL[:, u, 0, 0:kt, :], SPL[:, u, 1, 0:kt, :]
                pool.wait_ge(LOAD[u], (n - u) * 32 + 64)
                if count:
                    pool.wait_ge(sem("strip_done"), n - 1)
                PIN.tensor_tensor(TIC[:], EPSB[:], EPSB[:], ALU.add)
                PIN.tensor_scalar(hi, RAW[:, u, 0:kt, :], 1.0, 1.0, ALU.mult, ALU.mult).then_inc(sem("high_done"), 1)
                pool.wait_ge(sem("high_done"), n + 1)
                PIN.tensor_tensor(lo, RAW[:, u, 0:kt, :], hi.bitcast(F32), ALU.subtract).then_inc(sem("split_done"), 1)

            for name, n in order:
                kt = {"down": SLOT, "ple": KC + 2}.get(name.rstrip("01"), KC)
                if name == "glu":
                    for u in range(2):
                        split(name, 0, u, kt, False)
                with pool.Fori(1 if name == "glu" else 0, n // 2) as i:
                    for u in range(2):
                        split(name, i, u, kt, True)

        @block.tensor
        def _(pe):
            mm = nc.tensor.matmul
            tr = nc.tensor.transpose

            def turn(out, in_, rows):
                return tr(out, in_, IDN[0:rows, 0:rows])

            pe.wait_ge(sem("const_in"), 32)
            pe.wait_ge(sem("lam_in"), 48)
            turn(SS[:, 0, 0:64], LAMS[:], 64)
            mm(SS[:, 0, 64:96], SEL[:], LD2[:], start=True, stop=True).then_inc(sem("lam_turned"), 1)
            pe.wait_ge(sem("c_in"), 256)
            for r in range(2):
                for t in range(4):
                    last = turn(ACC[:, 2 + r, P * t:P * t + P], CS_[:, r, t, :], P)
                last.then_inc(sem("c_made"), 1)
            pe.wait_ge(sem("x_in"), 80)
            for m in range(KC):
                if m >= 2:
                    pe.wait_ge(sem("x_turned"), m - 1)
                for b in range(4):
                    last = turn(MI[:, m % 2, P * b:P * b + P], XS[:, b, P * m:P * m + P], P)
                last.then_inc(sem("x_made"), 1)
            for m in range(KC):
                last = turn(ACC[:, 0, 32 * m:32 * m + 32], XS[0:32, 4, P * m:P * m + P], 32)
            last.then_inc(sem("x_made"), 1)
            pe.wait_ge(sem("vec_in"), 160)
            turn(SS[:, 1, 0:V_N], VECS[:], V_N).then_inc(sem("vec_made"), 1)
            pe.wait_ge(sem("cp_in"), 128)
            for t in range(4):
                last = turn(ACC[:, 1, 88 * t:88 * t + 88], CPS[:, t, :], 88)
            last.then_inc(sem("cp_made"), 1)
            pe.wait_ge(sem("st_in"), 64)
            pe.wait_ge(sem("x_turned"), KC)
            for r in range(2):
                for h in range(2):
                    last = turn(MI[:, r, P * h:P * h + P], STS[:, r, h, :], P)
            last.then_inc(sem("st_made"), 1)

            def sumsq(name, m, start=False, stop=False):
                pe.wait_ge(sem(name + "_sq"), m + 1 + before(name + "_sq"))
                for h in range(2):
                    last = mm(SS[:, h, 0:HT], ONES[:], SQ[:, HT * h:HT * h + HT], start=start, stop=stop)
                last.then_inc(sem(name + "_summed"), 1)

            pe.wait_ge(sem("ones_set"), 1)
            pe.wait_ge(sem("lam_taken"), 1)
            pe.wait_ge(sem("vec_done"), 1)
            for m in range(KC):
                sumsq("n0", m, m == 0, m == KC - 1)

            Y = SS[:].rearrange("p a (i n) -> p (a i) n", i=2)

            def prep(f, par, early=False):
                pe.wait_ge(sem("pbd_ready"), f + 1)
                if not early:
                    pe.wait_ge(sem("bt_a"), f)
                    pe.wait_ge(sem("bt_d"), f)
                for j in range(8):
                    last = turn(MI[:, j // 4, P * (j % 4):P * (j % 4) + P], PBD[:, j, :], P)
                last.then_inc(sem("p_turned"), 1)

            def kernels(f, wait_y=True):
                if wait_y:
                    pe.wait_ge(sem("y_taken"), f - 1)
                for q in range(FQ):
                    rows = slice(32 * q, 32 * q + 32)
                    for t in range(4):
                        for r in range(2):
                            last = mm(SS[rows, 0, 32 * t:32 * t + 32], PBD[:, 2 * t + r, rows], C0BD[:, r, rows],
                                      start=r == 0, stop=r == 1, skip_group_check=True)
                last.then_inc(sem("k_made"), 1)

            def inputs(f, par, early=False):
                pe.wait_ge(sem("bt_a"), f + 1)
                pe.wait_ge(sem("bt_d"), f + 1)
                pe.wait_ge(sem("uf_ready"), f + 1)
                if not early:
                    pe.wait_ge(sem("v_taken"), f)
                for q in range(FQ):
                    rows = slice(64 * (q // 2), 64 * (q // 2) + 64)
                    for r in range(2):
                        for j in range(STEPS):
                            last = mm(ACC[:, q, NCOL * r:NCOL * r + NCOL], BT[rows, 2 * (3 - j) + r, q % 2, :],
                                      UF[rows, par, j:NTOK:STEPS], start=j == 0, stop=j == 3, skip_group_check=True)
                last.then_inc(sem("v_made"), 1)

            def outputs(f, par, early=False):
                pe.wait_ge(sem("k_done"), f + 1)
                pe.wait_ge(sem("cbd_ready"), f + 1)
                pe.wait_ge(sem("h_ready"), f + 1)
                pe.wait_ge(sem("h0_placed"), f + 1)
                if not early:
                    pe.wait_ge(sem("y_taken"), f)
                for i in range(STEPS):
                    for j in range(i + 1):
                        mm(Y[:, i, 0:NCOL], KM[:, par, i - j, :], UF[:, par, j:NTOK:STEPS], start=j == 0, stop=False,
                           skip_group_check=True)
                    for r in range(2):
                        for q in range(FQ):
                            rows = slice(32 * q, 32 * q + 32)
                            last = mm(Y[rows, i, 0:NCOL], CBD[:, i, r, rows], HSV[:, par, r, q, :], start=False,
                                      stop=r == 1, skip_group_check=True)
                last.then_inc(sem("y_made"), 1)

            prep(0, 0, True)
            pe.wait_ge(sem("n0_root"), 1 + before("n0_root"))
            pe.wait_ge(sem("c0_ready"), 1)
            kernels(0, False)
            inputs(0, 0, True)
            prep(1, 1)
            pe.wait_ge(sem("c0_ready"), 2)
            pe.wait_ge(sem("k_done"), 1)
            kernels(1, False)
            inputs(1, 1)
            pe.wait_ge(sem("k_done"), 2)
            outputs(0, 0, True)
            for f in range(2, KC):
                prep(f, f % 2)
                pe.wait_ge(sem("c0_ready"), f + 1)
                kernels(f)
                inputs(f, f % 2)
                pe.wait_ge(sem("k_done"), f + 1)
                outputs(f - 1, (f - 1) % 2)
            outputs(KC - 1, 1)
            pe.wait_ge(sem("fs_ready"), 1)
            for r in range(2):
                turn(MI[0:PAIRS, 1, P * r:P * r + P], FS[:, r, :], P)
                for h in range(2):
                    last = turn(MI[:, 0, P * (2 * r + h):P * (2 * r + h) + P],
                                VSM[:, r, 4 * h:4 * h + 4, :].rearrange("p b q -> p (b q)"), P)
            last.then_inc(sem("fs_turned"), 1)

            def product(u, out, kt, k0, xh, xl, start, stop, w0=0, ready=None):
                for k in range(kt):
                    if ready:
                        pe.wait_ge(sem(ready), k0 + k + 1 + before(ready))
                    for n, (w, x) in enumerate(((0, xh), (0, xl), (1, xh))):
                        for h in range(2):
                            last = mm(out[:, h, :], SPL[:, u, w, w0 + k, :], x[:, k0 + k, HT * h:HT * h + HT],
                                      start=start and k == 0 and n == 0, stop=stop and k == kt - 1 and n == 2)
                return last

            def strip(name, i, u, per=2):
                pe.wait_ge(sem("split_done"), i * per + (strip_of(name, u) + 1))

            def glu(i, ready=None, free=True):
                for u in range(2):
                    strip("glu", i, u)
                    if free:
                        pe.wait_ge(sem("glu_taken%d" % u), i + before("glu_taken%d" % u))
                    product(u, acc(u), KC, 0, NH, NL, True, True, ready=ready if u == 0 else None).then_inc(sem("strip_done"), 1)

            pe.wait_ge(sem("v_taken"), KC)
            glu(0, ready="z_split", free=False)
            glu(1)
            pe.wait_ge(sem("y_taken"), KC)
            sumsq("n1", 0, start=True)
            with pe.Fori(2, KC) as i:
                glu(i)
                sumsq("n1", i - 1)
            sumsq("n1", KC - 1, stop=True)

            def up(l):
                name = "up%d" % l
                pe.wait_ge(sem("cst_in%d" % l), 48 + before("cst_in%d" % l))
                if l == 0:
                    pe.wait_ge(sem("fs_out"), 1)
                    pe.wait_ge(sem("glu_taken1"), KC)
                    pe.wait_ge(sem("glu_taken0"), KC)
                else:
                    pe.wait_ge(sem("n4_h"), KC + before("n4_h"))
                for c in range(2 * FC):
                    last = turn(MI[:, c // FC, 16 * (c % FC):16 * (c % FC) + 16], CST[:, P * c:P * c + P], 16)
                last.then_inc(sem("cs_turned%d" % l), 1)
                pe.wait_ge(sem("cs_done%d" % l), 1 + before("cs_done%d" % l))
                for c in range(2):
                    for b in range(4):
                        turn(MI[:, c, P * b:P * b + P], PST[:, b, P * c:P * c + P], P)
                for c in range(2):
                    last = turn(ACC[:, 3, 32 * c:32 * c + 32], PST[0:32, 4, P * c:P * c + P], 32)
                last.then_inc(sem("p_made%d" % l), 1)

                def body(i, ready=None, free=True):
                    for u in range(2):
                        strip(name, i, u)
                        if free:
                            pe.wait_ge(sem(name + ("_gate", "_val")[u]), i + before(name + ("_gate", "_val")[u]))
                        elif u == 1:
                            pe.wait_ge(sem("p_done%d" % l), 1 + before("p_done%d" % l))
                        product(u, acc(u), KC, 0, NH, NL, True, True, ready=ready if u == 0 else None).then_inc(sem("strip_done"), 1)

                body(0, "n%d_split" % (1 + 3 * l), False)
                with pe.Fori(1, FC) as i:
                    body(i)

            def down(l):
                name, norm, upn = "down%d" % l, "n%d" % (2 + 3 * l), "up%d" % l

                def one(i, v, first=False, start=False):
                    for u in range(2):
                        pe.wait_ge(sem("split_done"), i * 4 + (strip_of(name, 2 * v + u) + 1))
                        if u == 0 and not start:
                            pe.wait_ge(sem(norm + "_h"), i * 2 + (v - 1) + before(norm + "_h"))
                        last = product(u, acc(v), SLOT, SLOT * u, AH, AL, u == 0, u == 1,
                                       ready=upn + "_low" if first else None)
                        last.then_inc(sem("strip_done"), 1)

                pe.wait_ge(sem(upn + "_gate"), FC + before(upn + "_gate"))
                one(0, 0, True, True)
                pe.wait_ge(sem(upn + "_val"), FC + before(upn + "_val"))
                one(0, 1, False, True)
                sumsq(norm, 0, start=True)
                with pe.Fori(1, KC // 2) as i:
                    one(i, 0)
                    sumsq(norm, i * 2 - 1)
                    one(i, 1)
                    sumsq(norm, i * 2)
                sumsq(norm, KC - 1, stop=True)
                for g in range(FC // 2):
                    if g >= 2:
                        pe.wait_ge(sem("ct_done%d" % l), g - 1 + before("ct_done%d" % l))
                    for c in range(4):
                        last = turn(MI[0:18, g % 2, P * c:P * c + P], CT[:, 4 * g + c, :], P)
                    last.then_inc(sem("ct_made%d" % l), 1)

            def ple(l):
                name, norm = "ple%d" % l, "n%d" % (3 + 3 * l)

                def one(i, u, ready=None, start=False):
                    strip(name, i, u)
                    if not start:
                        pe.wait_ge(sem(norm + "_h"), i * 2 + (u - 1) + before(norm + "_h"))
                    product(u, acc(u), KC, 0, NH, NL, True, True, ready=ready)
                    if ready:
                        pe.wait_ge(sem("ct_done%d" % l), FC // 2 + before("ct_done%d" % l))
                    else:
                        pe.wait_ge(sem(name + "_in"), i * 2 + u + before(name + "_in"))
                    product(u, MI[:, :, 0:HT], 2, 0, PTH, PTL, True, True, w0=KC).then_inc(sem("strip_done"), 1)

                one(0, 0, "n%d_split" % (2 + 3 * l), True)
                one(0, 1, None, True)
                if l == 0:
                    sumsq(norm, 0, start=True)
                with pe.Fori(1, KC // 2) as i:
                    one(i, 0)
                    if l == 0:
                        sumsq(norm, i * 2 - 1)
                    one(i, 1)
                    if l == 0:
                        sumsq(norm, i * 2)
                if l == 0:
                    sumsq(norm, KC - 1, stop=True)

            up(0)
            down(0)
            ple(0)

            pe.wait_ge(sem("rb_dma"), 32)
            pe.wait_ge(sem("rb_mask"), 1)
            pe.wait_ge(sem("n3_h"), KC + before("n3_h"))
            mm(MI[0:16, 0, 0:BW], RB[:], OHB[:], start=True, stop=True).then_inc(sem("rb_made"), 1)

            def head_sums(n):
                pe.wait_ge(sem("head_sq"), n + 1)
                for h in range(2):
                    last = mm(SS[:, h, 0:HT], BONES[:], SQ[:, HT * h:HT * h + HT], start=True, stop=True)
                last.then_inc(sem("head_summed"), 1)

            for s in range(4):
                pe.wait_ge(sem("split_done"), strip_of("kv", s) + 1)
                if s >= 2:
                    pe.wait_ge(sem("kvq_taken"), s - 1)
                product(s % 2, acc(s % 2), KC, 0, NH, NL, True, True,
                        ready="n3_split" if s == 0 else None).then_inc(sem("strip_done"), 1)
                if s in (1, 2):
                    head_sums(s - 1)
            for s in range(KC):
                pe.wait_ge(sem("split_done"), strip_of("q", s) + 1)
                pe.wait_ge(sem("kvq_taken"), s + 3)
                product(s % 2, acc(s % 2), KC, 0, XQH, XQL, True, True,
                        ready="xq_split" if s == 0 else None).then_inc(sem("strip_done"), 1)
                if s >= 1:
                    head_sums(s + 1)
            head_sums(KC + 1)

            pe.wait_ge(sem("rb_done"), 1)
            pe.wait_ge(sem("head_done"), 2)
            for b in range(4):
                if b >= 2:
                    pe.wait_ge(sem("tok_done"), b - 1)
                for c in range(2):
                    last = turn(MI[:, b % 2, P * c:P * c + P],
                                VT[:, c, HT * (b // 2) + P * (b % 2):HT * (b // 2) + P * (b % 2) + P], P)
                last.then_inc(sem("tok_made"), 1)
            pe.wait_ge(sem("tok_done"), 3)
            for c in range(2):
                last = turn(MI[:, 0, P * c:P * c + P], KN[:, c, SEQ - P:SEQ], P)
            last.then_inc(sem("tok_made"), 1)
            pe.wait_ge(sem("tok_done"), 4)
            for c in range(2):
                turn(MI[0:32, 1, P * c:P * c + P], KN[:, c, SEQ:NTOK], P)
                last = turn(MI[0:32, 1, 256 + P * c:256 + P * c + P], VTS[:, c, :], P)
            last.then_inc(sem("tok_made"), 1)

            groups = [(kv, n) for kv in range(KVH) for n in range(4)]
            NG = len(groups)
            S = ACC[:].rearrange("p (g a) (b n) -> p g (a b) n", g=2, b=2)

            def scores(g):
                kv, n = groups[g]
                p2, r0 = kv // 2, HD * (kv % 2)
                rows = slice(r0, r0 + HD)
                if g >= 2:
                    pe.wait_ge(sem("att_max"), 4 * (g - 1))
                tok = HT * (n // 2) + P * (n % 2)
                for r in range(RQ):
                    k0 = P if n == 0 else 0
                    last = mm(S[:, g % 2, r, k0:256], QN[rows, 4 * p2 + r, tok:tok + P],
                              KN[rows, p2, P * (n - 1) + k0:P * (n + 1)], start=True, stop=True, skip_group_check=True)
                last.then_inc(sem("att_scored"), 1)

            def turn_probs(g):
                kv, n = groups[g]
                pe.wait_ge(sem("att_probs"), g + 1)
                if g >= 1:
                    pe.wait_ge(sem("att_pt"), g)
                for kb in range(1 if n == 0 else 0, 2):
                    for r in range(RQ):
                        last = turn(MI[:, kb, P * r:P * r + P], PB[:, g % 2, r, P * kb:P * kb + P], P)
                last.then_inc(sem("att_turned"), 1)

            def values(g):
                kv, n = groups[g]
                rows = slice(HD * (kv % 2), HD * (kv % 2) + HD)
                pe.wait_ge(sem("att_pt"), g + 1)
                if g >= 2:
                    pe.wait_ge(sem("att_taken"), g - 1)
                kbs = [1] if n == 0 else [0, 1]
                for kb in kbs:
                    last = mm(SS[rows, g % 2, :], VTOK[:, n - 1 + kb, HD * kv:HD * kv + HD], PTR[:, g % 2, kb, :],
                              start=kb == kbs[0], stop=kb == 1, skip_group_check=True)
                last.then_inc(sem("att_out"), 1)

            pe.wait_ge(sem("tok_done"), 6)
            pe.wait_ge(sem("head_done"), KC + 2)
            pe.wait_ge(sem("kvq_taken"), 12)
            for g in range(NG + 2):
                if g < NG:
                    scores(g)
                if 1 <= g <= NG:
                    turn_probs(g - 1)
                if g >= 2:
                    values(g - 2)

            pe.wait_ge(sem("kc_in"), 16)
            pe.wait_ge(sem("att_pt"), NG)
            for g in range(4):
                if g >= 2:
                    pe.wait_ge(sem("kct_done"), g - 1)
                for b in range(4):
                    last = turn(MI[:, g % 2, P * b:P * b + P],
                                KCS[:, 4 * (g % 2) + b, P * (g // 2):P * (g // 2) + P], P)
                last.then_inc(sem("kct_made"), 1)
            pe.wait_ge(sem("kct_done"), 4)
            for kv in (0, 2, 1, 3):
                p2 = kv // 2
                rows = slice(HD * (kv % 2), HD * (kv % 2) + HD)
                if kv == 1:
                    last.then_inc(sem("smp_even"), 1)
                    pe.wait_ge(sem("smp_even"), 1)
                for b in range(NSEQ):
                    t0 = HT * (b // 4) + HP + STEPS * (b % 4)
                    mm(MI[:, 0, P * kv + 16 * b:P * kv + 16 * b + 16], KCT[rows, p2, b, :],
                       QN[rows, 4 * p2:4 * p2 + 4, t0:t0 + STEPS], start=True, stop=True, skip_group_check=True)
                for h in range(2):
                    for b in range(4):
                        t0 = HT * h + HP + STEPS * b
                        last = mm(MI[0:32, 1, P * kv + 64 * h + 16 * b:P * kv + 64 * h + 16 * b + 16],
                                  KN[rows, p2, SEQ:NTOK], QN[rows, 4 * p2:4 * p2 + 4, t0:t0 + STEPS],
                                  start=True, stop=True, skip_group_check=True)
            last.then_inc(sem("smp_scored"), 1)
            pe.wait_ge(sem("smp_copied"), 1)
            pe.wait_ge(sem("att_max"), 4 * (NG - 1))
            for kv in range(KVH):
                turn(S[:, 0, kv, 0:P], PTR[:, 0, 0, P * kv:P * kv + P], P)
                last = turn(S[:, 0, kv, P:160], PTR[0:32, 0, 1, P * kv:P * kv + P], 32)
            last.then_inc(sem("att_scored"), 1)
            pe.wait_ge(sem("att_probs"), NG + 1)
            for kv in range(KVH):
                turn(MI[:, 0, P * kv:P * kv + P], PB[:, 0, kv, 0:P], P)
                last = turn(MI[0:32, 1, P * kv:P * kv + P], PB[:, 0, kv, P:160], P)
            last.then_inc(sem("att_turned"), 1)
            pe.wait_ge(sem("att_pt"), NG + 1)
            pe.wait_ge(sem("att_taken"), NG - 1)
            pe.wait_ge(sem("vc_in"), 16)
            for kv in range(KVH):
                rows = slice(HD * (kv % 2), HD * (kv % 2) + HD)
                mm(SS[rows, 0, P * kv:P * kv + P], KVS[0:32, 1, HD * kv:HD * kv + HD], PTR[0:32, 0, 1, P * kv:P * kv + P],
                   start=True, stop=False, skip_group_check=True)
                for b in range(NSEQ):
                    c0 = P * kv + 16 * b
                    last = mm(SS[rows, 0, c0:c0 + 16], VCS[:, b, HD * kv:HD * kv + HD], PTR[:, 0, 0, c0:c0 + 16],
                              start=False, stop=True, skip_group_check=True)
            last.then_inc(sem("att_out"), 1)

            def wo(i, u, start=False):
                strip("wo", i, u)
                if not start:
                    pe.wait_ge(sem("n4_h"), i * 2 + (u - 1) + before("n4_h"))
                product(u, acc(u), KC, 0, NH, NL, True, True).then_inc(sem("strip_done"), 1)

            pe.wait_ge(sem("att_taken"), NG + 1)
            pe.wait_ge(sem("att_max"), 4 * (NG + 1))
            wo(0, 0, True)
            wo(0, 1, True)
            sumsq("n4", 0, start=True)
            with pe.Fori(1, KC // 2) as i:
                wo(i, 0)
                sumsq("n4", i * 2 - 1)
                wo(i, 1)
                sumsq("n4", i * 2)
            sumsq("n4", KC - 1, stop=True)

            up(1)
            down(1)
            ple(1)

            pe.wait_ge(sem("n6_h"), KC + before("n6_h"))
            pe.wait_ge(sem("hsmp"), 1)
            for b in range(5):
                if b >= 2:
                    pe.wait_ge(sem("y_done"), b - 1)
                for m in range(KC):
                    if b < 4:
                        src = H[:, m, HT * (b // 2) + P * (b % 2):HT * (b // 2) + P * (b % 2) + P]
                        last = turn(ACC[:, 2 * (b % 2) + m // 4, P * (m % 4):P * (m % 4) + P], src, P)
                    else:
                        last = turn(ACC[0:32, m // 4, P * (m % 4):P * (m % 4) + P], HSMP[:, m, :], P)
                last.then_inc(sem("y_turned"), 1)

        @block.scalar
        def _(act):
            chain = Chain(act, sem("act_chain"))
            A = nc.scalar.activation
            def copy(out, in_, **kw):
                return A(out, in_, ACT.Copy, **kw)

            def store(dst, src):
                act.dma_start(dst, src).then_inc(sem("out"), 16)
                outs[0] += 16

            def square(name, m, src, first=False, count=None):
                act.wait_ge(sem(name + "_h"), m + 1 + before(name + "_h"))
                if not first:
                    act.wait_ge(sem(name + "_summed"), m + before(name + "_summed"))
                A(SQ, src, ACT.Square).then_inc(sem(name + "_sq"), 1)

            def root(name):
                act.wait_ge(sem(name + "_summed"), KC + before(name + "_summed"))
                A(halves(RSTD[:]), SS[:, :, 0:HT], ACT.Sqrt, bias=EPSB[:], scale=1.0 / D).then_inc(sem(name + "_root"), 1)

            def high(name, dst):
                with act.Fori(0, KC // 2) as i:
                    for u in range(2):
                        act.wait_ge(sem(name + "_nt"), i * 2 + (u + 1) + before(name + "_nt"))
                        copy(dst[:, i * 2 + u, :], NT[u]).then_inc(sem(name + "_high"), 1)

            for r in range(2):
                act.wait_ge(sem("c_made"), r + 1)
                copy(CAC[:, 0, r].rearrange("p q c -> p (q c)"), ACC[:, 2 + r, :]).then_inc(sem("c_turned"), 1)
            for m in range(KC):
                act.wait_ge(sem("x_made"), m + 1)
                copy(halves(H[:, m, :])[:, :, 0:HP], MI[:, m % 2, :].rearrange("p (h t) -> p h t", h=2)).then_inc(sem("x_turned"), 1)
            act.wait_ge(sem("x_made"), KC + 1)
            copy(H[:].rearrange("p m (h t) -> p m h t", h=2)[:, :, :, HP:HT],
                 ACC[:, 0, 0:256].rearrange("p (m h t) -> p m h t", m=KC, h=2)).then_inc(sem("x_turned"), 1)
            act.wait_ge(sem("x_turned"), KC + 1)
            act.wait_ge(sem("vec_made"), 1)
            copy(VEC[:], SS[:, 1, 0:V_N]).then_inc(sem("vec_done"), 1)
            act.wait_ge(sem("cp_made"), 1)
            copy(CP[:].rearrange("p l v c -> p (l v c)"), ACC[:, 1, 0:352]).then_inc(sem("vec_done"), 1)
            act.wait_ge(sem("st_made"), 1)
            for r in range(2):
                copy(H0[:, r].rearrange("p b (h q) -> p h b q", h=2),
                     MI[:, r, 0:256].rearrange("p (h b q) -> p h b q", h=2, b=NSEQ)).then_inc(sem("h0_done"), 1)
            for m in range(KC):
                if m:
                    act.wait_ge(sem("n0_summed"), m + before("n0_summed"))
                A(SQ, H[:, m, :], ACT.Square).then_inc(sem("n0_sq"), 1)
            act.wait_ge(sem("ones_set"), 1)
            root("n0")

            def expand_b(f):
                src = PC[:, f, 0:512].rearrange("p (j q c) -> p j q c", j=8, q=FQ)
                dst = PBD[:].rearrange("p j (q a c) -> p j a q c", q=FQ, a=2)
                copy(dst[0:64, :, 0], src[0:64])
                copy(dst[64:128, :, 1], src[64:128]).then_inc(sem("pbd_ready"), 1)

            def expand_c(f, i0, n, dst, name):
                for r in range(2):
                    d = dst[:, :, r, :].rearrange("p i (q a c) -> p i a q c", q=FQ, a=2)
                    s_ = CAC[:, i0:i0 + n, r, FQ * f:FQ * f + FQ, :]
                    copy(d[0:64, :, 0], s_[0:64], scale=1.0 - 2.0 * r)
                    last = copy(d[64:128, :, 1], s_[64:128], scale=1.0 - 2.0 * r)
                last.then_inc(sem(name), 1)

            def place_u(f):
                copy(UF[:, f % 2, :], U[:, f, :]).then_inc(sem("uf_ready"), 1)

            C0V = C0BD[:].rearrange("p (i r) c -> p i r c", i=1)
            act.wait_ge(sem("zeros_set"), 1)
            act.wait_ge(sem("pc_ready"), 1)
            expand_b(0)
            act.wait_ge(sem("ca_ready"), 1)
            expand_c(0, 0, 1, C0V, "c0_ready")
            expand_c(0, 1, 4, CBD[:], "cbd_ready")
            act.wait_ge(sem("u_ready"), KC)
            act.wait_ge(sem("e_ready"), 1)
            place_u(0)

            def gelu(f):
                act.wait_ge(sem("y_taken"), f + 1)
                if f:
                    act.wait_ge(sem("z_split"), f)
                A(ZT, YT, ACT.Gelu_apprx_tanh).then_inc(sem("gelu_done"), 1)
                act.wait_ge(sem("gelu_done"), f + 1)
                copy(NH[:, f, :], ZT).then_inc(sem("z_high"), 1)

            for f in range(KC):
                act.wait_ge(sem("p_turned"), f + 1)
                if f:
                    act.wait_ge(sem("v_made"), f)
                for q in range(2):
                    rows = slice(32 * q, 32 * q + 32)
                    last = copy(BT[rows, :, q % 2, :], MI[rows].rearrange("p a (j s) -> p (a j) s", j=4))
                last.then_inc(sem("bt_a"), 1)
                act.wait_ge(sem("v_made"), f + 1)
                if f:
                    act.wait_ge(sem("h_ready"), f)
                for r in range(2):
                    src = ACC[:, :, NCOL * r:NCOL * r + NCOL].rearrange("p q (h c) -> p q h c", h=2)
                    copy(V[:, r].rearrange("p q (h c) -> p q h c", h=2), src[:, :, :, 0:HPB])
                    for h in range(2):
                        last = copy(VSM[:, r, 4 * h:4 * h + 4, FQ * f:FQ * f + FQ].rearrange("p b q -> p q b"),
                                    src[:, :, h, HPB:HB])
                last.then_inc(sem("v_taken"), 1)
                if f >= 2:
                    act.wait_ge(sem("y_made"), f - 1)
                for r in range(2):
                    for h in range(2):
                        last = copy(HSV[:, f % 2, r].rearrange("p q (h c) -> p q h c", h=2)[:, :, h, HPB:HB],
                                    H0[:, r, 4 * h:4 * h + 4, FQ * f:FQ * f + FQ].rearrange("p b q -> p q b"))
                last.then_inc(sem("h0_placed"), 1)
                if f + 1 < KC:
                    act.wait_ge(sem("k_made"), f + 1)
                    expand_b(f + 1)
                    expand_c(f + 1, 0, 1, C0V, "c0_ready")
                    if f:
                        act.wait_ge(sem("y_made"), f)
                    place_u(f + 1)
                if f:
                    act.wait_ge(sem("y_made"), f)
                    expand_c(f, 1, 4, CBD[:], "cbd_ready")
                    gelu(f - 1)
            gelu(KC - 1)
            act.wait_ge(sem("fs_turned"), 1)
            copy(FSO[:].rearrange("q r n -> q (r n)"), MI[0:PAIRS, 1, 0:256])
            copy(VSO[:].rearrange("p r h n -> p (r h n)"), MI[:, 0, :]).then_inc(sem("fs_out"), 1)
            act.wait_ge(sem("fs_out"), 1)
            for r, (dp, ds_) in enumerate(((ssm_re_p, ssm_re_s), (ssm_im_p, ssm_im_s))):
                store(dp[0, 0].rearrange("(q a) s -> q (a s)", a=2), FSO[:, r, :])
                for h in range(2):
                    store(ds_[0, 4 * h:4 * h + 4].rearrange("b (q a) s -> (b q) (a s)", a=2), VSO[:, r, h, :])

            def load_ffn(l):
                c = sem("cst_in%d" % l)
                act.dma_start(CST[:], state_ffn_conv[l].rearrange("b k n -> (b k) n")).then_inc(c, 16)
                act.dma_start(PST[:, 0:4, :], p_prompt[l, 0].rearrange("(b p) d -> p b d", p=P)).then_inc(c, 16)
                act.dma_start(PST[0:32, 4, :], p_sample[l].rearrange("b t d -> (b t) d")).then_inc(c, 16)

            act.wait_ge(sem("fs_ready"), 1)
            load_ffn(0)

            def gate(i):
                act.wait_ge(sem("strip_done"), i * 2 + 2)
                act.wait_ge(sem("glu_taken0"), i)
                A(halves(SG), acc(1), ACT.Sigmoid, bias=VEC[:, bass.ds(i + (V_BGLU + KC), 1)]).then_inc(sem("glu_taken1"), 1)

            act.wait_ge(sem("strip_done"), 2)
            act.wait_ge(sem("z_split"), KC)
            A(halves(SG), acc(1), ACT.Sigmoid, bias=VEC[:, V_BGLU + KC:V_BGLU + KC + 1]).then_inc(sem("glu_taken1"), 1)
            gate(1)
            square("n1", 0, H[:, 0, :], True)
            with act.Fori(2, KC) as i:
                gate(i)
                square("n1", i - 1, H[:, i - 1, :])
            square("n1", KC - 1, H[:, KC - 1, :])

            def up(l):
                name, n0, norm = "up%d" % l, first["up%d" % l], "n%d" % (1 + 3 * l)
                act.wait_ge(sem("cs_turned%d" % l), 1 + before("cs_turned%d" % l))
                for a in range(2):
                    last = copy(CSP[:, FC * a:FC * a + FC, :].rearrange("p c n -> p (c n)"), MI[:, a, 0:16 * FC])
                last.then_inc(sem("cs_done%d" % l), 1)
                act.wait_ge(sem("p_made%d" % l), 1 + before("p_made%d" % l))
                for c in range(2):
                    copy(halves(PTH[:, c, :])[:, :, 0:HP], MI[:, c, :].rearrange("p (h t) -> p h t", h=2))
                copy(PTH[:].rearrange("p c (h t) -> p c h t", h=2)[:, :, :, HP:HT],
                     ACC[:, 3, 0:64].rearrange("p (c h t) -> p c h t", c=2, h=2)).then_inc(sem("p_high%d" % l), 1)
                root(norm)
                high(norm, NH)

                def body(i, start=False):
                    for u, what in enumerate(("_gate", "_val")):
                        act.wait_ge(sem("strip_done"), i * 2 + (n0 + u + 1))
                        if not start:
                            act.wait_ge(sem(name + ("_cg", "_cv")[u]), i + before(name + ("_cg", "_cv")[u]))
                        E = WK[:, u, :]
                        copy(E[:, 2:2 + SEQ].rearrange("p (h t) -> p h t", h=2), acc(u)[:, :, 0:HP])
                        copy(E[:, 2 + SEQ:EXT].rearrange("p (h b s) -> p h b s", h=2, s=6)[:, :, :, 2:6],
                             acc(u)[:, :, HP:HT].rearrange("p h (b t) -> p h b t", t=STEPS)).then_inc(sem(name + what), 1)
                    act.wait_ge(sem(name + "_cg"), i + 1 + before(name + "_cg"))
                    A(WK[:, 2, 0:CONV], WK[:, 2, 0:CONV], ACT.Silu).then_inc(sem(name + "_silu"), 1)
                    act.wait_ge(sem(name + "_prod"), i + 1 + before(name + "_prod"))
                    copy(AH[:, i, :], TT[:]).then_inc(sem(name + "_high"), 1)

                body(0, True)
                with act.Fori(1, FC) as i:
                    body(i)

            def chunk_squares(name):
                square(name, 0, H[:, 0, :], True)
                with act.Fori(1, KC) as i:
                    square(name, i, H[:, i, :])

            def down(l):
                norm = "n%d" % (2 + 3 * l)
                chunk_squares(norm)
                for g in range(FC // 2):
                    act.wait_ge(sem("ct_made%d" % l), g + 1 + before("ct_made%d" % l))
                    copy(CTO[:, 512 * g:512 * g + 512], MI[0:18, g % 2, :]).then_inc(sem("ct_done%d" % l), 1)
                act.wait_ge(sem("ct_done%d" % l), FC // 2 + before("ct_done%d" % l))
                store(conv_p[l, 0], CTO[0:2, :])
                store(conv_s[l].rearrange("b k n -> (b k) n"), CTO[2:18, :])

            def ple(l):
                name, norm, nxt, n0 = "ple%d" % l, "n%d" % (2 + 3 * l), "n%d" % (3 + 3 * l), first["ple%d" % l]
                root(norm)
                high(norm, NH)

                def one(m, start=False):
                    act.wait_ge(sem("strip_done"), m + (n0 + 1))
                    if not start:
                        act.wait_ge(sem(name + "_in"), m + before(name + "_in"))

                def sig(m, u):
                    A(halves(SG), acc(u), ACT.Sigmoid).then_inc(sem(name + "_sig"), 1)

                one(0, True)
                sig(0, 0)
                one(1)
                sig(1, 1)
                if l == 0:
                    square(nxt, 0, H[:, 0, :], True)
                with act.Fori(1, KC // 2) as i:
                    for u in range(2):
                        one(i * 2 + u)
                        sig(i * 2 + u, u)
                        if l == 0:
                            square(nxt, i * 2 + (u - 1), H[:, i * 2 + (u - 1), :])
                if l == 0:
                    square(nxt, KC - 1, H[:, KC - 1, :])

            up(0)
            down(0)
            act.dma_start(RB[0:NBUCK, :], rel_bias).then_inc(sem("rb_dma"), 16)
            act.dma_start(OHB[:], consts[0:NBUCK + 1, C_OH:C_OH + BW]).then_inc(sem("rb_dma"), 16)
            act.dma_start(BM[:], consts[:, C_BM:C_BM + 32 + RQ]).then_inc(sem("snk_in"), 16)
            with nc.allow_non_contiguous_dma(reason="a few small vectors"):
                act.dma_start(SNK[:], sinks.to_broadcast([P, 16])).then_inc(sem("snk_in"), 16)
            act.dma_start(VCS[:], cache_v_win.rearrange("b s k d -> s b (k d)")).then_inc(sem("vc_in"), 16)
            ple(0)
            act.wait_ge(sem("rb_made"), 1)
            copy(RBR[:], MI[0:16, 0, 0:BW]).then_inc(sem("rb_done"), 1)
            act.wait_ge(sem("rb_done"), 1)
            act.dma_start(bias_rows, RBR[:].unsqueeze(1).to_broadcast([16, P, BW])).then_inc(sem("rows_out"), 16)

            root("n3")
            high("n3", NH)
            act.wait_ge(sem("rows_out"), 16)
            flat = bias_rows.rearrange("h a n -> h (a n)")

            def window(h0, h1, rows, cols):
                v = flat[h0:h1, 127:127 + rows * (BW - 1)].rearrange("h (t s) -> h t s", s=BW - 1)
                return v[:, :, 0:cols]

            act.dma_start(BIAS[:], window(0, 16, P, 256).rearrange("h t s -> t h s")).then_inc(sem("bias_in"), 16)
            for b in range(NSEQ):
                for k in range(KVH):
                    act.dma_start(SBT[16 * b:16 * b + 16, k, :], window(RQ * k, RQ * k + RQ, STEPS, WIN + STEPS)).then_inc(sem("sbt_in"), 16)
            high("xq", XQH)

            def head_square(n):
                src = KN[:, n, :] if n < 2 else QN[:, n - 2, :]
                if n:
                    act.wait_ge(sem("head_summed"), n)
                A(SQ, src, ACT.Square).then_inc(sem("head_sq"), 1)

            def head_root(n):
                act.wait_ge(sem("head_summed"), n + 1)
                if n:
                    act.wait_ge(sem("head_done"), n)
                A(halves(SG), SS[:, :, 0:HT], ACT.Sqrt, bias=EPSB[:], scale=1.0 / HD).then_inc(sem("head_root"), 1)

            for s in range(12):
                act.wait_ge(sem("strip_done"), first["kv"] + s + 1)
                if s == 0:
                    act.wait_ge(sem("xq_split"), KC + before("xq_split"))
                    act.wait_ge(sem("out"), outs[0])
                a = acc(s % 2)
                if s < 2:
                    copy(KN[:, s, 0:SEQ].rearrange("p (h t) -> p h t", h=2), a[:, :, 0:HP])
                    last = copy(KN[:, s, SEQ:NTOK].rearrange("p (h t) -> p h t", h=2), a[:, :, HP:HT])
                elif s < 4:
                    copy(halves(VT[:, s - 2, :]), a)
                    last = copy(VTS[:, s - 2, :].rearrange("p (h t) -> p h t", h=2), a[:, :, HP:HT])
                else:
                    last = copy(halves(QN[:, s - 4, :]), a)
                last.then_inc(sem("kvq_taken"), 1)
                act.wait_ge(sem("kvq_taken"), s + 1)
                n = s if s < 2 else s - 2
                if s < 2 or s >= 4:
                    if n >= 1:
                        head_root(n - 1)
                    head_square(n)
            head_root(9)

            for b in range(4):
                act.wait_ge(sem("tok_made"), b + 1)
                copy(VTOK[:, b, :], MI[:, b % 2, 0:256]).then_inc(sem("tok_done"), 1)
            act.wait_ge(sem("tok_made"), 5)
            copy(KTP[:], MI[:, 0, 0:256]).then_inc(sem("tok_done"), 1)
            act.wait_ge(sem("tok_made"), 6)
            copy(KVS[:].rearrange("p a n -> p (a n)"), MI[0:32, 1, :]).then_inc(sem("tok_done"), 1)
            act.wait_ge(sem("tok_done"), 6)
            store(k_win_p[0].rearrange("s k d -> s (k d)"), KTP[:])
            store(v_win_p[0].rearrange("s k d -> s (k d)"), VTOK[:, 3, :])
            act.dma_start(KCS[:], cache_k_win.rearrange("b s k d -> s b (k d)")).then_inc(sem("kc_in"), 16)
            for src, cache, out in ((0, cache_k_win, k_win_s), (1, cache_v_win, v_win_s)):
                store(out[:, 0:WIN - STEPS].rearrange("b s k d -> b s (k d)"), cache[:, STEPS:WIN].rearrange("b s k d -> b s (k d)"))
                for b in range(NSEQ):
                    store(out[b, WIN - STEPS:WIN].rearrange("s k d -> s (k d)"), KVS[STEPS * b:STEPS * b + STEPS, src, :])

            NG = 16

            def exps(g, w0, w):
                act.wait_ge(sem("att_neg"), g + 1)
                for r in range(4):
                    A(PB[:, g % 2, r, w0:w], PB[:, g % 2, r, w0:w], ACT.Exp, bias=SM[:, g % 2, 1, r:r + 1],
                      accum_out=SM[:, g % 2, 2, r:r + 1])
                A(SM[:, g % 2, 3, :], SM[:, g % 2, 3, :], ACT.Exp).then_inc(sem("att_exp"), 1)

            def take_turned(g):
                act.wait_ge(sem("att_turned"), g + 1)
                if g >= 2:
                    act.wait_ge(sem("att_out"), g - 1)
                kb = 1 if g % 4 == 0 else 0
                copy(PTR[:, g % 2, kb:2, :], MI[:, kb:2, :]).then_inc(sem("att_pt"), 1)

            def take_out(g):
                kv, n = g // 4, g % 4
                rows = slice(HD * (kv % 2), HD * (kv % 2) + HD)
                tok = HT * (n // 2) + P * (n % 2)
                act.wait_ge(sem("att_out"), g + 1)
                copy(NH[rows, 4 * (kv // 2):4 * (kv // 2) + 4, tok:tok + P],
                     SS[rows, g % 2, :].rearrange("p (r t) -> p r t", r=4)).then_inc(sem("att_high"), 1)

            for g in range(NG + 2):
                if g < NG:
                    exps(g, P if g % 4 == 0 else 0, 256)
                if 1 <= g <= NG:
                    take_turned(g - 1)
                if g >= 2:
                    take_out(g - 2)
            for g in range(4):
                act.wait_ge(sem("kct_made"), g + 1)
                copy(KCT[:, g // 2, 4 * (g % 2):4 * (g % 2) + 4, :].rearrange("p b n -> p (b n)"), MI[:, g % 2, :]).then_inc(sem("kct_done"), 1)
            act.wait_ge(sem("smp_scored"), 1)
            act.wait_ge(sem("att_out"), NG)
            copy(PTR[:, 0, 0, :], MI[:, 0, :])
            copy(PTR[0:32, 0, 1, :], MI[0:32, 1, :]).then_inc(sem("smp_copied"), 1)
            exps(NG, 0, 160)
            act.wait_ge(sem("att_turned"), NG + 1)
            copy(PTR[:, 0, 0, :], MI[:, 0, :])
            copy(PTR[0:32, 0, 1, :], MI[0:32, 1, :]).then_inc(sem("att_pt"), 1)
            act.wait_ge(sem("att_out"), NG + 1)
            for kv in range(KVH):
                rows = slice(HD * (kv % 2), HD * (kv % 2) + HD)
                for h in range(2):
                    last = copy(NH[rows, 4 * (kv // 2):4 * (kv // 2) + 4, HT * h + HP:HT * h + HT].rearrange("p r (b t) -> p r b t", t=STEPS),
                                SS[rows, 0, P * kv + 64 * h:P * kv + 64 * h + 64].rearrange("p (b r t) -> p r b t", b=4, r=4))
            last.then_inc(sem("att_high"), 1)
            act.wait_ge(sem("att_out"), NG + 1)
            act.wait_ge(sem("out"), outs[0])
            load_ffn(1)
            chunk_squares("n4")
            up(1)
            down(1)
            ple(1)

            act.wait_ge(sem("out"), outs[0])
            for b in range(5):
                rows = P if b < 4 else 32
                act.wait_ge(sem("y_turned"), b + 1)
                if b >= 2:
                    act.wait_ge(sem("y_out%d" % (b % 2)), 16 * (b // 2) + before("y_out%d" % (b % 2)))
                copy(YS[0:rows, b % 2, :].rearrange("p (a n) -> p a n", a=2),
                     ACC[0:rows, 2 * (b % 2):2 * (b % 2) + 2, :]).then_inc(sem("y_done"), 1)
                act.wait_ge(sem("y_done"), b + 1)
                dst = y_prompt[0, P * b:P * b + P, :] if b < 4 else y_sample.rearrange("b t d -> (b t) d")
                act.dma_start(dst, YS[0:rows, b % 2, :]).then_inc(sem("y_out%d" % (b % 2)), 16)
            act.wait_ge(sem("y_out0"), 48)
            act.wait_ge(sem("y_out1"), 32)

        @block.vector
        def _(dve):
            chain = Chain(dve, sem("dve_chain"))
            link = chain.link
            T = nc.vector.tensor_tensor
            TS = nc.vector.tensor_scalar
            cp = nc.vector.tensor_copy

            def STT(out, in0, scalar, in1, op0, op1):
                return nc.vector.scalar_tensor_tensor(out=out, in0=in0, scalar=scalar, in1=in1, op0=op0, op1=op1)

            M_, A_, S_ = ALU.mult, ALU.add, ALU.subtract

            def pr(j):
                return PR[:, j, :]

            ROUND = 1.5 * 2.0 ** 23

            dve.wait_ge(sem("lam_turned"), 1)
            link(cp(PR[:, LR:LR + 2, :].rearrange("p a q -> p (a q)"), SS[:, 0, 0:64]))
            cp(pr(X0), SS[:, 0, 64:96]).then_inc(sem("lam_taken"), 1)
            dve.wait_ge(sem("lam_taken"), 1)

            def exponential(out, x):
                link(TS(pr(X1), x, 1.0 / math.log(2.0), ROUND, M_, A_))
                link(TS(pr(X1), pr(X1), ROUND, -126.0, S_, ALU.max))
                link(TS(pr(X1), pr(X1), 127.0, None, ALU.min))
                link(STT(pr(X2), pr(X1), -0.693359375, x, M_, A_))
                link(STT(pr(X2), pr(X1), 2.12194440e-4, pr(X2), M_, A_))
                link(TS(pr(X3), pr(X2), 1.0 / 5040.0, None, M_))
                for n in (720.0, 120.0, 24.0, 6.0, 2.0, 1.0):
                    link(STT(pr(X3), pr(X3), 1.0 / n, pr(X2), A_, M_))
                link(TS(pr(X1), pr(X1), 127.0, None, A_))
                link(cp(pr(KI).bitcast(I32), pr(X1)))
                link(TS(pr(KI).bitcast(I32), pr(KI).bitcast(I32), 23, None, ALU.logical_shift_left))
                link(STT(out, pr(X3), 1.0, pr(KI), A_, M_))

            def times(o_re, o_im, a_re, a_im, b_re, b_im):
                link(T(pr(X4), a_re, b_re, M_))
                link(T(pr(X5), a_im, b_im, M_))
                link(T(pr(X6), a_re, b_im, M_))
                link(T(pr(X7), a_im, b_re, M_))
                link(T(o_re, pr(X4), pr(X5), S_))
                link(T(o_im, pr(X6), pr(X7), A_))

            exponential(pr(DT), pr(X0))
            link(T(pr(X0), pr(LR), pr(DT), M_))
            exponential(pr(MAG), pr(X0))
            link(T(pr(X0), pr(LI), pr(DT), M_))
            link(TS(pr(X1), pr(X0), 2.0 / math.pi, ROUND, M_, A_))
            link(TS(pr(X1), pr(X1), ROUND, None, S_))
            for part in (1.5703125, 4.837512969970703125e-4, 7.549789954891882e-8):
                link(STT(pr(X0), pr(X1), -part, pr(X0), M_, A_))
            link(T(pr(X2), pr(X0), pr(X0), M_))
            link(TS(pr(X3), pr(X2), -1.0 / 39916800.0, None, M_))
            for n in (362880.0, -5040.0, 120.0, -6.0):
                link(STT(pr(X3), pr(X3), 1.0 / n, pr(X2), A_, M_))
            link(STT(pr(X3), pr(X3), 1.0, pr(X0), A_, M_))
            link(TS(pr(X4), pr(X2), -1.0 / 3628800.0, None, M_))
            for n in (40320.0, -720.0, 24.0, -2.0):
                link(STT(pr(X4), pr(X4), 1.0 / n, pr(X2), A_, M_))
            link(TS(pr(X4), pr(X4), 1.0, None, A_))
            link(TS(pr(X5), pr(X1), 0.25, ROUND, M_, A_))
            link(TS(pr(X5), pr(X5), ROUND, -4.0, S_, M_))
            link(T(pr(X5), pr(X5), pr(X1), A_))
            link(STT(pr(X6), pr(X5), -1.0, pr(X5), M_, ALU.max))
            link(TS(pr(X7), pr(X6), -1.0, 1.0, M_, A_))
            link(TS(pr(X6), pr(X6), -1.0, 2.0, M_, A_))
            link(T(pr(X6), pr(X6), pr(X5), M_))
            link(T(pr(X5), pr(X4), pr(X7), M_))
            link(T(pr(X8), pr(X3), pr(X6), M_))
            link(T(pr(C1), pr(X5), pr(X8), S_))
            link(T(pr(X5), pr(X3), pr(X7), M_))
            link(T(pr(X8), pr(X4), pr(X6), M_))
            link(T(pr(S1), pr(X5), pr(X8), A_))
            link(T(pr(A_RE), pr(MAG), pr(C1), M_))
            T(pr(A_IM), pr(MAG), pr(S1), M_).then_inc(sem("a_ready"), 1)
            dve.wait_ge(sem("a_ready"), 1)
            link(T(pr(X0), pr(LR), pr(LR), M_))
            link(T(pr(X1), pr(LI), pr(LI), M_))
            link(T(pr(X0), pr(X0), pr(X1), A_))
            link(nc.vector.reciprocal(pr(X0), pr(X0)))
            link(TS(pr(X1), pr(A_RE), 1.0, None, S_))
            link(T(pr(X2), pr(X1), pr(LR), M_))
            link(T(pr(X3), pr(A_IM), pr(LI), M_))
            link(T(pr(X2), pr(X2), pr(X3), A_))
            link(T(pr(F_RE), pr(X2), pr(X0), M_))
            link(T(pr(X2), pr(A_IM), pr(LR), M_))
            link(T(pr(X3), pr(X1), pr(LI), M_))
            link(T(pr(X2), pr(X2), pr(X3), S_))
            link(T(pr(F_IM), pr(X2), pr(X0), M_))
            times(pr(A2_RE), pr(A2_IM), pr(A_RE), pr(A_IM), pr(A_RE), pr(A_IM))
            times(pr(A4_RE), pr(A4_IM), pr(A2_RE), pr(A2_IM), pr(A2_RE), pr(A2_IM))
            link(T(pr(R4), pr(MAG), pr(MAG), M_))
            link(T(pr(R4), pr(R4), pr(R4), M_))
            times(pr(E_RE), pr(E_IM), pr(C1), pr(S1), pr(C1), pr(S1))
            times(pr(E_RE), pr(E_IM), pr(E_RE), pr(E_IM), pr(E_RE), pr(E_IM))

            dve.wait_ge(sem("b_in"), 32)

            def pc(k, r):
                o = (2 * k + r) * FQ * CG
                return PC[:, :, o:o + FQ * CG].rearrange("p f (q c) -> p f q c", c=CG)

            def wide(j):
                return pr(j).rearrange("p (f q) -> p f q", q=FQ).unsqueeze(3).to_broadcast([P, KC, FQ, CG])

            def four(x):
                return x.rearrange("p (f q c) -> p f q c", f=KC, q=FQ)

            bc = [BC[:, r].rearrange("p (f q) c -> p f q c", q=FQ) for r in range(2)]
            te = [four(TE[:, j, 0:512]) for j in range(2)]
            for k in range(4):
                src = bc if k == 0 else [pc(k - 1, 0), pc(k - 1, 1)]
                re, im = (F_RE, F_IM) if k == 0 else (A_RE, A_IM)
                for o in range(2):
                    link(T(te[0], src[0], wide((re, im)[o]), M_))
                    link(T(te[1], src[1], wide((im, re)[o]), M_))
                    last = T(pc(k, o), te[0], te[1], (S_, A_)[o])
                    if k == 3 and o == 1:
                        last.then_inc(sem("pc_ready"), 1)
                    else:
                        link(last)

            def reciprocal_root(name):
                dve.wait_ge(sem(name + "_root"), 1 + before(name + "_root"))
                link(nc.vector.reciprocal(RSTD[:], RSTD[:]))

            dve.wait_ge(sem("vec_done"), 2)
            reciprocal_root("n0")
            for m in range(KC):
                STT(U[:, m, :], H[:, m, :], VEC[:, V_GMIX + m:V_GMIX + m + 1], RSTD[:], M_, M_).then_inc(sem("u_ready"), 1)

            link(nc.vector.memset(EROT[:, 0, :, 0:1], 1.0))
            link(nc.vector.memset(EROT[:, 1, :, 0:1], 0.0))
            m = 1
            while m < NBLK:
                npair = min(PAIRS, 1024 // m)
                for q0 in range(0, PAIRS, npair):
                    def sl(r, a):
                        return EROT[:, r, q0:q0 + npair, a:a + m]

                    def tw(j):
                        return PR[:, j, q0:q0 + npair].unsqueeze(2).to_broadcast([P, npair, m])

                    t = [TE[:, j, 0:npair * m].rearrange("p (q c) -> p q c", c=m) for j in range(2)]
                    for o in range(2):
                        link(T(t[0], sl(0, 0), tw((E_RE, E_IM)[o]), M_))
                        link(T(t[1], sl(1, 0), tw((E_IM, E_RE)[o]), M_))
                        link(T(sl(o, m), t[0], t[1], (S_, A_)[o]))
                times(pr(E_RE), pr(E_IM), pr(E_RE), pr(E_IM), pr(E_RE), pr(E_IM))
                m *= 2
            dve.wait_ge(sem("h0_done"), 2)
            dve.wait_ge(sem("ca_ready"), 1)
            for par in range(2):
                last = nc.vector.memset(HSV[:, par, :, :, 0:1], 0.0)
                link(last)
            nc.vector.memset(TIC2[:], 0.0).then_inc(sem("e_ready"), 1)
            dve.wait_ge(sem("e_ready"), 1)

            def scan(f):
                par = f % 2
                dve.wait_ge(sem("p_turned"), f + 1)
                if f:
                    dve.wait_ge(sem("v_made"), f)
                for q in range(2, 4):
                    rows = slice(32 * q, 32 * q + 32)
                    last = cp(BT[rows, :, q % 2, :], MI[rows].rearrange("p a (j s) -> p (a j) s", j=4))
                last.then_inc(sem("bt_d"), 1)
                dve.wait_ge(sem("k_made"), f + 1)
                if f >= 2:
                    dve.wait_ge(sem("y_made"), f - 1)
                for q in range(FQ):
                    rows = slice(32 * q, 32 * q + 32)
                    last = cp(KM[rows, par, :, rows], SS[rows, 0, 0:P].rearrange("p (t c) -> p t c", t=4))
                last.then_inc(sem("k_done"), 1)
                dve.wait_ge(sem("v_taken"), f + 1)
                t1 = T1.rearrange("p (r q c) -> p r (q c)", r=2, q=FQ)
                t2 = T2[:].rearrange("p r q c -> p r (q c)")
                v = V[:].rearrange("p r q c -> p r (q c)")
                e = [EROT[:, r, FQ * f:FQ * f + FQ, :].rearrange("p q c -> p (q c)").unsqueeze(1).to_broadcast([P, 2, FQ * NBLK])
                     for r in range(2)]
                link(T(t1, v, e[0], M_))
                link(T(t2, v, e[1], M_))
                link(T(v[:, 0], t1[:, 0], t2[:, 1], A_))
                link(T(v[:, 1], t1[:, 1], t2[:, 0], S_))
                for r in range(2):
                    for q in range(FQ):
                        last = nc.vector.tensor_tensor_scan(
                            t1[:, r, NBLK * q:NBLK * q + NBLK], PR[:, R4, FQ * f + q:FQ * f + q + 1].to_broadcast([P, NBLK]),
                            v[:, r, NBLK * q:NBLK * q + NBLK], 0.0, M_, A_)
                link(last)
                link(T(v, t1, e[0], M_))
                link(T(t2, t1, e[1], M_))
                if f >= 2:
                    dve.wait_ge(sem("y_made"), f - 1)
                for r in range(2):
                    a = V[:, r]
                    b = T2[:, 1 - r]
                    op = (S_, A_)[r]
                    T(HSV[:, par, r, :, 1:HPB], a[:, :, 0:HPB - 1], b[:, :, 0:HPB - 1], op)
                    T(HSV[:, par, r, :, HB:HB + HPB], a[:, :, HPB - 1:NBLK - 1], b[:, :, HPB - 1:NBLK - 1], op)
                    last = T(FS[:, r, FQ * f:FQ * f + FQ], a[:, :, NBLK - 1], b[:, :, NBLK - 1], op)
                last.then_inc(sem("h_ready"), 1)
                dve.wait_ge(sem("h_ready"), f + 1)

            YV = SS[:].rearrange("p a (i n) -> p (a i) n", i=2)[:, :, 0:NCOL].rearrange("p i c -> p c i")

            def skip(f):
                dve.wait_ge(sem("y_made"), f + 1)
                if f:
                    dve.wait_ge(sem("gelu_done"), f)
                STT(YT.rearrange("p (c i) -> p c i", i=STEPS), U[:, f, :].rearrange("p (c i) -> p c i", i=STEPS),
                    VEC[:, V_D + f:V_D + f + 1], YV, M_, A_).then_inc(sem("y_taken"), 1)
                dve.wait_ge(sem("z_high"), f + 1)
                T(NL[:, f, :], ZT, NH[:, f, :].bitcast(F32), S_).then_inc(sem("z_split"), 1)

            for f in range(KC):
                scan(f)
                if f:
                    skip(f - 1)
            a4 = [pr(j).unsqueeze(1).to_broadcast([P, NSEQ, PAIRS]) for j in (A4_RE, A4_IM)]
            tv = [V[:, j].rearrange("p q c -> p (q c)")[:, 0:NSEQ * PAIRS].rearrange("p (b q) -> p b q", b=NSEQ) for j in range(2)]
            for r in range(2):
                link(T(tv[0], H0[:, 0], a4[r], M_))
                link(T(tv[1], H0[:, 1], a4[1 - r], M_))
                link(T(tv[0], tv[0], tv[1], (S_, A_)[r]))
                last = T(VSM[:, r], VSM[:, r], tv[0], A_)
                if r:
                    last.then_inc(sem("fs_ready"), 1)
                else:
                    link(last)
            skip(KC - 1)

            with dve.Fori(0, KC) as i:
                dve.wait_ge(sem("strip_done"), i * 2 + 2)
                dve.wait_ge(sem("glu_taken1"), i + 1)
                STT(halves(NT[0]), acc(0), VEC[:, bass.ds(i + V_BGLU, 1)], halves(SG), A_, M_).then_inc(sem("glu_taken0"), 1)
                dve.wait_ge(sem("glu_taken0"), i + 1)
                T(H[:, i, :], H[:, i, :], NT[0], A_).then_inc(sem("n1_h"), 1)
                dve.wait_ge(sem("n1_h"), i + 1 + before("n1_h"))

            def normalize(name, g0, lo, hi, done):
                def chunk(m, u, later=True):
                    if later:
                        dve.wait_ge(sem(done), m - 1 + before(done))
                    STT(NT[u], H[:, m, :], VEC[:, bass.ds(m + g0, 1)] if later else VEC[:, g0 + m:g0 + m + 1], RSTD[:],
                        M_, M_).then_inc(sem(name + "_nt"), 1)

                def rest(m, u):
                    dve.wait_ge(sem(name + "_high"), m + 1 + before(name + "_high"))
                    T(lo[:, m, :], NT[u], hi[:, m, :].bitcast(F32), S_).then_inc(sem(done), 1)

                chunk(0, 0, False)
                chunk(1, 1, False)
                rest(0, 0)
                with dve.Fori(1, KC // 2) as i:
                    chunk(i * 2, 0)
                    rest(i * 2 - 1, 1)
                    chunk(i * 2 + 1, 1)
                    rest(i * 2, 0)
                rest(KC - 1, 1)

            def up(l):
                name = "up%d" % l
                dve.wait_ge(sem("p_high%d" % l), 1 + before("p_high%d" % l))
                for c in range(2):
                    T(halves(PTL[:, c, :])[:, :, 0:HP], MI[:, c, :].rearrange("p (h t) -> p h t", h=2),
                      halves(PTH[:, c, :])[:, :, 0:HP].bitcast(F32), S_)
                    last = T(halves(PTL[:, c, :])[:, :, HP:HT], ACC[:, 3, 32 * c:32 * c + 32].rearrange("p (h t) -> p h t", h=2),
                             halves(PTH[:, c, :])[:, :, HP:HT].bitcast(F32), S_)
                last.then_inc(sem("p_done%d" % l), 1)
                norm = "n%d" % (1 + 3 * l)
                reciprocal_root(norm)
                normalize(norm, V_GFFN + KC * l, NL, NH, norm + "_split")
                dve.wait_ge(sem(norm + "_split"), KC + before(norm + "_split"))
                for u in range(2):
                    link(nc.vector.memset(WK[:, u, 0:2], 0.0))

                def body(i, start=False):
                    for u, what in enumerate(("_gate", "_val")):
                        E, C = WK[:, u, :], WK[:, 2 + u, 0:CONV]
                        ch = i + FC * u
                        dve.wait_ge(sem(name + what), i + 1 + before(name + what))
                        link(cp(E[:, 2 + SEQ:EXT].rearrange("p (b s) -> p b s", s=6)[:, :, 0:2],
                                CSP[:, ch, :].rearrange("p (b s) -> p b s", s=2)))
                        cp(CT[:, ch, :].rearrange("p (j s) -> p j s", s=2),
                           E[:, TAIL0:TAIL0 + 54].rearrange("p (j s) -> p j s", s=6)[:, :, 0:2])

                        def col(vec):
                            return CP[:, l, vec, bass.ds(ch, 1)] if not start else CP[:, l, vec, ch:ch + 1]

                        link(TS(C, E[:, 2:2 + CONV], col(3), col(0), M_, A_))
                        link(STT(C, E[:, 1:1 + CONV], col(2), C, M_, A_))
                        STT(C, E[:, 0:CONV], col(1), C, M_, A_).then_inc(sem(name + ("_cg", "_cv")[u]), 1)
                    dve.wait_ge(sem(name + "_silu"), i + 1 + before(name + "_silu"))
                    dve.wait_ge(sem(name + "_cv"), i + 1 + before(name + "_cv"))
                    T(halves(TT[:])[:, :, 0:HP], WK[:, 2, 0:SEQ].rearrange("p (h t) -> p h t", h=2),
                      WK[:, 3, 0:SEQ].rearrange("p (h t) -> p h t", h=2), M_)

                    def smp(k):
                        return WK[:, k, 2 + SEQ:EXT].rearrange("p (h b s) -> p h b s", h=2, s=6)[:, :, :, 0:STEPS]

                    T(halves(TT[:])[:, :, HP:HT].rearrange("p h (b t) -> p h b t", t=STEPS), smp(2), smp(3), M_).then_inc(sem(name + "_prod"), 1)
                    dve.wait_ge(sem(name + "_high"), i + 1 + before(name + "_high"))
                    T(AL[:, i, :], TT[:], AH[:, i, :].bitcast(F32), S_).then_inc(sem(name + "_low"), 1)
                    dve.wait_ge(sem(name + "_low"), i + 1 + before(name + "_low"))

                with dve.Fori(0, FC) as i:
                    chain.enter(i, 6)
                    body(i)
                    chain.leave(FC)

            def add_chunks(stage, norm, per):
                with dve.Fori(0, KC // 2) as i:
                    for u in range(2):
                        dve.wait_ge(sem("strip_done"), i * (2 * per) + (first[stage] + per * (u + 1)))
                        T(halves(H[:, i * 2 + u, :]), acc(u), halves(H[:, i * 2 + u, :]), A_).then_inc(sem(norm + "_h"), 1)

            def ple(l):
                name, norm, nxt = "ple%d" % l, "n%d" % (2 + 3 * l), "n%d" % (3 + 3 * l)
                reciprocal_root(norm)
                normalize(norm, V_GPLE + KC * l, NL, NH, norm + "_split")
                dve.wait_ge(sem(norm + "_split"), KC + before(norm + "_split"))
                with dve.Fori(0, KC) as i:
                    dve.wait_ge(sem(name + "_sig"), i + 1 + before(name + "_sig"))
                    T(halves(NT[0]), MI[:, :, 0:HT], halves(SG), M_).then_inc(sem(name + "_in"), 1)
                    dve.wait_ge(sem(name + "_in"), i + 1 + before(name + "_in"))
                    T(H[:, i, :], H[:, i, :], NT[0], A_).then_inc(sem(nxt + "_h"), 1)
                    dve.wait_ge(sem(nxt + "_h"), i + 1 + before(nxt + "_h"))

            up(0)
            add_chunks("down0", "n2", 2)
            dve.wait_ge(sem("strip_done"), first["ple0"])
            nc.vector.memset(RB[NBUCK:NBUCK + 1, :], NEG).then_inc(sem("rb_mask"), 1)
            ple(0)

            reciprocal_root("n3")
            normalize("n3", V_GKV, NL, NH, "n3_split")
            dve.wait_ge(sem("n3_split"), KC + before("n3_split"))
            normalize("xq", V_GMIX + KC, XQL, XQH, "xq_split")
            link(TS(VEC[:, V_QN:V_QN + 1], VEC[:, V_QN:V_QN + 1], HD ** -0.5, None, M_))
            for n in range(10):
                dve.wait_ge(sem("head_root"), n + 1)
                link(nc.vector.reciprocal(SG, SG))
                row, g = (KN[:, n, :], V_KN) if n < 2 else (QN[:, n - 2, :], V_QN)
                if n < 2:
                    STT(row, row, VEC[:, g:g + 1], SG, M_, M_).then_inc(sem("head_done"), 1)
                else:
                    STT(row, row, VEC[:, g:g + 1], SG, M_, M_).then_inc(sem("head_done"), 1)

            NG = 16
            dve.wait_ge(sem("bias_in"), 16)
            dve.wait_ge(sem("sbt_in"), 16 * NSEQ * KVH)
            dve.wait_ge(sem("snk_in"), 32)
            link(cp(SBI[:, :, 0:P], SBT[:, :, 0:P]))
            link(T(SBI[:, :, P:160].rearrange("p k (b t) -> p k b t", t=STEPS),
                   SBT[:, :, P:P + STEPS].unsqueeze(2).to_broadcast([P, KVH, NSEQ, STEPS]),
                   BM[:, 0:32].rearrange("p (b t) -> p b t", t=STEPS).unsqueeze(1).to_broadcast([P, KVH, NSEQ, STEPS]), A_))
            snk = PB[:, 0, 0, 0:16]
            link(T(snk.rearrange("p (k r) -> p k r", r=RQ), SNK[:].rearrange("p (k r) -> p k r", r=RQ),
                   BM[:, 32:32 + RQ].unsqueeze(1).to_broadcast([P, KVH, RQ]), M_))
            link(nc.vector.tensor_reduce(SNKS[:], snk.rearrange("p (k r) -> p k r", r=RQ), AX_X, A_))
            S = ACC[:].rearrange("p (g a) (b n) -> p g (a b) n", g=2, b=2)

            def maxima(g, w0, w, bias, sink):
                dve.wait_ge(sem("att_scored"), g + 1)
                if g >= 2:
                    dve.wait_ge(sem("att_turned"), g - 1)
                m = SM[:, g % 2]
                for r in range(4):
                    nc.vector.tensor_tensor_reduce(out=PB[:, g % 2, r, w0:w], in0=S[:, g % 2, r, w0:w], in1=bias(r), scale=1.0,
                                                   scalar=NEG, op0=A_, op1=ALU.max, accum_out=m[:, 0, r:r + 1]).then_inc(sem("att_max"), 1)
                dve.wait_ge(sem("att_max"), 4 * (g + 1))
                link(T(m[:, 1], m[:, 0], sink, ALU.max))
                link(TS(m[:, 1], m[:, 1], -1.0, None, M_))
                T(m[:, 3], sink, m[:, 1], A_).then_inc(sem("att_neg"), 1)

            def scale(g, w0, w):
                m = SM[:, g % 2]
                dve.wait_ge(sem("att_exp"), g + 1)
                link(T(m[:, 4], m[:, 2], m[:, 3], A_))
                link(nc.vector.reciprocal(m[:, 5], m[:, 4]))
                for r in range(4):
                    last = TS(PB[:, g % 2, r, w0:w], PB[:, g % 2, r, w0:w], m[:, 5, r:r + 1], None, M_)
                last.then_inc(sem("att_probs"), 1)

            def rest(g):
                kv, n = g // 4, g % 4
                rows = slice(HD * (kv % 2), HD * (kv % 2) + HD)
                tok = HT * (n // 2) + P * (n % 2)
                dve.wait_ge(sem("att_high"), g + 1)
                T(NL[rows, 4 * (kv // 2):4 * (kv // 2) + 4, tok:tok + P], SS[rows, g % 2, :].rearrange("p (r t) -> p r t", r=4),
                  NH[rows, 4 * (kv // 2):4 * (kv // 2) + 4, tok:tok + P].bitcast(F32), S_).then_inc(sem("att_taken"), 1)

            for g in range(NG + 2):
                if g < NG:
                    kv = g // 4
                    w0 = P if g % 4 == 0 else 0
                    maxima(g, w0, 256, lambda r: BIAS[:, 4 * kv + r, w0:256], SNK[:, 4 * kv:4 * kv + 4])
                if 1 <= g <= NG:
                    scale(g - 1, P if (g - 1) % 4 == 0 else 0, 256)
                if g >= 2:
                    rest(g - 2)
            maxima(NG, 0, 160, lambda r: SBI[:, r, :], SNKS[:])
            scale(NG, 0, 160)
            dve.wait_ge(sem("att_high"), NG + 1)
            for kv in range(KVH):
                rows = slice(HD * (kv % 2), HD * (kv % 2) + HD)
                for h in range(2):
                    dst = (slice(4 * (kv // 2), 4 * (kv // 2) + 4), slice(HT * h + HP, HT * h + HT))
                    last = T(NL[rows, dst[0], dst[1]].rearrange("p r (b t) -> p r b t", t=STEPS),
                             SS[rows, 0, P * kv + 64 * h:P * kv + 64 * h + 64].rearrange("p (b r t) -> p r b t", b=4, r=4),
                             NH[rows, dst[0], dst[1]].bitcast(F32).rearrange("p r (b t) -> p r b t", t=STEPS), S_)
            last.then_inc(sem("att_taken"), 1)
            add_chunks("wo", "n4", 1)
            up(1)
            add_chunks("down1", "n5", 2)
            ple(1)
            dve.wait_ge(sem("out"), outs[0])
            cp(HSMP[:].rearrange("p m (h t) -> p m h t", h=2),
               H[:].rearrange("p m (h t) -> p m h t", h=2)[:, :, :, HP:HT]).then_inc(sem("hsmp"), 1)


_INS = ['x_prompt', 'x_sample', 'state_ssm_re', 'state_ssm_im', 'state_ffn_conv', 'cache_k_win', 'cache_v_win',
        'p_prompt', 'p_sample', 'g_mix', 'g_ffn', 'g_ple', 'ssm_lam_re', 'ssm_lam_im', 'ssm_log_dt', 'ssm_b_re',
        'ssm_b_im', 'ssm_c_re', 'ssm_c_im', 'ssm_d', 'w_glu', 'b_glu', 'g_kv', 'w_k', 'w_v', 'k_norm', 'w_q',
        'q_norm', 'sinks', 'w_o', 'rel_bias', 'w_up', 'conv_w', 'conv_b', 'w_down', 'w_ple_in', 'w_ple_gate']
_OUTS = [(1, SEQ, D), (NSEQ, STEPS, D), (1, 1, 64, 64), (1, 1, 64, 64), (1, NSEQ, 64, 64), (1, NSEQ, 64, 64),
         (2, 1, 2, 2 * FF), (2, NSEQ, 2, 2 * FF), (1, WIN, KVH, HD), (1, WIN, KVH, HD), (NSEQ, WIN, KVH, HD),
         (NSEQ, WIN, KVH, HD)]


def kernel(**inputs):
    import concourse.bacc as _bacc
    from concourse.bass_utils import run_bass_kernel_spmd as _run

    nc = _bacc.Bacc("TRN2", target_bir_lowering=False, num_devices=1)
    arrays, args = {}, []
    for name in _INS + ['consts']:
        a = constants() if name == 'consts' else np.ascontiguousarray(inputs[name])
        arrays[f"in_{name}_dram"] = a
        args.append(nc.dram_tensor(f"in_{name}_dram", a.shape, mybir.dt.from_np(a.dtype), kind="ExternalInput").ap())
    args.append(nc.dram_tensor("bias_rows", (16, P, BW), F32, kind="Internal").ap())
    for i, shape in enumerate(_OUTS):
        args.append(nc.dram_tensor(f"out_{i}_dram", shape, F32, kind="ExternalOutput").ap())
    build(nc, *args)
    r = _run(nc, [arrays], core_ids=[0])
    return tuple(r.results[0][f"out_{i}_dram"] for i in range(len(_OUTS)))
```

```python
import math
from contextlib import ExitStack

import numpy as np
import concourse.bass as bass
from concourse import mybir

F32 = mybir.dt.float32
F32R = mybir.dt.float32r
I32 = mybir.dt.int32
ALU = mybir.AluOpType
ACT = mybir.ActivationFunctionType
AX_X = mybir.AxisListType.X

P = 128
D = 1024
KC = D // P
SEQ = 512
NSEQ = 8
STEPS = 4
NTOK = SEQ + NSEQ * STEPS
HT = NTOK // 2
HP = SEQ // 2
HS_ = HT - HP
NBLK = SEQ // STEPS
HB = HT // STEPS
HPB = HP // STEPS
NCOL = NTOK // STEPS
PAIRS = 32
FQ = 4
CG = 16
FF = 2816
FC = FF // P
EXT = 2 + SEQ + NSEQ * (2 + STEPS)
CONV = EXT - 2
WKW = EXT + 4
TAIL0 = SEQ
KVH = 4
RQ = 4
HD = 64
WIN = 128
NBUCK = 32
MAXD = 128
PLE = 256
SLOT = 11
EPS = 1e-6
NEG = -1.0e30
BW = 384

C_ID, C_OH, C_BM, C_SEL, C_W = 0, 128, 128 + BW, 164 + BW, 292 + BW

(LR, LI, DT, A_RE, A_IM, C1, S1, R4, E_RE, E_IM, MAG, X0, X1, X2, X3, X4, X5, X6, X7, X8, F_RE, F_IM,
 A2_RE, A2_IM, A4_RE, A4_IM, KI) = range(27)
TURNS = 27
PR_ROWS = TURNS + 3 * 7

V_GMIX, V_GFFN, V_GPLE, V_GKV, V_D, V_BGLU, V_KN, V_QN, V_N = 0, 16, 32, 48, 56, 64, 80, 81, 82


def constants():
    c = np.zeros((P, C_W), np.float32)
    c[:, C_ID:C_ID + P] = np.eye(P, dtype=np.float32)
    for x in range(BW):
        d = BW - P - 1 - x
        if 0 <= d <= WIN:
            half = NBUCK // 2
            if d < half:
                b = d
            else:
                f = np.log(np.float32(d) / np.float32(half)) / np.float32(math.log(MAXD / half))
                b = min(half + int(np.float32(f) * np.float32(NBUCK - half)), NBUCK - 1)
            c[b, C_OH + x] = 1.0
        else:
            c[NBUCK, C_OH + x] = 1.0
    for b in range(NSEQ):
        for b2 in range(NSEQ):
            if b != b2:
                c[16 * b:16 * b + 16, C_BM + 4 * b2:C_BM + 4 * b2 + 4] = NEG
    for row in range(P):
        c[row, C_BM + 32 + row // STEPS % RQ] = 1.0
    c[0, C_SEL:C_SEL + 64] = 1.0
    c[1, C_SEL + 64:C_SEL + 128] = 1.0
    return c


class Chain:

    def __init__(self, eng, sem):
        self.eng, self.sem, self.base, self.k, self.i, self.per = eng, sem, 0, 0, None, 0

    def link(self, ins):
        self.k += 1
        ins.then_inc(self.sem, 1)
        at = self.base + self.k
        self.eng.wait_ge(self.sem, at if self.i is None else self.i * self.per + at)

    def enter(self, i, per):
        self.base += self.k
        self.k, self.i, self.per = 0, i, per

    def leave(self, turns):
        assert self.k == self.per, (self.k, self.per)
        self.base += turns * self.per
        self.k, self.i = 0, None


def build(nc, x_prompt, x_sample, state_ssm_re, state_ssm_im, state_ffn_conv, cache_k_win, cache_v_win,
          p_prompt, p_sample, g_mix, g_ffn, g_ple, ssm_lam_re, ssm_lam_im, ssm_log_dt, ssm_b_re,
          ssm_b_im, ssm_c_re, ssm_c_im, ssm_d, w_glu, b_glu, g_kv, w_k, w_v, k_norm, w_q, q_norm,
          sinks, w_o, rel_bias, w_up, conv_w, conv_b, w_down, w_ple_in, w_ple_gate, consts, bias_rows,
          y_prompt, y_sample, ssm_re_p, ssm_im_p, ssm_re_s, ssm_im_s, conv_p, conv_s,
          k_win_p, v_win_p, k_win_s, v_win_s):
    with ExitStack() as ctx:
        sems = {}

        def shared(name):
            stage, _, what = name.partition("_")
            if stage in ("n0", "n1", "n2", "n3", "n4", "n5", "n6", "xq") and what:
                if what in ("sq", "summed"):
                    return "norm_" + what, KC * int(stage[1])
                if what == "root":
                    return "norm_root", int(stage[1])
                if what == "total":
                    return "norm_total", int(stage[1]) - 1
                if what == "h":
                    return "residual_added", KC * (int(stage[1]) - 1)
                return "norm_" + what, KC * ("n1", "n2", "n3", "xq", "n4", "n5").index(stage)
            if stage in ("up0", "up1"):
                return "up_" + what, FC * int(stage[2])
            if stage in ("ple0", "ple1"):
                return "ple_" + what, KC * int(stage[3])
            if name[:-1] in ("cst_in", "ct_done", "ct_made", "cs_turned", "cs_done", "p_made", "p_high", "p_done", "cs_low"):
                return name[:-1], {"cst_in": 48, "ct_done": FC // 2, "ct_made": FC // 2}.get(name[:-1], 1) * int(name[-1])
            return name, 0

        def sem(name):
            name, _ = shared(name)
            if name not in sems:
                sems[name] = ctx.enter_context(nc.semaphore(name))
            return sems[name]

        def before(name):
            return shared(name)[1]

        base = (nc.sbuf_base + 31) // 32 * 32
        room = (nc.sbuf_usable_end - base) // 32 * 32
        ctx.enter_context(nc.sbuf_tensor("arena", [P, room // 4 - 8], F32))

        class Region:
            def __init__(self, at):
                self.at = at

            def __call__(self, name, shape, dt=F32):
                t = nc.alloc_sbuf_tensor_at(name, shape, dt, offset=self.at)
                self.at += (int(np.prod(shape[1:])) * 4 + 31) // 32 * 32
                assert self.at <= base + room - 32, (name, self.at - base - room)
                return t

        perm = Region(base)
        H = perm("H", [P, KC, NTOK])
        n_at = perm.at
        NH = perm("NH", [P, KC, NTOK], F32R)
        nl_at = perm.at
        NL = perm("NL", [P, KC, NTOK], F32R)
        RAW = perm("RAW", [P, 2, SLOT, P])
        SPL = perm("SPL", [P, 2, 2, SLOT, P], F32R)
        WK = perm("WK", [P, 4, WKW])
        RSTD = perm("RSTD", [P, NTOK])
        ONES = perm("ONES", [P, P])
        BONES = perm("BONES", [P, P])
        IDN = perm("IDN", [P, P])
        VEC = perm("VEC", [P, V_N])
        CP = perm("CP", [P, 2, 4, FC * 2])
        EPSB = perm("EPSB", [P, 1])
        TIC2 = perm("TIC2", [P, 1])
        TIC = perm("TIC", [P, 1])
        SQ = WK[:, 0, 0:NTOK]
        NEW = WK[:, 1, 0:NTOK]
        GATE = WK[:, 2, 0:NTOK]
        SG = WK[:, 3, 0:NTOK]
        CTO = WK[0:18, 1:3, 0:512]

        U = nc.alloc_sbuf_tensor_at("U", [P, KC, NTOK], F32, offset=n_at)
        PC = nc.alloc_sbuf_tensor_at("PC", [P, KC, NTOK], F32, offset=nl_at)
        ph1 = Region(perm.at)
        EROT = ph1("EROT", [P, 2, PAIRS, NBLK])
        CAC = ph1("CAC", [P, 5, 2, PAIRS, CG])
        H0 = ph1("H0", [P, 2, NSEQ, PAIRS])
        VSM = ph1("VSM", [P, 2, NSEQ, PAIRS])
        FS = ph1("FS", [P, 2, PAIRS])
        PR = ph1("PR", [P, PR_ROWS, PAIRS])
        xs_at = ph1.at
        BT = ph1("BT", [P, FQ, 2, P])
        PBD = ph1("PBD", [P, FQ, 2, 4, 32])
        CBD = ph1("CBD", [P, 4, 2, P])
        C0BD = ph1("C0BD", [P, 2, P])
        KM = ph1("KM", [P, 2, 4, P])
        TB = ph1("TB", [P, 2, 2, 8, NBLK // 2])
        xs_room = ph1.at
        UZ = ph1("UZ", [P, 2, FQ, NCOL])
        V = ph1("V", [P, 2, FQ, NBLK])
        T2 = ph1("T2", [P, 2, FQ, NBLK])
        HSV = ph1("HSV", [P, 2, 2, FQ, NCOL])
        T1 = WK[:, 2:4, :].rearrange("p a b -> p (a b)")[:, 0:2 * FQ * NBLK]
        ZT = WK[:, 1, 0:NTOK]
        XS = nc.alloc_sbuf_tensor_at("XS", [P, 5, D], F32, offset=xs_at)
        stg = Region(max(xs_room, xs_at + 5 * D * 4))
        LAMS = stg("LAMS", [64, P])
        VECS = stg("VECS", [V_N, P])
        CPS = stg("CPS", [88, 4, P])
        CS_ = stg("CSTG", [P, 2, 4, P])
        STS = stg("STS", [P, 2, 2, P])
        BC = stg("BC", [P, 2, PAIRS, CG])
        TAB = stg("TAB", [P, 2, 512])
        TE = stg("TE", [P, 2, 512])
        LD2 = stg("LD2", [2, PAIRS])
        SEL = stg("SEL", [2, P])

        ff = Region(perm.at)
        AH = ff("AH", [P, FC, NTOK], F32R)
        AL = ff("AL", [P, FC, NTOK], F32R)
        PTH = ff("PTH", [P, 2, NTOK], F32R)
        PTL = ff("PTL", [P, 2, NTOK], F32R)
        CT = ff("CT", [P, 2 * FC, 18])
        CSP = CT[:, :, 0:2 * NSEQ]
        TT = ff("TT", [P, NTOK])
        SQS = TT

        fst = Region(perm.at)
        CST = fst("CST", [16, 2 * FF])
        yst = Region(perm.at)
        YS = yst("YS", [P, 4, D])
        YSS = yst("YSS", [32, D])
        HSMP = yst("HSMP", [P, KC, 32])
        FSO = nc.alloc_sbuf_tensor_at("FSO", [PAIRS, 2, P], F32, offset=xs_at)
        VSO = nc.alloc_sbuf_tensor_at("VSO", [P, 2, 2, P], F32, offset=xs_at + 1024)
        PST = nc.alloc_sbuf_tensor_at("PST", [P, 5, PLE], F32, offset=fst.at + 32)

        at = Region(perm.at)
        QN = at("QN", [P, KC, NTOK])
        KN = at("KN", [P, 2, NTOK])
        VT = at("VT", [P, 2, NTOK])
        VTOK = at("VTOK", [P, 4, KVH * HD])
        KVS = at("KVS", [2 * NSEQ * 2, 2, KVH * HD])
        KTP = at("KTP", [P, KVH * HD])
        KCT = at("KCT", [P, 2, NSEQ, WIN])
        VCS = at("VCS", [P, NSEQ, KVH * HD])
        RBR = at("RBR", [16, BW])
        RB = at("RB", [NBUCK + 1, 16])
        OHB = at("OHB", [NBUCK + 1, BW])
        BM = at("BM", [P, 32 + RQ])
        SNK = at("SNK", [P, 16])
        SNKS = at("SNKS", [P, KVH])
        SBT = at("SBT", [P, KVH, WIN + STEPS])
        SBI = at("SBI", [P, KVH, 160])
        BIAS = at("BIAS", [P, 16, 256])
        VTS = at("VTS", [P, 2, 32])
        SM = at("SM", [P, 2, 6, 4])
        ux = Region(at.at)
        XQH = ux("XQH", [P, KC, NTOK], F32R)
        XQL = ux("XQL", [P, KC, NTOK], F32R)
        ug = Region(at.at)
        PB = ug("PB", [P, 2, 4, 256])
        KCS = ug("KCS", [P, NSEQ, KVH * HD])
        PTR = ug("PTR", [P, 2, 2, 512])

        ACC = ctx.enter_context(nc.psum_tensor("ACC", [P, 4, 512], F32))
        SS = ctx.enter_context(nc.psum_tensor("SS", [P, 2, 512], F32))
        MI = ctx.enter_context(nc.psum_tensor("MI", [P, 2, 512], F32))

        def acc(u):
            return ACC[:, 2 * u:2 * u + 2, 0:HT]

        def halves(row):
            return row.rearrange("p (h t) -> p h t", h=2)

        order = [("glu", 16), ("up0", 44), ("down0", 16), ("ple0", 8), ("kv", 4), ("q", 8), ("wo", 8),
                 ("up1", 44), ("down1", 16), ("ple1", 8)]
        first, at_ = {}, 0
        for name, n in order:
            first[name] = at_
            at_ += n

        def strip_of(name, n):
            return n + first[name]

        block = ctx.enter_context(nc.Block())
        outs = [0]
        outs_mid = [0]

        @block.sync
        def _(sp):
            LOAD = [sem("load0"), sem("load1")]

            with nc.allow_non_contiguous_dma(reason="64 small elements"):
                sp.dma_start(IDN[:], consts[:, C_ID:C_ID + P]).then_inc(sem("const_in"), 16)
                sp.dma_start(SEL[:], consts[0:2, C_SEL:C_SEL + P]).then_inc(sem("const_in"), 16)
                sp.dma_start(LAMS[0:32, :], ssm_lam_re[0].rearrange("(q a) s -> q (a s)", a=2)).then_inc(sem("lam_in"), 16)
                sp.dma_start(LAMS[32:64, :], ssm_lam_im[0].rearrange("(q a) s -> q (a s)", a=2)).then_inc(sem("lam_in"), 16)
                sp.dma_start(LD2[:], ssm_log_dt[0].rearrange("(q a) -> a q", a=2)).then_inc(sem("lam_in"), 16)
            for r, src in enumerate((ssm_b_re, ssm_b_im)):
                sp.dma_start(BC[:, r], src[0].rearrange("(q a) s c -> (a s) q c", a=2)).then_inc(sem("b_in"), 16)
            for r, src in enumerate((ssm_c_re, ssm_c_im)):
                for t in range(4):
                    for a in range(2):
                        sp.dma_start(CS_[:, r, t, 64 * a:64 * a + 64],
                                     src[0].rearrange("(t q a) c s -> t a q c s", t=4, a=2)[t, a]).then_inc(sem("c_in"), 16)
            for b in range(4):
                sp.dma_start(XS[:, b, :], x_prompt[0, P * b:P * b + P, :]).then_inc(sem("x_in"), 16)
            sp.dma_start(XS[0:32, 4, :], x_sample.rearrange("b t d -> (b t) d")).then_inc(sem("x_in"), 16)
            for at0, src in ((V_GMIX, g_mix), (V_GFFN, g_ffn), (V_GPLE, g_ple)):
                sp.dma_start(VECS[at0:at0 + 16, :], src.rearrange("l (c p) -> (l c) p", p=P)).then_inc(sem("vec_in"), 16)
            sp.dma_start(VECS[V_GKV:V_GKV + 8, :], g_kv.rearrange("(c p) -> c p", p=P)).then_inc(sem("vec_in"), 16)
            sp.dma_start(VECS[V_D:V_D + 8, :], ssm_d.rearrange("l (c p) -> (l c) p", p=P)).then_inc(sem("vec_in"), 16)
            sp.dma_start(VECS[V_BGLU:V_BGLU + 16, :], b_glu.rearrange("l (c p) -> (l c) p", p=P)).then_inc(sem("vec_in"), 16)
            for row, src in ((V_KN, k_norm.rearrange("(a d) -> a d", a=1)), (V_QN, q_norm)):
                for a in range(2):
                    sp.dma_start(VECS[row:row + 1, 64 * a:64 * a + 64], src).then_inc(sem("vec_in"), 16)
            for r, src in enumerate((state_ssm_re, state_ssm_im)):
                for hf in range(2):
                    sp.dma_start(STS[:, r, hf, :],
                                 src[0].rearrange("b (h q a) s -> h b q (a s)", h=2, a=2)[hf]).then_inc(sem("st_in"), 16)
            for l in range(2):
                sp.dma_start(CPS[0:44, 2 * l, :], conv_b[l].rearrange("(c p) -> c p", p=P)).then_inc(sem("cp_in"), 16)
                sp.dma_start(CPS[44:88, 2 * l, :], conv_w[l, 0].rearrange("(c p) -> c p", p=P)).then_inc(sem("cp_in"), 16)
                sp.dma_start(CPS[0:44, 2 * l + 1, :], conv_w[l, 1].rearrange("(c p) -> c p", p=P)).then_inc(sem("cp_in"), 16)
                sp.dma_start(CPS[44:88, 2 * l + 1, :], conv_w[l, 2].rearrange("(c p) -> c p", p=P)).then_inc(sem("cp_in"), 16)

            def columns(w, c0, n=P):
                return w.rearrange("(k p) n -> p k n", p=P)[:, :, bass.ds(c0, n)]

            def stream(name, parts):
                def turn(i, free):
                    for u in range(2):
                        if free:
                            sp.wait_ge(sem("split_done"), i * 2 + (strip_of(name, u) - 1))
                        todo = parts(i, u)
                        for dst, src in todo:
                            sp.dma_start(dst, src).then_inc(LOAD[u], 64 // len(todo))

                n = dict(order)[name] // 2
                if name == "glu":
                    turn(0, False)
                    for f in range(KC):
                        sp.wait_ge(sem("u_ready"), f + 1)
                        if f >= 2:
                            sp.wait_ge(sem("v_made"), f - 1)
                        for j in range(STEPS):
                            for q in range(FQ):
                                sp.dma_start(UZ[32 * j:32 * j + 32, f % 2, q, :],
                                             U[32 * q:32 * q + 32, f, NCOL * j:NCOL * j + NCOL]).then_inc(sem("uz_in%d" % (f % 2)), 16)
                    with sp.Fori(1, n) as i:
                        turn(i, True)
                else:
                    with sp.Fori(0, n) as i:
                        turn(i, True)

            def up_parts(l):
                return lambda i, u: [(RAW[:, u, 0:KC, :], columns(w_up[l], i * P + FF * u))]

            def down_parts(l):
                return lambda i, u: [(RAW[:, u, 0:SLOT, :],
                                      w_down[l, SLOT * P * u:SLOT * P * (u + 1), :].rearrange("(k p) n -> p k n", p=P)[:, :, bass.ds(i * P, P)])]

            def ple_parts(l):
                return lambda i, u: [(RAW[:, u, 0:KC, :], columns(w_ple_gate[l], i * 2 * P + P * u)),
                                     (RAW[:, u, KC:KC + 2, :], columns(w_ple_in[l], i * 2 * P + P * u))]

            stream("glu", lambda i, u: [(RAW[:, u, 0:KC, :], columns(w_glu[0], (i + 1) * P + (D * (1 - u) - P)))])
            stream("up0", up_parts(0))
            stream("down0", down_parts(0))
            stream("ple0", ple_parts(0))
            flat = bias_rows.rearrange("h a n -> h (a n)")

            def window(h0, h1, rows, cols):
                v = flat[h0:h1, 127:127 + rows * (BW - 1)].rearrange("h (t s) -> h t s", s=BW - 1)
                return v[:, :, 0:cols]

            for s in range(4):
                sp.wait_ge(sem("split_done"), strip_of("kv", s) - 1)
                sp.dma_start(RAW[:, s % 2, 0:KC, :], columns((w_k, w_v)[s // 2], (s % 2) * P)).then_inc(LOAD[s % 2], 64)
            for s in range(8):
                p2, r = s // 4, s % 4
                sp.wait_ge(sem("split_done"), strip_of("q", s) - 1)
                for a in range(2):
                    sp.dma_start(RAW[:, s % 2, 0:KC, HD * a:HD * a + HD],
                                 columns(w_q[0], (8 * p2 + 4 * a + r) * HD, HD)).then_inc(LOAD[s % 2], 32)
                if s == 0:
                    sp.wait_ge(sem("rows_out"), 16)
                    sp.dma_start(BIAS[:], window(0, 16, P, 256).rearrange("h t s -> t h s")).then_inc(sem("bias_in"), 16)
                for k in range(KVH):
                    sp.dma_start(SBT[16 * s:16 * s + 16, k, :], window(RQ * k, RQ * k + RQ, STEPS, WIN + STEPS)).then_inc(sem("sbt_in"), 16)
            sp.wait_ge(sem("tok_done"), 6)
            sp.dma_start(k_win_p[0].rearrange("s k d -> s (k d)"), KTP[:]).then_inc(sem("kv_out"), 16)
            sp.dma_start(v_win_p[0].rearrange("s k d -> s (k d)"), VTOK[:, 3, :]).then_inc(sem("kv_out"), 16)
            for src, cache, out in ((0, cache_k_win, k_win_s), (1, cache_v_win, v_win_s)):
                sp.dma_start(out[:, 0:WIN - STEPS].rearrange("b s k d -> b s (k d)"),
                             cache[:, STEPS:WIN].rearrange("b s k d -> b s (k d)")).then_inc(sem("kv_out"), 16)
                for b in range(NSEQ):
                    sp.dma_start(out[b, WIN - STEPS:WIN].rearrange("s k d -> s (k d)"),
                                 KVS[STEPS * b:STEPS * b + STEPS, src, :]).then_inc(sem("kv_out"), 16)
            wo_v = w_o[0].rearrange("(p a r d) n -> p a d r n", p=2, a=2, r=4)
            stream("wo", lambda i, u: [(RAW[HD * a:HD * a + HD, u, 4 * p2:4 * p2 + 4, :],
                                        wo_v[p2, a, :, :, bass.ds(i * 2 * P + P * u, P)])
                                       for p2 in range(2) for a in range(2)])
            stream("up1", up_parts(1))
            stream("down1", down_parts(1))
            stream("ple1", ple_parts(1))

        @block.gpsimd
        def _(pool):
            chain = Chain(pool, sem("pool_chain"))
            LOAD = [sem("load0"), sem("load1")]
            PIN = nc.gpsimd
            chain.link(PIN.memset(ONES[:], 1.0))
            chain.link(PIN.memset(EPSB[:], EPS))
            chain.link(PIN.memset(BONES[0:64, 64:128], 0.0))
            chain.link(PIN.memset(BONES[64:128, 0:64], 0.0))
            chain.link(PIN.memset(BONES[0:64, 0:64], 1.0))
            chain.link(PIN.memset(BONES[64:128, 64:128], 1.0))
            PIN.memset(TIC[:], 0.0).then_inc(sem("ones_set"), 1)
            pool.wait_ge(sem("a_ready"), 1)
            pool.wait_ge(sem("c_turned"), 2)

            def wide(j):
                return PR[:, j, :].unsqueeze(2).to_broadcast([P, PAIRS, CG])

            def more_c(i, tabs):
                tab = [t.rearrange("p (q c) -> p q c", c=CG) for t in tabs]
                for o in range(2):
                    PIN.tensor_tensor(tab[0], CAC[:, i, 0], wide(A_RE + o), ALU.mult)
                    chain.link(PIN.tensor_tensor(tab[1], CAC[:, i, 1], wide(A_IM - o), ALU.mult))
                    chain.link(PIN.tensor_tensor(CAC[:, i + 1, o], tab[0], tab[1], (ALU.subtract, ALU.add)[o]))

            def turns(g):
                pairs = slice(8 * g, 8 * g + 8)
                for lv in range(7):
                    m = 2 ** lv
                    for r in range(2):
                        by = PR[:, TURNS + 3 * lv + r:TURNS + 3 * lv + r + 2, pairs].unsqueeze(3).to_broadcast([P, 2, 8, m])
                        last = PIN.tensor_tensor(TB[:, r, :, :, 0:m],
                                                 EROT[:, r, pairs, 0:m].unsqueeze(1).to_broadcast([P, 2, 8, m]), by, ALU.mult)
                    chain.link(last)
                    PIN.tensor_tensor(EROT[:, 0, pairs, m:2 * m], TB[:, 0, 0, :, 0:m], TB[:, 1, 0, :, 0:m], ALU.subtract)
                    last = PIN.tensor_tensor(EROT[:, 1, pairs, m:2 * m], TB[:, 0, 1, :, 0:m], TB[:, 1, 1, :, 0:m], ALU.add)
                    if lv < 6:
                        chain.link(last)
                last.then_inc(sem("turns_ready"), 1)
                pool.wait_ge(sem("turns_ready"), g + 1)

            for i in range(2):
                more_c(i, (TAB[:, 0, :], TAB[:, 1, :]))
            PIN.memset(TAB[:, 0, 0:1], 0.0).then_inc(sem("tab_free"), 1)
            pool.wait_ge(sem("x_turned"), KC + 1)
            for t in (PBD, CBD, C0BD):
                PIN.memset(t[:], 0.0)
            PIN.memset(KM[:], 0.0).then_inc(sem("zeros_set"), 1)
            pool.wait_ge(sem("turns_in"), 1)
            PIN.memset(EROT[:, 0, :, 0:1], 1.0)
            chain.link(PIN.memset(EROT[:, 1, :, 0:1], 0.0))
            turns(0)
            tb = TB[:].rearrange("p a o q c -> p (a o) (q c)")
            for i in range(2, 4):
                more_c(i, (tb[:, 0, :], tb[:, 1, :]))
            PIN.memset(TIC[:], 0.0).then_inc(sem("ca_ready"), 1)
            for g in range(1, PAIRS // 8):
                turns(g)

            def split(name, i, u, kt, count):
                n = i * 2 + strip_of(name, u)
                hi, lo = SPL[:, u, 0, 0:kt, :], SPL[:, u, 1, 0:kt, :]
                pool.wait_ge(LOAD[u], (n - u) * 32 + 64)
                if count:
                    pool.wait_ge(sem("strip_done"), n - 1)
                PIN.tensor_tensor(TIC[:], EPSB[:], EPSB[:], ALU.add)
                PIN.tensor_scalar(hi, RAW[:, u, 0:kt, :], 1.0, 1.0, ALU.mult, ALU.mult).then_inc(sem("high_done"), 1)
                pool.wait_ge(sem("high_done"), n + 1)
                PIN.tensor_tensor(lo, RAW[:, u, 0:kt, :], hi.bitcast(F32), ALU.subtract).then_inc(sem("split_done"), 1)

            for name, n in order:
                kt = {"down": SLOT, "ple": KC + 2}.get(name.rstrip("01"), KC)
                if name == "glu":
                    for u in range(2):
                        split(name, 0, u, kt, False)
                with pool.Fori(1 if name == "glu" else 0, n // 2) as i:
                    for u in range(2):
                        split(name, i, u, kt, True)

        @block.tensor
        def _(pe):
            mm = nc.tensor.matmul
            tr = nc.tensor.transpose

            def turn(out, in_, rows):
                return tr(out, in_, IDN[0:rows, 0:rows])

            pe.wait_ge(sem("const_in"), 32)
            pe.wait_ge(sem("lam_in"), 48)
            turn(SS[:, 0, 0:64], LAMS[:], 64)
            mm(SS[:, 0, 64:96], SEL[:], LD2[:], start=True, stop=True).then_inc(sem("lam_turned"), 1)
            pe.wait_ge(sem("c_in"), 256)
            for r in range(2):
                for t in range(4):
                    last = turn(ACC[:, 2 + r, P * t:P * t + P], CS_[:, r, t, :], P)
                last.then_inc(sem("c_made"), 1)
            pe.wait_ge(sem("x_in"), 80)
            for m in range(KC):
                if m >= 2:
                    pe.wait_ge(sem("x_turned"), m - 1)
                for b in range(4):
                    last = turn(MI[:, m % 2, P * b:P * b + P], XS[:, b, P * m:P * m + P], P)
                last.then_inc(sem("x_made"), 1)
            for m in range(KC):
                last = turn(ACC[:, 0, 32 * m:32 * m + 32], XS[0:32, 4, P * m:P * m + P], 32)
            last.then_inc(sem("x_made"), 1)
            pe.wait_ge(sem("vec_in"), 160)
            turn(SS[:, 1, 0:V_N], VECS[:], V_N).then_inc(sem("vec_made"), 1)
            pe.wait_ge(sem("cp_in"), 128)
            for t in range(4):
                last = turn(ACC[:, 1, 88 * t:88 * t + 88], CPS[:, t, :], 88)
            last.then_inc(sem("cp_made"), 1)
            pe.wait_ge(sem("st_in"), 64)
            pe.wait_ge(sem("x_turned"), KC)
            for r in range(2):
                for h in range(2):
                    last = turn(MI[:, r, P * h:P * h + P], STS[:, r, h, :], P)
            last.then_inc(sem("st_made"), 1)

            def sumsq(name, m, start=False, stop=False, row=SQ):
                pe.wait_ge(sem(name + "_sq"), m + 1 + before(name + "_sq"))
                for h in range(2):
                    last = mm(SS[:, h, 0:HT], ONES[:], row[:, HT * h:HT * h + HT], start=start, stop=stop)
                last.then_inc(sem(name + "_summed"), 1)

            def total(name):
                pe.wait_ge(sem(name + "_summed"), KC + before(name + "_summed"))
                for h in range(2):
                    last = mm(SS[:, h, 0:HT], ONES[:], SQS[:, HT * h:HT * h + HT], start=True, stop=True)
                last.then_inc(sem(name + "_total"), 1)

            pe.wait_ge(sem("ones_set"), 1)
            pe.wait_ge(sem("lam_taken"), 1)
            pe.wait_ge(sem("vec_done"), 1)
            for m in range(KC):
                sumsq("n0", m, m == 0, m == KC - 1, WK[:, m % 2, 0:NTOK])

            Y = SS[:].rearrange("p a (i n) -> p (a i) n", i=2)
            KAT = 2 * NCOL

            def prep(f):
                pe.wait_ge(sem("pbd_ready"), f + 1)
                if f:
                    pe.wait_ge(sem("bt_done"), f)
                for q in range(FQ):
                    for r in range(2):
                        last = turn(MI[:, q // 2, P * (2 * (q % 2) + r):P * (2 * (q % 2) + r) + P],
                                    PBD[:, q, r].rearrange("p j c -> p (j c)"), P)
                last.then_inc(sem("p_turned"), 1)

            def inputs(f):
                pe.wait_ge(sem("c0_ready"), f + 1)
                if f:
                    pe.wait_ge(sem("v_taken"), f)
                    pe.wait_ge(sem("k_done"), f)
                    pe.wait_ge(sem("vsm_done"), f)
                for q in range(FQ):
                    rows = slice(32 * q, 32 * q + 32)
                    for t in range(4):
                        for r in range(2):
                            last = mm(ACC[rows, 0, KAT + 32 * t:KAT + 32 * t + 32], PBD[:, q, r, 3 - t, :], C0BD[:, r, rows],
                                      start=r == 0, stop=r == 1, skip_group_check=True)
                last.then_inc(sem("k_made"), 1)
                pe.wait_ge(sem("bt_done"), f + 1)
                pe.wait_ge(sem("uz_in%d" % (f % 2)), 16 * FQ * STEPS * (f // 2 + 1))
                for q in range(FQ):
                    for r in range(2):
                        last = mm(ACC[:, q, NCOL * r:NCOL * r + NCOL], BT[:, q, r, :], UZ[:, f % 2, q, :],
                                  start=True, stop=True, skip_group_check=True)
                last.then_inc(sem("v_made"), 1)

            def outputs(f):
                par = f % 2
                pe.wait_ge(sem("k_done"), f + 1)
                pe.wait_ge(sem("cbd_ready"), f + 1)
                pe.wait_ge(sem("h_ready"), f + 1)
                pe.wait_ge(sem("h0_placed"), f + 1)
                if f:
                    pe.wait_ge(sem("y_taken"), f)
                else:
                    pe.wait_ge(sem("n0_root"), 1 + before("n0_root"))
                for i in range(STEPS):
                    for j in range(i + 1):
                        mm(Y[:, i, 0:NCOL], KM[:, par, i - j, :], U[:, f, NCOL * j:NCOL * j + NCOL], start=j == 0, stop=False,
                           skip_group_check=True)
                    for r in range(2):
                        for q in range(FQ):
                            rows = slice(32 * q, 32 * q + 32)
                            last = mm(Y[rows, i, 0:NCOL], CBD[:, i, r, rows], HSV[:, par, r, q, :], start=False,
                                      stop=r == 1, skip_group_check=True)
                last.then_inc(sem("y_made"), 1)

            for f in range(KC):
                prep(f)
                inputs(f)
                if f:
                    outputs(f - 1)
            outputs(KC - 1)
            pe.wait_ge(sem("fs_ready"), 1)
            for r in range(2):
                turn(MI[0:PAIRS, 1, P * r:P * r + P], FS[:, r, :], P)
                for h in range(2):
                    last = turn(MI[:, 0, P * (2 * r + h):P * (2 * r + h) + P],
                                VSM[:, r, 4 * h:4 * h + 4, :].rearrange("p b q -> p (b q)"), P)
            last.then_inc(sem("fs_turned"), 1)

            def product(u, out, kt, k0, xh, xl, start, stop, w0=0, ready=None):
                for k in range(kt):
                    if ready:
                        pe.wait_ge(sem(ready), k0 + k + 1 + before(ready))
                    for n, (w, x) in enumerate(((0, xh), (0, xl), (1, xh))):
                        for h in range(2):
                            last = mm(out[:, h, :], SPL[:, u, w, w0 + k, :], x[:, k0 + k, HT * h:HT * h + HT],
                                      start=start and k == 0 and n == 0, stop=stop and k == kt - 1 and n == 2)
                return last

            def strip(name, i, u, per=2):
                pe.wait_ge(sem("split_done"), i * per + (strip_of(name, u) + 1))

            def glu(i, ready=None, free=True, between=(None, None)):
                for u in range(2):
                    if between[u]:
                        between[u](0)
                    strip("glu", i, u)
                    if free:
                        pe.wait_ge(sem("glu_taken%d" % u), i + before("glu_taken%d" % u))
                    product(u, acc(u), KC, 0, NH, NL, True, True, ready=ready if u == 0 else None).then_inc(sem("strip_done"), 1)

            pe.wait_ge(sem("v_taken"), KC)
            glu(0, ready="z_split", free=False)
            glu(1)
            pe.wait_ge(sem("y_taken"), KC)
            with pe.Fori(2, KC - 1) as i:
                glu(i)

            def turn_past(l):
                name = "up%d" % l
                pe.wait_ge(sem("cst_in%d" % l), 48 + before("cst_in%d" % l))
                if l == 0:
                    pe.wait_ge(sem("fs_out"), 1)
                for c in range(2 * FC):
                    turn(MI[:, c // FC, 16 * (c % FC):16 * (c % FC) + 16], CST[:, P * c:P * c + P], 16)
                for c in range(2):
                    last = turn(MI[:, c, 16 * FC:16 * FC + 32], PST[0:32, 4, P * c:P * c + P], 32)
                last.then_inc(sem("cs_turned%d" % l), 1)

            def turn_ple(l):
                pe.wait_ge(sem("cs_done%d" % l), 1 + before("cs_done%d" % l))
                pe.wait_ge(sem("cs_low%d" % l), 1 + before("cs_low%d" % l))
                for c in range(2):
                    for b in range(4):
                        last = turn(MI[:, c, P * b:P * b + P], PST[:, b, P * c:P * c + P], P)
                last.then_inc(sem("p_made%d" % l), 1)

            glu(KC - 1, between=(turn_past, turn_ple))
            def up(l):
                name, norm = "up%d" % l, "n%d" % (1 + 3 * l)

                def body(i, ready=None, free=True):
                    for u in range(2):
                        strip(name, i, u)
                        if free:
                            pe.wait_ge(sem(name + ("_gate", "_val")[u]), i + before(name + ("_gate", "_val")[u]))
                        elif u == 1:
                            pe.wait_ge(sem("p_done%d" % l), 1 + before("p_done%d" % l))
                        product(u, acc(u), KC, 0, NH, NL, True, True, ready=ready if u == 0 else None).then_inc(sem("strip_done"), 1)
                        if not free and u == 0:
                            total(norm)

                pe.wait_ge(sem(norm + "_h"), KC + before(norm + "_h"))
                body(0, norm + "_split", False)
                with pe.Fori(1, FC) as i:
                    body(i)

            def down(l):
                name, norm, upn = "down%d" % l, "n%d" % (2 + 3 * l), "up%d" % l

                def turn_last(g):
                    if g >= 2:
                        pe.wait_ge(sem("ct_done%d" % l), g - 1 + before("ct_done%d" % l))
                    for c in range(4):
                        last = turn(MI[0:18, g % 2, P * c:P * c + P], CT[:, 4 * g + c, :], P)
                    last.then_inc(sem("ct_made%d" % l), 1)

                def one(i, v, first=False, start=False, groups=((), ())):
                    for u in range(2):
                        pe.wait_ge(sem("split_done"), i * 4 + (strip_of(name, 2 * v + u) + 1))
                        if u == 0 and not start:
                            pe.wait_ge(sem(norm + "_h"), i * 2 + (v - 1) + before(norm + "_h"))
                        last = product(u, acc(v), SLOT, SLOT * u, AH, AL, u == 0, u == 1,
                                       ready=upn + "_low" if first else None)
                        last.then_inc(sem("strip_done"), 1)
                        for g in groups[u]:
                            turn_last(g)

                pe.wait_ge(sem(upn + "_gate"), FC + before(upn + "_gate"))
                one(0, 0, True, True, groups=((0, 1), (2, 3)))
                pe.wait_ge(sem(upn + "_val"), FC + before(upn + "_val"))
                one(0, 1, False, True, groups=((4, 5), (6, 7)))
                one(1, 0, groups=((8, 9), (10,)))
                one(1, 1)
                with pe.Fori(2, KC // 2) as i:
                    one(i, 0)
                    one(i, 1)

            def ple(l):
                name, norm = "ple%d" % l, "n%d" % (3 + 3 * l)

                def one(i, u, ready=None, start=False):
                    strip(name, i, u)
                    if not start:
                        pe.wait_ge(sem(norm + "_h"), i * 2 + (u - 1) + before(norm + "_h"))
                    product(u, acc(u), KC, 0, NH, NL, True, True, ready=ready)
                    if ready:
                        total("n%d" % (2 + 3 * l))
                        pe.wait_ge(sem("ct_done%d" % l), FC // 2 + before("ct_done%d" % l))
                    else:
                        pe.wait_ge(sem(name + "_in"), i * 2 + u + before(name + "_in"))
                    product(u, MI[:, :, 0:HT], 2, 0, PTH, PTL, True, True, w0=KC).then_inc(sem("strip_done"), 1)

                pe.wait_ge(sem("n%d_h" % (2 + 3 * l)), KC + before("n%d_h" % (2 + 3 * l)))
                one(0, 0, "n%d_split" % (2 + 3 * l), True)
                one(0, 1, None, True)

                def turn_result(m, u, first=False):
                    pe.wait_ge(sem("n6_h"), m + 1 + before("n6_h"))
                    if not first:
                        pe.wait_ge(sem("y_done"), m)
                    for b in range(4):
                        at_ = HT * (b // 2) + P * (b % 2)
                        last = turn(SS[:, u, P * b:P * b + P], (SQ, TT[:])[u][:, at_:at_ + P], P)
                    last.then_inc(sem("y_turned"), 1)

                if l == 1:
                    turn_result(0, 0, True)
                with pe.Fori(1, KC // 2) as i:
                    one(i, 0)
                    if l == 1:
                        turn_result(i * 2 - 1, 1)
                    one(i, 1)
                    if l == 1:
                        turn_result(i * 2, 0)
                if l == 1:
                    turn_result(KC - 1, 1)
                    for m in range(KC):
                        last = turn(ACC[0:32, m // 4, P * (m % 4):P * (m % 4) + P], HSMP[:, m, :], P)
                    last.then_inc(sem("y_turned"), 1)

            up(0)
            down(0)
            ple(0)

            pe.wait_ge(sem("rb_dma"), 32)
            pe.wait_ge(sem("rb_mask"), 1)
            pe.wait_ge(sem("n3_h"), KC + before("n3_h"))
            mm(MI[0:16, 0, 0:BW], RB[:], OHB[:], start=True, stop=True).then_inc(sem("rb_made"), 1)

            def head_sums(n):
                pe.wait_ge(sem("head_sq"), n + 1)
                for h in range(2):
                    last = mm(SS[:, h, 0:HT], BONES[:], SQ[:, HT * h:HT * h + HT], start=True, stop=True)
                last.then_inc(sem("head_summed"), 1)

            def turn_tokens():
                pe.wait_ge(sem("rb_done"), 1)
                pe.wait_ge(sem("head_done"), 2)
                for b in range(4):
                    if b >= 2:
                        pe.wait_ge(sem("tok_done"), b - 1)
                    for c in range(2):
                        last = turn(MI[:, b % 2, P * c:P * c + P],
                                    VT[:, c, HT * (b // 2) + P * (b % 2):HT * (b // 2) + P * (b % 2) + P], P)
                    last.then_inc(sem("tok_made"), 1)
                pe.wait_ge(sem("tok_done"), 3)
                for c in range(2):
                    last = turn(MI[:, 0, P * c:P * c + P], KN[:, c, SEQ - P:SEQ], P)
                last.then_inc(sem("tok_made"), 1)
                pe.wait_ge(sem("tok_done"), 4)
                for c in range(2):
                    turn(MI[0:32, 1, P * c:P * c + P], KN[:, c, SEQ:NTOK], P)
                    last = turn(MI[0:32, 1, 256 + P * c:256 + P * c + P], VTS[:, c, :], P)
                last.then_inc(sem("tok_made"), 1)

            for s in range(4):
                pe.wait_ge(sem("split_done"), strip_of("kv", s) + 1)
                if s >= 2:
                    pe.wait_ge(sem("kvq_taken"), s - 1)
                product(s % 2, acc(s % 2), KC, 0, NH, NL, True, True,
                        ready="n3_split" if s == 0 else None).then_inc(sem("strip_done"), 1)
                if s == 0:
                    total("n3")
                if s in (1, 2):
                    head_sums(s - 1)
            for s in range(KC):
                pe.wait_ge(sem("split_done"), strip_of("q", s) + 1)
                pe.wait_ge(sem("kvq_taken"), s + 3)
                product(s % 2, acc(s % 2), KC, 0, XQH, XQL, True, True,
                        ready="xq_split" if s == 0 else None).then_inc(sem("strip_done"), 1)
                if s >= 1:
                    head_sums(s + 1)
                if s == 2:
                    turn_tokens()
            head_sums(KC + 1)

            groups = [(kv, n) for kv in range(KVH) for n in range(4)]
            NG = len(groups)
            S = ACC[:].rearrange("p (g a) (b n) -> p g (a b) n", g=2, b=2)

            def scores(g):
                kv, n = groups[g]
                p2, r0 = kv // 2, HD * (kv % 2)
                rows = slice(r0, r0 + HD)
                if g >= 2:
                    pe.wait_ge(sem("att_max"), 4 * (g - 1))
                tok = HT * (n // 2) + P * (n % 2)
                for r in range(RQ):
                    k0 = P if n == 0 else 0
                    last = mm(S[:, g % 2, r, k0:256], QN[rows, 4 * p2 + r, tok:tok + P],
                              KN[rows, p2, P * (n - 1) + k0:P * (n + 1)], start=True, stop=True, skip_group_check=True)
                last.then_inc(sem("att_scored"), 1)

            def turn_probs(g):
                kv, n = groups[g]
                pe.wait_ge(sem("att_probs"), g + 1)
                if g >= 1:
                    pe.wait_ge(sem("att_pt"), g)
                for kb in range(1 if n == 0 else 0, 2):
                    for r in range(RQ):
                        last = turn(MI[:, kb, P * r:P * r + P], PB[:, g % 2, r, P * kb:P * kb + P], P)
                last.then_inc(sem("att_turned"), 1)

            def values(g):
                kv, n = groups[g]
                rows = slice(HD * (kv % 2), HD * (kv % 2) + HD)
                pe.wait_ge(sem("att_pt"), g + 1)
                if g >= 2:
                    pe.wait_ge(sem("att_taken"), g - 1)
                kbs = [1] if n == 0 else [0, 1]
                for kb in kbs:
                    last = mm(SS[rows, g % 2, :], VTOK[:, n - 1 + kb, HD * kv:HD * kv + HD], PTR[:, g % 2, kb, :],
                              start=kb == kbs[0], stop=kb == 1, skip_group_check=True)
                last.then_inc(sem("att_out"), 1)

            pe.wait_ge(sem("tok_done"), 6)
            pe.wait_ge(sem("head_done"), 6)
            pe.wait_ge(sem("kvq_taken"), 12)
            scores(0)
            for g in range(NG + 2):
                if g + 1 == NG // 2:
                    pe.wait_ge(sem("head_done"), KC + 2)
                if g + 1 < NG:
                    scores(g + 1)
                if g >= 2:
                    values(g - 2)
                if 1 <= g <= NG:
                    turn_probs(g - 1)

            pe.wait_ge(sem("kc_in"), 16)
            pe.wait_ge(sem("att_pt"), NG)
            for g in range(4):
                if g >= 2:
                    pe.wait_ge(sem("kct_done"), g - 1)
                for b in range(4):
                    last = turn(MI[:, g % 2, P * b:P * b + P],
                                KCS[:, 4 * (g % 2) + b, P * (g // 2):P * (g // 2) + P], P)
                last.then_inc(sem("kct_made"), 1)
            pe.wait_ge(sem("kct_done"), 4)
            for kv in (0, 2, 1, 3):
                p2 = kv // 2
                rows = slice(HD * (kv % 2), HD * (kv % 2) + HD)
                if kv == 1:
                    last.then_inc(sem("smp_even"), 1)
                    pe.wait_ge(sem("smp_even"), 1)
                for b in range(NSEQ):
                    t0 = HT * (b // 4) + HP + STEPS * (b % 4)
                    mm(MI[:, 0, P * kv + 16 * b:P * kv + 16 * b + 16], KCT[rows, p2, b, :],
                       QN[rows, 4 * p2:4 * p2 + 4, t0:t0 + STEPS], start=True, stop=True, skip_group_check=True)
                for h in range(2):
                    for b in range(4):
                        t0 = HT * h + HP + STEPS * b
                        last = mm(MI[0:32, 1, P * kv + 64 * h + 16 * b:P * kv + 64 * h + 16 * b + 16],
                                  KN[rows, p2, SEQ:NTOK], QN[rows, 4 * p2:4 * p2 + 4, t0:t0 + STEPS],
                                  start=True, stop=True, skip_group_check=True)
            last.then_inc(sem("smp_scored"), 1)
            pe.wait_ge(sem("smp_copied"), 1)
            pe.wait_ge(sem("att_max"), 4 * (NG - 1))
            for kv in range(KVH):
                turn(S[:, 0, kv, 0:P], PTR[:, 0, 0, P * kv:P * kv + P], P)
                last = turn(S[:, 0, kv, P:160], PTR[0:32, 0, 1, P * kv:P * kv + P], 32)
            last.then_inc(sem("att_scored"), 1)
            pe.wait_ge(sem("att_probs"), NG + 1)
            for kv in range(KVH):
                turn(MI[:, 0, P * kv:P * kv + P], PB[:, 0, kv, 0:P], P)
                last = turn(MI[0:32, 1, P * kv:P * kv + P], PB[:, 0, kv, P:160], P)
            last.then_inc(sem("att_turned"), 1)
            pe.wait_ge(sem("att_pt"), NG + 1)
            pe.wait_ge(sem("att_taken"), NG - 1)
            pe.wait_ge(sem("vc_in"), 16)
            for kv in range(KVH):
                rows = slice(HD * (kv % 2), HD * (kv % 2) + HD)
                mm(SS[rows, 0, P * kv:P * kv + P], KVS[0:32, 1, HD * kv:HD * kv + HD], PTR[0:32, 0, 1, P * kv:P * kv + P],
                   start=True, stop=False, skip_group_check=True)
                for b in range(NSEQ):
                    c0 = P * kv + 16 * b
                    last = mm(SS[rows, 0, c0:c0 + 16], VCS[:, b, HD * kv:HD * kv + HD], PTR[:, 0, 0, c0:c0 + 16],
                              start=False, stop=True, skip_group_check=True)
            last.then_inc(sem("att_out"), 1)

            def wo(i, u, start=False):
                strip("wo", i, u)
                if not start:
                    pe.wait_ge(sem("n4_h"), i * 2 + (u - 1) + before("n4_h"))
                product(u, acc(u), KC, 0, NH, NL, True, True).then_inc(sem("strip_done"), 1)

            pe.wait_ge(sem("att_taken"), NG + 1)
            pe.wait_ge(sem("att_max"), 4 * (NG + 1))
            wo(0, 0, True)
            wo(0, 1, True)
            with pe.Fori(1, KC // 2 - 1) as i:
                wo(i, 0)
                wo(i, 1)
            turn_past(1)
            wo(KC // 2 - 1, 0)
            turn_ple(1)
            wo(KC // 2 - 1, 1)

            up(1)
            down(1)
            ple(1)

        @block.scalar
        def _(act):
            chain = Chain(act, sem("act_chain"))
            A = nc.scalar.activation
            def copy(out, in_, **kw):
                return A(out, in_, ACT.Copy, **kw)

            def store(dst, src):
                act.dma_start(dst, src).then_inc(sem("out"), 16)
                outs[0] += 16

            def square(name, m, src, first=False):
                act.wait_ge(sem(name + "_h"), m + 1 + before(name + "_h"))
                if not first:
                    act.wait_ge(sem(name + "_summed"), m + before(name + "_summed"))
                A(SQ, src, ACT.Square).then_inc(sem(name + "_sq"), 1)

            def root(name):
                if name == "n0":
                    act.wait_ge(sem("n0_summed"), KC)
                else:
                    act.wait_ge(sem(name + "_total"), 1 + before(name + "_total"))
                A(halves(RSTD[:]), SS[:, :, 0:HT], ACT.Sqrt, bias=EPSB[:], scale=1.0 / D).then_inc(sem(name + "_root"), 1)

            def high(name, of, g0, dst):
                with act.Fori(0, KC) as i:
                    act.wait_ge(sem(of + "_h"), i + 1 + before(of + "_h"))
                    A(dst[:, i, :], H[:, i, :], ACT.Copy, scale=VEC[:, bass.ds(i + g0, 1)]).then_inc(sem(name + "_high"), 1)

            for r in range(2):
                act.wait_ge(sem("c_made"), r + 1)
                copy(CAC[:, 0, r].rearrange("p q c -> p (q c)"), ACC[:, 2 + r, :]).then_inc(sem("c_turned"), 1)
            for m in range(KC):
                act.wait_ge(sem("x_made"), m + 1)
                copy(halves(H[:, m, :])[:, :, 0:HP], MI[:, m % 2, :].rearrange("p (h t) -> p h t", h=2)).then_inc(sem("x_turned"), 1)
            act.wait_ge(sem("x_made"), KC + 1)
            copy(H[:].rearrange("p m (h t) -> p m h t", h=2)[:, :, :, HP:HT],
                 ACC[:, 0, 0:256].rearrange("p (m h t) -> p m h t", m=KC, h=2)).then_inc(sem("x_turned"), 1)
            act.wait_ge(sem("x_turned"), KC + 1)
            act.wait_ge(sem("vec_made"), 1)
            copy(VEC[:], SS[:, 1, 0:V_N]).then_inc(sem("vec_done"), 1)
            act.wait_ge(sem("cp_made"), 1)
            copy(CP[:].rearrange("p l v c -> p (l v c)"), ACC[:, 1, 0:352]).then_inc(sem("vec_done"), 1)
            act.wait_ge(sem("st_made"), 1)
            for r in range(2):
                copy(H0[:, r].rearrange("p b (h q) -> p h b q", h=2),
                     MI[:, r, 0:256].rearrange("p (h b q) -> p h b q", h=2, b=NSEQ)).then_inc(sem("h0_done"), 1)
            for m in range(KC):
                if m >= 2:
                    act.wait_ge(sem("n0_summed"), m - 1 + before("n0_summed"))
                A(WK[:, m % 2, 0:NTOK], H[:, m, :], ACT.Square).then_inc(sem("n0_sq"), 1)
            act.wait_ge(sem("ones_set"), 1)
            root("n0")

            def expand_b(f):
                src = PC[:, f, 0:512].rearrange("p (x c) -> p x c", c=CG)
                dst = PBD[:].rearrange("p q r j (a c) -> p (q r j) a c", a=2)
                copy(dst[0:64, :, 0], src[0:64])
                copy(dst[64:128, :, 1], src[64:128]).then_inc(sem("pbd_ready"), 1)

            def expand_c(f, i0, n, dst, name):
                for r in range(2):
                    d = dst[:, :, r, :].rearrange("p i (q a c) -> p i a q c", q=FQ, a=2)
                    s_ = CAC[:, i0:i0 + n, r, FQ * f:FQ * f + FQ, :]
                    copy(d[0:64, :, 0], s_[0:64], scale=1.0 - 2.0 * r)
                    last = copy(d[64:128, :, 1], s_[64:128], scale=1.0 - 2.0 * r)
                last.then_inc(sem(name), 1)

            C0V = C0BD[:].rearrange("p (i r) c -> p i r c", i=1)
            act.wait_ge(sem("zeros_set"), 1)
            act.wait_ge(sem("pc_ready"), 1)
            expand_b(0)
            expand_c(0, 0, 1, C0V, "c0_ready")
            act.wait_ge(sem("e_ready"), 1)

            def gelu(f):
                act.wait_ge(sem("y_made"), f + 1)
                if f:
                    act.wait_ge(sem("z_split"), f)
                A(ZT.rearrange("p (c i) -> p i c", i=STEPS), SS[:].rearrange("p a (i n) -> p (a i) n", i=2)[:, :, 0:NCOL],
                  ACT.Gelu_apprx_tanh).then_inc(sem("y_taken"), 1)
                act.wait_ge(sem("y_taken"), f + 1)
                copy(NH[:, f, :], ZT).then_inc(sem("z_high"), 1)

            for f in range(KC):
                act.wait_ge(sem("p_turned"), f + 1)
                if f:
                    act.wait_ge(sem("v_made"), f)
                for h in range(2):
                    last = copy(BT[:, 2 * h:2 * h + 2].rearrange("p q r s -> p (q r s)"), MI[:, h, :])
                last.then_inc(sem("bt_done"), 1)
                act.wait_ge(sem("k_made"), f + 1)
                if f + 1 < KC:
                    expand_b(f + 1)
                    expand_c(f + 1, 0, 1, C0V, "c0_ready")
                act.wait_ge(sem("v_made"), f + 1)
                if f >= 2:
                    act.wait_ge(sem("y_made"), f - 1)
                for q in range(FQ):
                    rows = slice(32 * q, 32 * q + 32)
                    last = copy(KM[rows, f % 2, :, rows],
                                ACC[rows, 0, 2 * NCOL:2 * NCOL + P].rearrange("p (t c) -> p t c", t=4))
                last.then_inc(sem("k_done"), 1)
                for r in range(2):
                    src = ACC[:, :, NCOL * r:NCOL * r + NCOL].rearrange("p q (h c) -> p q h c", h=2)
                    for h in range(2):
                        last = copy(VSM[:, r, 4 * h:4 * h + 4, FQ * f:FQ * f + FQ].rearrange("p b q -> p q b"),
                                    src[:, :, h, HPB:HB])
                last.then_inc(sem("vsm_done"), 1)
                for r in range(2):
                    for h in range(2):
                        last = copy(HSV[:, f % 2, r].rearrange("p q (h c) -> p q h c", h=2)[:, :, h, HPB:HB],
                                    H0[:, r, 4 * h:4 * h + 4, FQ * f:FQ * f + FQ].rearrange("p b q -> p q b"))
                last.then_inc(sem("h0_placed"), 1)
                if f:
                    act.wait_ge(sem("y_made"), f)
                else:
                    act.wait_ge(sem("ca_ready"), 1)
                expand_c(f, 1, 4, CBD[:], "cbd_ready")
                if f:
                    gelu(f - 1)
            gelu(KC - 1)
            act.wait_ge(sem("fs_turned"), 1)
            copy(FSO[:].rearrange("q r n -> q (r n)"), MI[0:PAIRS, 1, 0:256])
            copy(VSO[:].rearrange("p r h n -> p (r h n)"), MI[:, 0, :]).then_inc(sem("fs_out"), 1)
            act.wait_ge(sem("fs_out"), 1)
            for r, (dp, ds_) in enumerate(((ssm_re_p, ssm_re_s), (ssm_im_p, ssm_im_s))):
                store(dp[0, 0].rearrange("(q a) s -> q (a s)", a=2), FSO[:, r, :])
                for h in range(2):
                    store(ds_[0, 4 * h:4 * h + 4].rearrange("b (q a) s -> (b q) (a s)", a=2), VSO[:, r, h, :])

            def load_ffn(l):
                c = sem("cst_in%d" % l)
                act.dma_start(CST[:], state_ffn_conv[l].rearrange("b k n -> (b k) n")).then_inc(c, 16)
                act.dma_start(PST[:, 0:4, :], p_prompt[l, 0].rearrange("(b p) d -> p b d", p=P)).then_inc(c, 16)
                act.dma_start(PST[0:32, 4, :], p_sample[l].rearrange("b t d -> (b t) d")).then_inc(c, 16)

            act.wait_ge(sem("fs_ready"), 1)
            load_ffn(0)

            def gate(i):
                act.wait_ge(sem("strip_done"), i * 2 + 1)
                act.wait_ge(sem("glu_taken1"), i)
                A(halves(SG), acc(0), ACT.Sigmoid, bias=VEC[:, bass.ds(i + (V_BGLU + KC), 1)]).then_inc(sem("glu_taken0"), 1)

            act.wait_ge(sem("strip_done"), 1)
            act.wait_ge(sem("z_split"), KC)
            A(halves(SG), acc(0), ACT.Sigmoid, bias=VEC[:, V_BGLU + KC:V_BGLU + KC + 1]).then_inc(sem("glu_taken0"), 1)
            square("n1", 0, H[:, 0, :], True)
            gate(1)
            with act.Fori(2, KC - 1) as i:
                square("n1", i - 1, H[:, i - 1, :])
                gate(i)

            def take_small(l):
                act.wait_ge(sem("cs_turned%d" % l), 1 + before("cs_turned%d" % l))
                for a in range(2):
                    copy(CSP[:, FC * a:FC * a + FC, :], MI[:, a, 0:16 * FC].rearrange("p (c n) -> p c n", n=16))
                copy(PTH[:].rearrange("p c (h t) -> p c h t", h=2)[:, :, :, HP:HT],
                     MI[:, :, 16 * FC:16 * FC + 32].rearrange("p c (h t) -> p c h t", h=2)).then_inc(sem("cs_done%d" % l), 1)
                act.wait_ge(sem("p_made%d" % l), 1 + before("p_made%d" % l))
                for c in range(2):
                    last = copy(halves(PTH[:, c, :])[:, :, 0:HP], MI[:, c, :].rearrange("p (h t) -> p h t", h=2))
                last.then_inc(sem("p_high%d" % l), 1)

            square("n1", KC - 2, H[:, KC - 2, :])
            take_small(0)
            gate(KC - 1)
            act.wait_ge(sem("strip_done"), 2 * KC)
            high("n1", "n1", V_GFFN, NH)
            square("n1", KC - 1, H[:, KC - 1, :])

            def up(l):
                name, n0, norm = "up%d" % l, first["up%d" % l], "n%d" % (1 + 3 * l)
                root(norm)

                def body(i):
                    act.wait_ge(sem(name + "_cg"), i + 1 + before(name + "_cg"))
                    A(WK[:, 2, 0:CONV], WK[:, 2, 0:CONV], ACT.Silu).then_inc(sem(name + "_silu"), 1)
                    act.wait_ge(sem(name + "_prod"), i + 1 + before(name + "_prod"))
                    copy(AH[:, i, :], TT[:]).then_inc(sem(name + "_high"), 1)

                with act.Fori(0, FC) as i:
                    body(i)

            def down(l):
                norm, g0 = "n%d" % (2 + 3 * l), V_GPLE + KC * l

                def take_last(g):
                    b = g % 2
                    used = g // 2 + (FC // 2 + 1 - b) // 2 * l
                    if used:
                        act.wait_ge(sem("ct_out%d" % b), 32 * used)
                    act.wait_ge(sem("ct_made%d" % l), g + 1 + before("ct_made%d" % l))
                    copy(CTO[:, b, :], MI[0:18, b, :]).then_inc(sem("ct_done%d" % l), 1)
                    act.wait_ge(sem("ct_done%d" % l), g + 1 + before("ct_done%d" % l))
                    act.dma_start(conv_p[l, 0, :, 512 * g:512 * g + 512], CTO[0:2, b, :]).then_inc(sem("ct_out%d" % b), 16)
                    act.dma_start(conv_s[l].rearrange("b k n -> (b k) n")[:, 512 * g:512 * g + 512],
                                  CTO[2:18, b, :]).then_inc(sem("ct_out%d" % b), 16)

                def high_square(m):
                    act.wait_ge(sem(norm + "_h"), m + 1 + before(norm + "_h"))
                    act.wait_ge(sem(norm + "_summed"), m + before(norm + "_summed"))
                    gain = VEC[:, g0 + m:g0 + m + 1] if isinstance(m, int) else VEC[:, bass.ds(m + g0, 1)]
                    A(NH[:, m, :], H[:, m, :], ACT.Copy, scale=gain).then_inc(sem(norm + "_high"), 1)
                    A(SQ, H[:, m, :], ACT.Square).then_inc(sem(norm + "_sq"), 1)

                for g in range(4):
                    take_last(g)
                high_square(0)
                for g in range(4, 8):
                    take_last(g)
                high_square(1)
                for g in range(8, FC // 2):
                    take_last(g)
                with act.Fori(2, KC) as i:
                    high_square(i)
                for b in range(2):
                    act.wait_ge(sem("ct_out%d" % b), 32 * ((FC // 2 + 1 - b) // 2) * (l + 1))

            def ple(l):
                name, norm, nxt, n0 = "ple%d" % l, "n%d" % (2 + 3 * l), "n%d" % (3 + 3 * l), first["ple%d" % l]
                root(norm)

                def one(m, start=False):
                    act.wait_ge(sem(name + "_raw"), m + 1 + before(name + "_raw"))
                    if not start:
                        act.wait_ge(sem(name + "_in"), m + before(name + "_in"))

                def sig(m, u):
                    A(SG, GATE, ACT.Sigmoid).then_inc(sem(name + "_sig"), 1)

                one(0, True)
                def take_result(m, u):
                    act.wait_ge(sem("y_turned"), m + 1)
                    cols = slice(P * m, P * m + P) if isinstance(m, int) else bass.ds(m * P, P)
                    copy(YS[:, :, cols], SS[:, u, :].rearrange("p (b n) -> p b n", b=4)).then_inc(sem("y_done"), 1)

                def send(i):
                    act.wait_ge(sem("y_done"), i * 2 + 2)
                    cols = slice(2 * P * i, 2 * P * i + 2 * P) if isinstance(i, int) else bass.ds(i * 2 * P, 2 * P)
                    act.dma_start(y_prompt[0].rearrange("(b p) n -> p b n", p=P)[:, :, cols], YS[:, :, cols]).then_inc(sem("y_out"), 16)

                sig(0, 0)
                if l == 0:
                    square(nxt, 0, H[:, 0, :], True)
                one(1)
                sig(1, 1)
                if l == 1:
                    take_result(0, 0)
                with act.Fori(1, KC // 2) as i:
                    for u in range(2):
                        if l == 0:
                            square(nxt, i * 2 + (u - 1), H[:, i * 2 + (u - 1), :])
                        one(i * 2 + u)
                        sig(i * 2 + u, u)
                        if l == 1:
                            take_result(i * 2 + (u - 1), 1 - u)
                            if u == 0:
                                send(i - 1)
                if l == 0:
                    act.wait_ge(sem("strip_done"), n0 + KC)
                    high("n3", "n3", V_GKV, NH)
                    square(nxt, KC - 1, H[:, KC - 1, :])
                else:
                    take_result(KC - 1, 1)
                    send(KC // 2 - 1)

            up(0)
            down(0)
            act.dma_start(RB[0:NBUCK, :], rel_bias).then_inc(sem("rb_dma"), 16)
            act.dma_start(OHB[:], consts[0:NBUCK + 1, C_OH:C_OH + BW]).then_inc(sem("rb_dma"), 16)
            act.dma_start(BM[:], consts[:, C_BM:C_BM + 32 + RQ]).then_inc(sem("snk_in"), 16)
            with nc.allow_non_contiguous_dma(reason="a few small vectors"):
                act.dma_start(SNK[:], sinks.to_broadcast([P, 16])).then_inc(sem("snk_in"), 16)
            act.dma_start(VCS[:], cache_v_win.rearrange("b s k d -> s b (k d)")).then_inc(sem("vc_in"), 16)
            ple(0)
            act.wait_ge(sem("rb_made"), 1)
            copy(RBR[:], MI[0:16, 0, 0:BW]).then_inc(sem("rb_done"), 1)
            act.wait_ge(sem("rb_done"), 1)
            act.dma_start(bias_rows, RBR[:].unsqueeze(1).to_broadcast([16, P, BW])).then_inc(sem("rows_out"), 16)

            root("n3")
            high("xq", "n3", V_GMIX + KC, XQH)

            def head_square(n):
                src = KN[:, n, :] if n < 2 else QN[:, n - 2, :]
                if n:
                    act.wait_ge(sem("head_summed"), n)
                A(SQ, src, ACT.Square).then_inc(sem("head_sq"), 1)

            def head_root(n):
                act.wait_ge(sem("head_summed"), n + 1)
                if n:
                    act.wait_ge(sem("head_done"), n)
                A(halves(SG), SS[:, :, 0:HT], ACT.Sqrt, bias=EPSB[:], scale=1.0 / HD).then_inc(sem("head_root"), 1)

            for s in range(12):
                if s == 0:
                    outs_mid[0] = outs[0]
                act.wait_ge(sem("kvq_taken"), s + 1)
                n = s if s < 2 else s - 2
                if s < 2 or s >= 4:
                    if n >= 1:
                        head_root(n - 1)
                    head_square(n)
                if s == 6:
                    for b in range(4):
                        act.wait_ge(sem("tok_made"), b + 1)
                        copy(VTOK[:, b, :], MI[:, b % 2, 0:256]).then_inc(sem("tok_done"), 1)
                    act.wait_ge(sem("tok_made"), 5)
                    copy(KTP[:], MI[:, 0, 0:256]).then_inc(sem("tok_done"), 1)
                    act.wait_ge(sem("tok_made"), 6)
                    copy(KVS[:].rearrange("p a n -> p (a n)"), MI[0:32, 1, :]).then_inc(sem("tok_done"), 1)
                    act.wait_ge(sem("tok_done"), 6)
            head_root(9)

            act.dma_start(KCS[:], cache_k_win.rearrange("b s k d -> s b (k d)")).then_inc(sem("kc_in"), 16)

            NG = 16

            def exps(g, w0, w):
                act.wait_ge(sem("att_neg"), g + 1)
                for r in range(4):
                    A(PB[:, g % 2, r, w0:w], PB[:, g % 2, r, w0:w], ACT.Exp, bias=SM[:, g % 2, 1, r:r + 1],
                      accum_out=SM[:, g % 2, 2, r:r + 1])
                A(SM[:, g % 2, 3, :], SM[:, g % 2, 3, :], ACT.Exp).then_inc(sem("att_exp"), 1)

            def take_turned(g):
                act.wait_ge(sem("att_turned"), g + 1)
                if g >= 2:
                    act.wait_ge(sem("att_out"), g - 1)
                kb = 1 if g % 4 == 0 else 0
                copy(PTR[:, g % 2, kb:2, :], MI[:, kb:2, :]).then_inc(sem("att_pt"), 1)

            def take_out(g):
                kv, n = g // 4, g % 4
                rows = slice(HD * (kv % 2), HD * (kv % 2) + HD)
                tok = HT * (n // 2) + P * (n % 2)
                act.wait_ge(sem("att_out"), g + 1)
                copy(NH[rows, 4 * (kv // 2):4 * (kv // 2) + 4, tok:tok + P],
                     SS[rows, g % 2, :].rearrange("p (r t) -> p r t", r=4)).then_inc(sem("att_high"), 1)

            for g in range(NG + 2):
                if g < NG:
                    exps(g, P if g % 4 == 0 else 0, 256)
                if 1 <= g <= NG:
                    take_turned(g - 1)
                if g >= 2:
                    take_out(g - 2)
            for g in range(4):
                act.wait_ge(sem("kct_made"), g + 1)
                copy(KCT[:, g // 2, 4 * (g % 2):4 * (g % 2) + 4, :].rearrange("p b n -> p (b n)"), MI[:, g % 2, :]).then_inc(sem("kct_done"), 1)
            act.wait_ge(sem("smp_scored"), 1)
            act.wait_ge(sem("att_out"), NG)
            copy(PTR[:, 0, 0, :], MI[:, 0, :])
            copy(PTR[0:32, 0, 1, :], MI[0:32, 1, :]).then_inc(sem("smp_copied"), 1)
            exps(NG, 0, 160)
            act.wait_ge(sem("att_turned"), NG + 1)
            copy(PTR[:, 0, 0, :], MI[:, 0, :])
            copy(PTR[0:32, 0, 1, :], MI[0:32, 1, :]).then_inc(sem("att_pt"), 1)
            act.wait_ge(sem("att_out"), NG + 1)
            for kv in range(KVH):
                rows = slice(HD * (kv % 2), HD * (kv % 2) + HD)
                for h in range(2):
                    last = copy(NH[rows, 4 * (kv // 2):4 * (kv // 2) + 4, HT * h + HP:HT * h + HT].rearrange("p r (b t) -> p r b t", t=STEPS),
                                SS[rows, 0, P * kv + 64 * h:P * kv + 64 * h + 64].rearrange("p (b r t) -> p r b t", b=4, r=4))
            last.then_inc(sem("att_high"), 1)
            act.wait_ge(sem("att_out"), NG + 1)
            act.wait_ge(sem("out"), outs[0])
            act.wait_ge(sem("kv_out"), 16 * (2 + 2 * (1 + NSEQ)))
            load_ffn(1)
            square("n4", 0, H[:, 0, :], True)
            with act.Fori(1, KC - 2) as i:
                square("n4", i, H[:, i, :])
            take_small(1)
            square("n4", KC - 2, H[:, KC - 2, :])
            act.wait_ge(sem("strip_done"), first["up1"])
            high("n4", "n4", V_GFFN + KC, NH)
            square("n4", KC - 1, H[:, KC - 1, :])
            up(1)
            down(1)
            ple(1)

            act.wait_ge(sem("y_turned"), KC + 1)
            copy(YSS[:].rearrange("p (a n) -> p a n", a=2), ACC[0:32, 0:2, :]).then_inc(sem("y_done"), 1)
            act.wait_ge(sem("y_done"), KC + 1)
            store(y_sample.rearrange("b t d -> (b t) d"), YSS[:])
            act.wait_ge(sem("y_out"), 16 * (KC // 2))
            act.wait_ge(sem("out"), outs[0])

        @block.vector
        def _(dve):
            chain = Chain(dve, sem("dve_chain"))
            link = chain.link
            T = nc.vector.tensor_tensor
            TS = nc.vector.tensor_scalar
            cp = nc.vector.tensor_copy

            def STT(out, in0, scalar, in1, op0, op1):
                return nc.vector.scalar_tensor_tensor(out=out, in0=in0, scalar=scalar, in1=in1, op0=op0, op1=op1)

            M_, A_, S_ = ALU.mult, ALU.add, ALU.subtract

            def pr(j):
                return PR[:, j, :]

            ROUND = 1.5 * 2.0 ** 23

            dve.wait_ge(sem("lam_turned"), 1)
            link(cp(PR[:, LR:LR + 2, :].rearrange("p a q -> p (a q)"), SS[:, 0, 0:64]))
            cp(pr(X0), SS[:, 0, 64:96]).then_inc(sem("lam_taken"), 1)
            dve.wait_ge(sem("lam_taken"), 1)

            def exponential(out, x):
                link(TS(pr(X1), x, 1.0 / math.log(2.0), ROUND, M_, A_))
                link(TS(pr(X1), pr(X1), ROUND, -126.0, S_, ALU.max))
                link(TS(pr(X1), pr(X1), 127.0, None, ALU.min))
                link(STT(pr(X2), pr(X1), -0.693359375, x, M_, A_))
                link(STT(pr(X2), pr(X1), 2.12194440e-4, pr(X2), M_, A_))
                link(TS(pr(X3), pr(X2), 1.0 / 5040.0, None, M_))
                for n in (720.0, 120.0, 24.0, 6.0, 2.0, 1.0):
                    link(STT(pr(X3), pr(X3), 1.0 / n, pr(X2), A_, M_))
                link(TS(pr(X1), pr(X1), 127.0, None, A_))
                link(cp(pr(KI).bitcast(I32), pr(X1)))
                link(TS(pr(KI).bitcast(I32), pr(KI).bitcast(I32), 23, None, ALU.logical_shift_left))
                link(STT(out, pr(X3), 1.0, pr(KI), A_, M_))

            def times(o_re, o_im, a_re, a_im, b_re, b_im):
                link(T(pr(X4), a_re, b_re, M_))
                link(T(pr(X5), a_im, b_im, M_))
                link(T(pr(X6), a_re, b_im, M_))
                link(T(pr(X7), a_im, b_re, M_))
                link(T(o_re, pr(X4), pr(X5), S_))
                link(T(o_im, pr(X6), pr(X7), A_))

            exponential(pr(DT), pr(X0))
            link(T(pr(X0), pr(LR), pr(DT), M_))
            exponential(pr(MAG), pr(X0))
            link(T(pr(X0), pr(LI), pr(DT), M_))
            link(TS(pr(X1), pr(X0), 2.0 / math.pi, ROUND, M_, A_))
            link(TS(pr(X1), pr(X1), ROUND, None, S_))
            for part in (1.5703125, 4.837512969970703125e-4, 7.549789954891882e-8):
                link(STT(pr(X0), pr(X1), -part, pr(X0), M_, A_))
            link(T(pr(X2), pr(X0), pr(X0), M_))
            link(TS(pr(X3), pr(X2), -1.0 / 39916800.0, None, M_))
            for n in (362880.0, -5040.0, 120.0, -6.0):
                link(STT(pr(X3), pr(X3), 1.0 / n, pr(X2), A_, M_))
            link(STT(pr(X3), pr(X3), 1.0, pr(X0), A_, M_))
            link(TS(pr(X4), pr(X2), -1.0 / 3628800.0, None, M_))
            for n in (40320.0, -720.0, 24.0, -2.0):
                link(STT(pr(X4), pr(X4), 1.0 / n, pr(X2), A_, M_))
            link(TS(pr(X4), pr(X4), 1.0, None, A_))
            link(TS(pr(X5), pr(X1), 0.25, ROUND, M_, A_))
            link(TS(pr(X5), pr(X5), ROUND, -4.0, S_, M_))
            link(T(pr(X5), pr(X5), pr(X1), A_))
            link(STT(pr(X6), pr(X5), -1.0, pr(X5), M_, ALU.max))
            link(TS(pr(X7), pr(X6), -1.0, 1.0, M_, A_))
            link(TS(pr(X6), pr(X6), -1.0, 2.0, M_, A_))
            link(T(pr(X6), pr(X6), pr(X5), M_))
            link(T(pr(X5), pr(X4), pr(X7), M_))
            link(T(pr(X8), pr(X3), pr(X6), M_))
            link(T(pr(C1), pr(X5), pr(X8), S_))
            link(T(pr(X5), pr(X3), pr(X7), M_))
            link(T(pr(X8), pr(X4), pr(X6), M_))
            link(T(pr(S1), pr(X5), pr(X8), A_))
            link(T(pr(A_RE), pr(MAG), pr(C1), M_))
            T(pr(A_IM), pr(MAG), pr(S1), M_).then_inc(sem("a_ready"), 1)
            dve.wait_ge(sem("a_ready"), 1)
            link(T(pr(X0), pr(LR), pr(LR), M_))
            link(T(pr(X1), pr(LI), pr(LI), M_))
            link(T(pr(X0), pr(X0), pr(X1), A_))
            link(nc.vector.reciprocal(pr(X0), pr(X0)))
            link(TS(pr(X1), pr(A_RE), 1.0, None, S_))
            link(T(pr(X2), pr(X1), pr(LR), M_))
            link(T(pr(X3), pr(A_IM), pr(LI), M_))
            link(T(pr(X2), pr(X2), pr(X3), A_))
            link(T(pr(F_RE), pr(X2), pr(X0), M_))
            link(T(pr(X2), pr(A_IM), pr(LR), M_))
            link(T(pr(X3), pr(X1), pr(LI), M_))
            link(T(pr(X2), pr(X2), pr(X3), S_))
            link(T(pr(F_IM), pr(X2), pr(X0), M_))
            times(pr(A2_RE), pr(A2_IM), pr(A_RE), pr(A_IM), pr(A_RE), pr(A_IM))
            times(pr(A4_RE), pr(A4_IM), pr(A2_RE), pr(A2_IM), pr(A2_RE), pr(A2_IM))
            link(T(pr(R4), pr(MAG), pr(MAG), M_))
            link(T(pr(R4), pr(R4), pr(R4), M_))

            tw = [pr(TURNS + j) for j in range(2)]
            times(tw[0], tw[1], pr(C1), pr(S1), pr(C1), pr(S1))
            times(tw[0], tw[1], tw[0], tw[1], tw[0], tw[1])
            link(cp(pr(TURNS + 2), tw[0]))
            for lv in range(1, 7):
                t = TURNS + 3 * lv
                T(PR[:, X4:X4 + 2, :], PR[:, t - 3:t - 1, :], PR[:, t - 3:t - 1, :], M_)
                link(T(pr(X6), pr(t - 3), pr(t - 2), M_))
                T(pr(t), pr(X4), pr(X5), S_)
                T(pr(t + 2), pr(X4), pr(X5), S_)
                link(T(pr(t + 1), pr(X6), pr(X6), A_))
            cp(pr(X0), pr(X4)).then_inc(sem("turns_in"), 1)

            dve.wait_ge(sem("b_in"), 32)

            def pc(k, r):
                return PC[:, :, 0:FQ * 8 * CG].rearrange("p f (q x c) -> p f q x c", q=FQ, x=8)[:, :, :, 4 * r + 3 - k, :]

            def wide(j):
                return pr(j).rearrange("p (f q) -> p f q", q=FQ).unsqueeze(3).to_broadcast([P, KC, FQ, CG])

            def four(x):
                return x.rearrange("p (f q c) -> p f q c", f=KC, q=FQ)

            bc = [BC[:, r].rearrange("p (f q) c -> p f q c", q=FQ) for r in range(2)]
            te = [four(TE[:, j, 0:512]) for j in range(2)]
            for k in range(4):
                src = bc if k == 0 else [pc(k - 1, 0), pc(k - 1, 1)]
                re, im = (F_RE, F_IM) if k == 0 else (A_RE, A_IM)
                for o in range(2):
                    link(T(te[0], src[0], wide((re, im)[o]), M_))
                    link(T(te[1], src[1], wide((im, re)[o]), M_))
                    last = T(pc(k, o), te[0], te[1], (S_, A_)[o])
                    if k == 3 and o == 1:
                        last.then_inc(sem("pc_ready"), 1)
                    else:
                        link(last)

            def reciprocal_root(name):
                dve.wait_ge(sem(name + "_root"), 1 + before(name + "_root"))
                link(nc.vector.reciprocal(RSTD[:], RSTD[:]))

            dve.wait_ge(sem("vec_done"), 2)
            reciprocal_root("n0")
            for m in range(KC):
                STT(U[:, m, :].rearrange("p (i c) -> p c i", i=STEPS), H[:, m, :].rearrange("p (c i) -> p c i", i=STEPS),
                    VEC[:, V_GMIX + m:V_GMIX + m + 1], RSTD[:].rearrange("p (c i) -> p c i", i=STEPS),
                    M_, M_).then_inc(sem("u_ready"), 1)

            dve.wait_ge(sem("h0_done"), 2)
            dve.wait_ge(sem("tab_free"), 1)
            for par in range(2):
                last = nc.vector.memset(HSV[:, par, :, :, 0:1], 0.0)
                link(last)
            nc.vector.memset(TIC2[:], 0.0).then_inc(sem("e_ready"), 1)
            dve.wait_ge(sem("e_ready"), 1)

            def scan(f):
                par = f % 2
                t1 = T1.rearrange("p (r q c) -> p r (q c)", r=2, q=FQ)
                t2 = T2[:].rearrange("p r q c -> p r (q c)")
                v = V[:].rearrange("p r q c -> p r (q c)")
                e = [EROT[:, r, FQ * f:FQ * f + FQ, :].rearrange("p q c -> p (q c)").unsqueeze(1).to_broadcast([P, 2, FQ * NBLK])
                     for r in range(2)]
                dve.wait_ge(sem("v_made"), f + 1)
                dve.wait_ge(sem("vsm_done"), f + 1)
                if f % 2 == 0:
                    dve.wait_ge(sem("turns_ready"), f // 2 + 1)
                STT(KM[:, par, 0, :], IDN[:], VEC[:, V_D + f:V_D + f + 1], KM[:, par, 0, :], M_, A_)
                for j, dst in enumerate((T1.rearrange("p (r x) -> p r x", r=2), t2)):
                    for r in range(2):
                        last = T(dst[:, r].rearrange("p (q h c) -> p q h c", q=FQ, h=2),
                                 ACC[:, :, NCOL * r:NCOL * r + NCOL].rearrange("p q (h c) -> p q h c", h=2)[:, :, :, 0:HPB],
                                 EROT[:, j, FQ * f:FQ * f + FQ, :].rearrange("p q (h c) -> p q h c", h=2), M_)
                last.then_inc(sem("v_taken"), 1)
                dve.wait_ge(sem("v_taken"), f + 1)
                link(T(v[:, 0], t1[:, 0], t2[:, 1], A_))
                link(T(v[:, 1], t1[:, 1], t2[:, 0], S_))
                for r in range(2):
                    for q in range(FQ):
                        last = nc.vector.tensor_tensor_scan(
                            t1[:, r, NBLK * q:NBLK * q + NBLK], PR[:, R4, FQ * f + q:FQ * f + q + 1].to_broadcast([P, NBLK]),
                            v[:, r, NBLK * q:NBLK * q + NBLK], 0.0, M_, A_)
                link(last)
                link(T(v, t1, e[0], M_))
                link(T(t2, t1, e[1], M_))
                if f >= 2:
                    dve.wait_ge(sem("y_made"), f - 1)
                for r in range(2):
                    a = V[:, r]
                    b = T2[:, 1 - r]
                    op = (S_, A_)[r]
                    T(HSV[:, par, r, :, 1:HPB], a[:, :, 0:HPB - 1], b[:, :, 0:HPB - 1], op)
                    T(HSV[:, par, r, :, HB:HB + HPB], a[:, :, HPB - 1:NBLK - 1], b[:, :, HPB - 1:NBLK - 1], op)
                    last = T(FS[:, r, FQ * f:FQ * f + FQ], a[:, :, NBLK - 1], b[:, :, NBLK - 1], op)
                last.then_inc(sem("h_ready"), 1)
                dve.wait_ge(sem("h_ready"), f + 1)

            def rest(f):
                dve.wait_ge(sem("z_high"), f + 1)
                T(NL[:, f, :], ZT, NH[:, f, :].bitcast(F32), S_).then_inc(sem("z_split"), 1)

            for f in range(KC):
                scan(f)
                if f:
                    rest(f - 1)
            a4 = [pr(j).unsqueeze(1).to_broadcast([P, NSEQ, PAIRS]) for j in (A4_RE, A4_IM)]
            tv = [V[:, j].rearrange("p q c -> p (q c)")[:, 0:NSEQ * PAIRS].rearrange("p (b q) -> p b q", b=NSEQ) for j in range(2)]
            for r in range(2):
                link(T(tv[0], H0[:, 0], a4[r], M_))
                link(T(tv[1], H0[:, 1], a4[1 - r], M_))
                link(T(tv[0], tv[0], tv[1], (S_, A_)[r]))
                last = T(VSM[:, r], VSM[:, r], tv[0], A_)
                if r:
                    last.then_inc(sem("fs_ready"), 1)
                else:
                    link(last)
            rest(KC - 1)

            def glu(i):
                dve.wait_ge(sem("strip_done"), i * 2 + 2)
                dve.wait_ge(sem("glu_taken0"), i + 1)
                bias = VEC[:, V_BGLU + i:V_BGLU + i + 1] if isinstance(i, int) else VEC[:, bass.ds(i + V_BGLU, 1)]
                STT(halves(NEW), acc(1), bias, halves(SG), A_, M_).then_inc(sem("glu_taken1"), 1)
                dve.wait_ge(sem("glu_taken1"), i + 1)
                T(H[:, i, :], H[:, i, :], NEW, A_).then_inc(sem("n1_h"), 1)
                dve.wait_ge(sem("n1_h"), i + 1 + before("n1_h"))

            def take_small(l):
                dve.wait_ge(sem("cs_done%d" % l), 1 + before("cs_done%d" % l))
                for c in range(2):
                    last = T(halves(PTL[:, c, :])[:, :, HP:HT], MI[:, c, 16 * FC:16 * FC + 32].rearrange("p (h t) -> p h t", h=2),
                             halves(PTH[:, c, :])[:, :, HP:HT].bitcast(F32), S_)
                last.then_inc(sem("cs_low%d" % l), 1)
                dve.wait_ge(sem("p_high%d" % l), 1 + before("p_high%d" % l))
                for c in range(2):
                    last = T(halves(PTL[:, c, :])[:, :, 0:HP], MI[:, c, :].rearrange("p (h t) -> p h t", h=2),
                             halves(PTH[:, c, :])[:, :, 0:HP].bitcast(F32), S_)
                last.then_inc(sem("p_done%d" % l), 1)

            def add_squares(name, m):
                dve.wait_ge(sem(name + "_sq"), m + 1 + before(name + "_sq"))
                T(SQS[:], SQS[:], SQ, A_).then_inc(sem(name + "_summed"), 1)
                dve.wait_ge(sem(name + "_summed"), m + 1 + before(name + "_summed"))

            link(nc.vector.memset(SQS[:], 0.0))
            with dve.Fori(0, KC - 1) as i:
                glu(i)
                add_squares("n1", i)
            take_small(0)
            glu(KC - 1)

            def low(name, m, g0, hi, lo):
                dve.wait_ge(sem(name + "_high"), m + 1 + before(name + "_high"))
                gain = VEC[:, g0 + m:g0 + m + 1] if isinstance(m, int) else VEC[:, bass.ds(m + g0, 1)]
                STT(lo[:, m, :], H[:, m, :], gain, hi[:, m, :].bitcast(F32), M_, S_).then_inc(sem(name + "_split"), 1)

            def lows(name, g0, hi, lo):
                with dve.Fori(0, KC) as i:
                    low(name, i, g0, hi, lo)

            def up(l):
                name = "up%d" % l
                norm = "n%d" % (1 + 3 * l)
                lows(norm, V_GFFN + KC * l, NH, NL)
                add_squares(norm, KC - 1)
                reciprocal_root(norm)
                for u in range(2):
                    link(nc.vector.memset(WK[:, u, 0:2], 0.0))
                n0 = first[name]

                def body(i, start=False):
                    for u, what in enumerate(("_gate", "_val")):
                        E, C = WK[:, u, :], WK[:, 2 + u, 0:CONV]
                        ch = i + FC * u
                        dve.wait_ge(sem("strip_done"), i * 2 + (n0 + u + 1))
                        T(E[:, 2:2 + SEQ].rearrange("p (h t) -> p h t", h=2), acc(u)[:, :, 0:HP], halves(RSTD[:])[:, :, 0:HP], M_)
                        T(E[:, 2 + SEQ:EXT].rearrange("p (h b s) -> p h b s", h=2, s=6)[:, :, :, 2:6],
                          acc(u)[:, :, HP:HT].rearrange("p h (b t) -> p h b t", t=STEPS),
                          halves(RSTD[:])[:, :, HP:HT].rearrange("p h (b t) -> p h b t", t=STEPS), M_).then_inc(sem(name + what), 1)
                        dve.wait_ge(sem(name + what), i + 1 + before(name + what))
                        link(TS(E[:, 2 + SEQ:EXT].rearrange("p (b s) -> p b s", s=6)[:, :, 0:2],
                                CSP[:, ch, :].rearrange("p (b s) -> p b s", s=2), 1.0, None, M_))
                        TS(CT[:, ch, :].rearrange("p (j s) -> p j s", s=2),
                           E[:, TAIL0:TAIL0 + 54].rearrange("p (j s) -> p j s", s=6)[:, :, 0:2], 1.0, None, M_)

                        def col(vec):
                            return CP[:, l, vec, bass.ds(ch, 1)] if not start else CP[:, l, vec, ch:ch + 1]

                        link(TS(C, E[:, 2:2 + CONV], col(3), col(0), M_, A_))
                        link(STT(C, E[:, 1:1 + CONV], col(2), C, M_, A_))
                        STT(C, E[:, 0:CONV], col(1), C, M_, A_).then_inc(sem(name + ("_cg", "_cv")[u]), 1)
                    dve.wait_ge(sem(name + "_silu"), i + 1 + before(name + "_silu"))
                    dve.wait_ge(sem(name + "_cv"), i + 1 + before(name + "_cv"))
                    T(halves(TT[:])[:, :, 0:HP], WK[:, 2, 0:SEQ].rearrange("p (h t) -> p h t", h=2),
                      WK[:, 3, 0:SEQ].rearrange("p (h t) -> p h t", h=2), M_)

                    def smp(k):
                        return WK[:, k, 2 + SEQ:EXT].rearrange("p (h b s) -> p h b s", h=2, s=6)[:, :, :, 0:STEPS]

                    T(halves(TT[:])[:, :, HP:HT].rearrange("p h (b t) -> p h b t", t=STEPS), smp(2), smp(3), M_).then_inc(sem(name + "_prod"), 1)
                    dve.wait_ge(sem(name + "_high"), i + 1 + before(name + "_high"))
                    T(AL[:, i, :], TT[:], AH[:, i, :].bitcast(F32), S_).then_inc(sem(name + "_low"), 1)
                    dve.wait_ge(sem(name + "_low"), i + 1 + before(name + "_low"))

                with dve.Fori(0, FC) as i:
                    chain.enter(i, 6)
                    body(i)
                    chain.leave(FC)

            def add_chunks(stage, norm, per, g0=None):
                def two(i):
                    for u in range(2):
                        dve.wait_ge(sem("strip_done"), i * (2 * per) + (first[stage] + per * (u + 1)))
                        T(halves(H[:, i * 2 + u, :]), acc(u), halves(H[:, i * 2 + u, :]), A_).then_inc(sem(norm + "_h"), 1)
                        if g0 is not None:
                            dve.wait_ge(sem(norm + "_h"), i * 2 + (u + 1) + before(norm + "_h"))
                            low(norm, i * 2 + u, g0, NH, NL)
                        if not (stage == "wo" and isinstance(i, int) and u == 1):
                            add_squares(norm, i * 2 + u)

                link(nc.vector.memset(SQS[:], 0.0))
                with dve.Fori(0, KC // 2 - 1) as i:
                    two(i)
                if stage == "wo":
                    take_small(1)
                two(KC // 2 - 1)

            def ple(l):
                name, norm, nxt = "ple%d" % l, "n%d" % (2 + 3 * l), "n%d" % (3 + 3 * l)
                n0 = first[name]
                reciprocal_root(norm)

                def one(i, u):
                    m = i * 2 + u
                    dve.wait_ge(sem("strip_done"), m + (n0 + 1))
                    T(halves(GATE), acc(u), halves(RSTD[:]), M_).then_inc(sem(name + "_raw"), 1)
                    dve.wait_ge(sem(name + "_sig"), m + 1 + before(name + "_sig"))
                    T(halves(NEW), MI[:, :, 0:HT], halves(SG), M_).then_inc(sem(name + "_in"), 1)
                    dve.wait_ge(sem(name + "_in"), m + 1 + before(name + "_in"))
                    if l == 0:
                        T(H[:, m, :], H[:, m, :], NEW, A_).then_inc(sem(nxt + "_h"), 1)
                    else:
                        T((SQ, TT[:])[u], H[:, m, :], NEW, A_)
                        T(HSMP[:, m, :].rearrange("p (h t) -> p h t", h=2), halves(H[:, m, :])[:, :, HP:HT],
                          halves(NEW)[:, :, HP:HT], A_).then_inc(sem(nxt + "_h"), 1)
                    dve.wait_ge(sem(nxt + "_h"), m + 1 + before(nxt + "_h"))

                if l == 0:
                    link(nc.vector.memset(SQS[:], 0.0))
                with dve.Fori(0, KC // 2 - 1) as i:
                    for u in range(2):
                        one(i, u)
                        if l == 0:
                            add_squares(nxt, i * 2 + u)
                one(KC // 2 - 1, 0)
                if l == 0:
                    add_squares(nxt, KC - 2)
                one(KC // 2 - 1, 1)

            up(0)
            add_chunks("down0", "n2", 2, V_GPLE)
            dve.wait_ge(sem("strip_done"), first["ple0"])
            nc.vector.memset(RB[NBUCK:NBUCK + 1, :], NEG).then_inc(sem("rb_mask"), 1)
            ple(0)

            lows("n3", V_GKV, NH, NL)
            add_squares("n3", KC - 1)
            reciprocal_root("n3")
            link(TS(VEC[:, V_QN:V_QN + 1], VEC[:, V_QN:V_QN + 1], HD ** -0.5, None, M_))

            def head(n):
                dve.wait_ge(sem("head_root"), n + 1)
                link(nc.vector.reciprocal(SG, SG))
                row, g = (KN[:, n, :], V_KN) if n < 2 else (QN[:, n - 2, :], V_QN)
                STT(row, row, VEC[:, g:g + 1], SG, M_, M_).then_inc(sem("head_done"), 1)

            for s in range(12):
                dve.wait_ge(sem("strip_done"), first["kv"] + s + 1)
                if s == 0:
                    dve.wait_ge(sem("out"), outs_mid[0])
                a, rs = acc(s % 2), halves(RSTD[:])
                if s < 2:
                    T(KN[:, s, 0:SEQ].rearrange("p (h t) -> p h t", h=2), a[:, :, 0:HP], rs[:, :, 0:HP], M_)
                    last = T(KN[:, s, SEQ:NTOK].rearrange("p (h t) -> p h t", h=2), a[:, :, HP:HT], rs[:, :, HP:HT], M_)
                elif s < 4:
                    T(halves(VT[:, s - 2, :]), a, rs, M_)
                    last = T(VTS[:, s - 2, :].rearrange("p (h t) -> p h t", h=2), a[:, :, HP:HT], rs[:, :, HP:HT], M_)
                else:
                    last = T(halves(QN[:, s - 4, :]), a, rs, M_)
                last.then_inc(sem("kvq_taken"), 1)
                if s == 1:
                    lows("xq", V_GMIX + KC, XQH, XQL)
                n = s if s < 2 else s - 2
                if (s < 2 or s >= 4) and n >= 1:
                    head(n - 1)

            NG = 16
            dve.wait_ge(sem("bias_in"), 16)
            dve.wait_ge(sem("sbt_in"), 16 * NSEQ * KVH)
            dve.wait_ge(sem("snk_in"), 32)
            link(cp(SBI[:, :, 0:P], SBT[:, :, 0:P]))
            link(T(SBI[:, :, P:160].rearrange("p k (b t) -> p k b t", t=STEPS),
                   SBT[:, :, P:P + STEPS].unsqueeze(2).to_broadcast([P, KVH, NSEQ, STEPS]),
                   BM[:, 0:32].rearrange("p (b t) -> p b t", t=STEPS).unsqueeze(1).to_broadcast([P, KVH, NSEQ, STEPS]), A_))
            snk = PB[:, 0, 0, 0:16]
            link(T(snk.rearrange("p (k r) -> p k r", r=RQ), SNK[:].rearrange("p (k r) -> p k r", r=RQ),
                   BM[:, 32:32 + RQ].unsqueeze(1).to_broadcast([P, KVH, RQ]), M_))
            link(nc.vector.tensor_reduce(SNKS[:], snk.rearrange("p (k r) -> p k r", r=RQ), AX_X, A_))
            S = ACC[:].rearrange("p (g a) (b n) -> p g (a b) n", g=2, b=2)

            def maxima(g, w0, w, bias, sink):
                dve.wait_ge(sem("att_scored"), g + 1)
                if g >= 2:
                    dve.wait_ge(sem("att_turned"), g - 1)
                m = SM[:, g % 2]
                for r in range(4):
                    nc.vector.tensor_tensor_reduce(out=PB[:, g % 2, r, w0:w], in0=S[:, g % 2, r, w0:w], in1=bias(r), scale=1.0,
                                                   scalar=NEG, op0=A_, op1=ALU.max, accum_out=m[:, 0, r:r + 1]).then_inc(sem("att_max"), 1)
                dve.wait_ge(sem("att_max"), 4 * (g + 1))
                link(T(m[:, 1], m[:, 0], sink, ALU.max))
                link(TS(m[:, 1], m[:, 1], -1.0, None, M_))
                T(m[:, 3], sink, m[:, 1], A_).then_inc(sem("att_neg"), 1)

            def scale(g, w0, w):
                m = SM[:, g % 2]
                dve.wait_ge(sem("att_exp"), g + 1)
                link(T(m[:, 4], m[:, 2], m[:, 3], A_))
                link(nc.vector.reciprocal(m[:, 5], m[:, 4]))
                for r in range(4):
                    last = TS(PB[:, g % 2, r, w0:w], PB[:, g % 2, r, w0:w], m[:, 5, r:r + 1], None, M_)
                last.then_inc(sem("att_probs"), 1)

            def rest(g):
                kv, n = g // 4, g % 4
                rows = slice(HD * (kv % 2), HD * (kv % 2) + HD)
                tok = HT * (n // 2) + P * (n % 2)
                dve.wait_ge(sem("att_high"), g + 1)
                T(NL[rows, 4 * (kv // 2):4 * (kv // 2) + 4, tok:tok + P], SS[rows, g % 2, :].rearrange("p (r t) -> p r t", r=4),
                  NH[rows, 4 * (kv // 2):4 * (kv // 2) + 4, tok:tok + P].bitcast(F32), S_).then_inc(sem("att_taken"), 1)

            for g in range(NG + 3):
                if g == 1:
                    head(9)
                if g < NG:
                    kv = g // 4
                    w0 = P if g % 4 == 0 else 0
                    maxima(g, w0, 256, lambda r: BIAS[:, 4 * kv + r, w0:256], SNK[:, 4 * kv:4 * kv + 4])
                if 1 <= g <= NG:
                    scale(g - 1, P if (g - 1) % 4 == 0 else 0, 256)
                if g >= 3:
                    rest(g - 3)
            maxima(NG, 0, 160, lambda r: SBI[:, r, :], SNKS[:])
            scale(NG, 0, 160)
            dve.wait_ge(sem("att_high"), NG + 1)
            for kv in range(KVH):
                rows = slice(HD * (kv % 2), HD * (kv % 2) + HD)
                for h in range(2):
                    dst = (slice(4 * (kv // 2), 4 * (kv // 2) + 4), slice(HT * h + HP, HT * h + HT))
                    last = T(NL[rows, dst[0], dst[1]].rearrange("p r (b t) -> p r b t", t=STEPS),
                             SS[rows, 0, P * kv + 64 * h:P * kv + 64 * h + 64].rearrange("p (b r t) -> p r b t", b=4, r=4),
                             NH[rows, dst[0], dst[1]].bitcast(F32).rearrange("p r (b t) -> p r b t", t=STEPS), S_)
            last.then_inc(sem("att_taken"), 1)
            add_chunks("wo", "n4", 1)
            up(1)
            add_chunks("down1", "n5", 2, V_GPLE + KC)
            ple(1)


_INS = ['x_prompt', 'x_sample', 'state_ssm_re', 'state_ssm_im', 'state_ffn_conv', 'cache_k_win', 'cache_v_win',
        'p_prompt', 'p_sample', 'g_mix', 'g_ffn', 'g_ple', 'ssm_lam_re', 'ssm_lam_im', 'ssm_log_dt', 'ssm_b_re',
        'ssm_b_im', 'ssm_c_re', 'ssm_c_im', 'ssm_d', 'w_glu', 'b_glu', 'g_kv', 'w_k', 'w_v', 'k_norm', 'w_q',
        'q_norm', 'sinks', 'w_o', 'rel_bias', 'w_up', 'conv_w', 'conv_b', 'w_down', 'w_ple_in', 'w_ple_gate']
_OUTS = [(1, SEQ, D), (NSEQ, STEPS, D), (1, 1, 64, 64), (1, 1, 64, 64), (1, NSEQ, 64, 64), (1, NSEQ, 64, 64),
         (2, 1, 2, 2 * FF), (2, NSEQ, 2, 2 * FF), (1, WIN, KVH, HD), (1, WIN, KVH, HD), (NSEQ, WIN, KVH, HD),
         (NSEQ, WIN, KVH, HD)]


def kernel(**inputs):
    import concourse.bacc as _bacc
    from concourse.bass_utils import run_bass_kernel_spmd as _run

    nc = _bacc.Bacc("TRN2", target_bir_lowering=False, num_devices=1)
    arrays, args = {}, []
    for name in _INS + ['consts']:
        a = constants() if name == 'consts' else np.ascontiguousarray(inputs[name])
        arrays[f"in_{name}_dram"] = a
        args.append(nc.dram_tensor(f"in_{name}_dram", a.shape, mybir.dt.from_np(a.dtype), kind="ExternalInput").ap())
    args.append(nc.dram_tensor("bias_rows", (16, P, BW), F32, kind="Internal").ap())
    for i, shape in enumerate(_OUTS):
        args.append(nc.dram_tensor(f"out_{i}_dram", shape, F32, kind="ExternalOutput").ap())
    build(nc, *args)
    r = _run(nc, [arrays], core_ids=[0])
    return tuple(r.results[0][f"out_{i}_dram"] for i in range(len(_OUTS)))
```
